# Optimizing a Trainium2 kernel written in Bass

```python
import math
import jax
import jax.numpy as jnp
from jax import lax
import numpy as np
import jax, jax.numpy as jnp

D_MODEL = 1024
BATCH = 1
SEQ = 256
DEPTH = 2

PLE_DIM = 256
N_EVEN = (DEPTH + 1) // 2
N_ODD = DEPTH // 2

DA_HEADS = 4
DA_HEAD_DIM = 64
DA_V_DIM = 2 * DA_HEAD_DIM
DA_QK_WIDTH = DA_HEADS * 2 * DA_HEAD_DIM
DA_WIDTH = DA_HEADS * DA_V_DIM
ROPE_THETA = 500000.0
ROT_DIM = DA_HEAD_DIM // 4
Q_BLOCK = 128

SC_WIDTH = 512
SC_WIDTH_CONV = 3
EVEN_IN_WIDTH = 3 * DA_QK_WIDTH // 2 * 2 // 2 * 0 + DA_QK_WIDTH * 2 + DA_WIDTH + 3 * SC_WIDTH

GM_WIDTH = D_MODEL
GM_GROUPS = 8
GM_GROUP_CH = GM_WIDTH // GM_GROUPS
GM_CHUNK = 128

D_FF = 2816
N_EXPERTS = 8
TOP_K = 2
MOE_BLOCK = 256

RMS_EPS = 1e-6
LN_EPS = 1e-5


def rms_norm(x, g):
    xf = x.astype(jnp.float32)
    y = xf * lax.rsqrt(jnp.mean(xf * xf, axis=-1, keepdims=True) + RMS_EPS)
    return (y * g.astype(jnp.float32)).astype(x.dtype)

def layer_norm(x, g, b):
    xf = x.astype(jnp.float32)
    mu = jnp.mean(xf, axis=-1, keepdims=True)
    var = jnp.mean(jnp.square(xf - mu), axis=-1, keepdims=True)
    y = (xf - mu) * lax.rsqrt(var + LN_EPS)
    return (y * g.astype(jnp.float32) + b.astype(jnp.float32)).astype(x.dtype)

def rope_partial(t, positions):
    half = ROT_DIM // 2
    inv_freq = ROPE_THETA ** (-jnp.arange(0, ROT_DIM, 2, dtype=jnp.float32) / ROT_DIM)
    ang = positions.astype(jnp.float32)[:, :, None] * inv_freq
    cos = jnp.cos(ang)[:, :, None, None, :].astype(t.dtype)
    sin = jnp.sin(ang)[:, :, None, None, :].astype(t.dtype)
    t1 = t[..., :half]
    t2 = t[..., half:ROT_DIM]
    return jnp.concatenate([t1 * cos - t2 * sin, t2 * cos + t1 * sin, t[..., ROT_DIM:]], axis=-1)

def diff_attention(q, k, v, lam, lambda_init, subln_g):
    bsz, seq = q.shape[0], q.shape[1]
    n_blocks = seq // Q_BLOCK
    q = q * (DA_HEAD_DIM ** -0.5)
    kpos = jnp.arange(seq)

    def one_block(i):
        qb = lax.dynamic_slice_in_dim(q, i * Q_BLOCK, Q_BLOCK, axis=1)
        s = jnp.einsum('bqhcd,bkhcd->bhcqk', qb, k, preferred_element_type=jnp.float32)
        qpos = i * Q_BLOCK + jnp.arange(Q_BLOCK)
        mask = kpos[None, :] <= qpos[:, None]
        pr = jax.nn.softmax(jnp.where(mask, s, -jnp.inf), axis=-1)
        w = pr[:, :, 0] - lam * pr[:, :, 1]
        return jnp.einsum('bhqk,bkhe->bqhe', w.astype(v.dtype), v)

    out = lax.map(one_block, jnp.arange(n_blocks))
    out = jnp.moveaxis(out, 0, 1).reshape(bsz, seq, DA_HEADS, DA_V_DIM)
    out = rms_norm(out, subln_g) * (1.0 - lambda_init)
    return out.reshape(bsz, seq, DA_WIDTH)

def causal_short_conv(z, w):
    ch = z.shape[-1]
    rhs = jnp.transpose(w).astype(z.dtype)[:, None, :]
    return lax.conv_general_dilated(z, rhs, window_strides=(1,), padding=[(SC_WIDTH_CONV - 1, 0)],
                                    dimension_numbers=('NWC', 'WIO', 'NWC'), feature_group_count=ch)

def spatial_gating(u, v, w_s, b_s):
    bsz, seq, _ = v.shape
    vr = v.reshape(bsz, seq // GM_CHUNK, GM_CHUNK, GM_GROUPS, GM_GROUP_CH)
    tril = jnp.tril(jnp.ones((GM_CHUNK, GM_CHUNK), dtype=w_s.dtype))
    vs = jnp.einsum('gts,bnsgc->bntgc', w_s * tril, vr)
    vs = vs + jnp.transpose(b_s)[None, None, :, :, None]
    return u * vs.reshape(bsz, seq, GM_WIDTH)

def swiglu(h, w1, w3, w2):
    return (jax.nn.silu(h @ w1) * (h @ w3)) @ w2

def moe_swiglu(h, router_w, w1, w3, w2):
    bsz, seq, dm = h.shape
    n_tok = bsz * seq
    n_assign = n_tok * TOP_K
    n_blocks = -(-(n_assign + N_EXPERTS * (MOE_BLOCK - 1)) // MOE_BLOCK)
    xt = h.reshape(n_tok, dm)
    logits = jnp.einsum('nd,de->ne', xt, router_w, preferred_element_type=jnp.float32)
    top_val, top_idx = lax.top_k(logits, TOP_K)
    gates = jax.nn.softmax(top_val, axis=-1)
    expert_flat = top_idx.reshape(-1)
    token_flat = jnp.arange(n_assign) // TOP_K
    gate_flat = gates.reshape(-1)
    order = jnp.argsort(expert_flat)
    sorted_expert = expert_flat[order]
    sorted_token = token_flat[order]
    counts = jnp.bincount(expert_flat, length=N_EXPERTS)
    starts = jnp.cumsum(counts) - counts
    padded = (counts + MOE_BLOCK - 1) // MOE_BLOCK * MOE_BLOCK
    pad_ends = jnp.cumsum(padded)
    pad_starts = pad_ends - padded
    dest = pad_starts[sorted_expert] + (jnp.arange(n_assign) - starts[sorted_expert])
    rows = jnp.zeros((n_blocks * MOE_BLOCK, dm), h.dtype).at[dest].set(xt[sorted_token])
    block_start = jnp.arange(n_blocks) * MOE_BLOCK
    block_expert = jnp.minimum(jnp.searchsorted(pad_ends, block_start, side='right'), N_EXPERTS - 1)

    def expert_block(args):
        xb, e = args
        return (jax.nn.silu(xb @ w1[e]) * (xb @ w3[e])) @ w2[e]

    y_rows = lax.map(expert_block, (rows.reshape(n_blocks, MOE_BLOCK, dm), block_expert))
    y_sorted = y_rows.reshape(n_blocks * MOE_BLOCK, dm)[dest]
    contrib = y_sorted * gate_flat[order][:, None].astype(h.dtype)
    out = jax.ops.segment_sum(contrib, sorted_token, num_segments=n_tok)
    return out.reshape(bsz, seq, dm)

def first_inputs(seed: int = 0) -> dict:
    key = jax.random.key(seed)
    ks = list(jax.random.split(key, 40))
    cnt = [0]

    def nk():
        cnt[0] += 1
        return ks[cnt[0] - 1]

    def nrm(shape, scale):
        return scale * jax.random.normal(nk(), shape, jnp.float32)

    def gain(shape):
        return 1.0 + nrm(shape, 0.05)

    x = nrm((BATCH, SEQ, D_MODEL), 1.0)
    p = nrm((DEPTH, BATCH, SEQ, PLE_DIM), 1.0)
    positions = (jax.random.randint(nk(), (BATCH, 1), 0, 1024, jnp.int32)
                 + jnp.arange(SEQ, dtype=jnp.int32)[None, :])
    dsc = D_MODEL ** -0.5
    return {
        "x": x,
        "p": p,
        "positions": positions,
        "ln_mix": gain((DEPTH, D_MODEL)),
        "ln_ffn": gain((DEPTH, D_MODEL)),
        "ln_ple": gain((DEPTH, D_MODEL)),
        "a_w_in": nrm((N_EVEN, D_MODEL, EVEN_IN_WIDTH), dsc),
        "a_lambda": nrm((N_EVEN, 4, DA_HEAD_DIM), 0.1),
        "a_subln": gain((N_EVEN, DA_V_DIM)),
        "a_conv_w": nrm((N_EVEN, SC_WIDTH, SC_WIDTH_CONV), SC_WIDTH_CONV ** -0.5),
        "a_w_out": nrm((N_EVEN, DA_WIDTH + SC_WIDTH, D_MODEL), (DA_WIDTH + SC_WIDTH) ** -0.5),
        "ffn_w1": nrm((N_EVEN, D_MODEL, D_FF), dsc),
        "ffn_w3": nrm((N_EVEN, D_MODEL, D_FF), dsc),
        "ffn_w2": nrm((N_EVEN, D_FF, D_MODEL), D_FF ** -0.5),
        "c_w_in": nrm((N_ODD, D_MODEL, 2 * GM_WIDTH), dsc),
        "c_ln_g": gain((N_ODD, GM_WIDTH)),
        "c_ln_b": nrm((N_ODD, GM_WIDTH), 0.02),
        "c_w_s": nrm((N_ODD, GM_GROUPS, GM_CHUNK, GM_CHUNK), GM_CHUNK ** -0.5),
        "c_b_s": 1.0 + nrm((N_ODD, GM_GROUPS, GM_CHUNK), 0.1),
        "c_w_out": nrm((N_ODD, GM_WIDTH, D_MODEL), GM_WIDTH ** -0.5),
        "router_w": nrm((N_ODD, D_MODEL, N_EXPERTS), dsc),
        "moe_w1": nrm((N_ODD, N_EXPERTS, D_MODEL, D_FF), dsc),
        "moe_w3": nrm((N_ODD, N_EXPERTS, D_MODEL, D_FF), dsc),
        "moe_w2": nrm((N_ODD, N_EXPERTS, D_FF, D_MODEL), D_FF ** -0.5),
        "ple_gate": nrm((DEPTH, D_MODEL, D_MODEL), dsc),
        "ple_proj": nrm((DEPTH, PLE_DIM, D_MODEL), PLE_DIM ** -0.5),
        "final_norm": gain((D_MODEL,)),
    }

def first_block(x, p, positions, ln_mix, ln_ffn, ln_ple, a_w_in, a_lambda, a_subln, a_conv_w,
              a_w_out, ffn_w1, ffn_w3, ffn_w2, c_w_in, c_ln_g, c_ln_b, c_w_s, c_b_s, c_w_out,
              router_w, moe_w1, moe_w3, moe_w2, ple_gate, ple_proj, final_norm):
    h = x
    bsz, seq, _ = x.shape
    splits = [DA_QK_WIDTH, 2 * DA_QK_WIDTH, 2 * DA_QK_WIDTH + DA_WIDTH,
              2 * DA_QK_WIDTH + DA_WIDTH + SC_WIDTH, 2 * DA_QK_WIDTH + DA_WIDTH + 2 * SC_WIDTH]
    for i in range(DEPTH):
        j = i // 2
        hn = rms_norm(h, ln_mix[i])
        if i % 2 == 0:
            z = hn @ a_w_in[j]
            q, k, v, b_gate, c_gate, hc = jnp.split(z, splits, axis=-1)
            q = rope_partial(q.reshape(bsz, seq, DA_HEADS, 2, DA_HEAD_DIM), positions)
            k = rope_partial(k.reshape(bsz, seq, DA_HEADS, 2, DA_HEAD_DIM), positions)
            v = v.reshape(bsz, seq, DA_HEADS, DA_V_DIM)
            lambda_init = 0.8 - 0.6 * math.exp(-0.3 * i)
            lp = a_lambda[j].astype(jnp.float32)
            lam = jnp.exp(jnp.sum(lp[0] * lp[1])) - jnp.exp(jnp.sum(lp[2] * lp[3])) + lambda_init
            attn = diff_attention(q, k, v, lam, lambda_init, a_subln[j])
            conv = b_gate * causal_short_conv(c_gate * hc, a_conv_w[j])
            h = h + jnp.concatenate([attn, conv], axis=-1) @ a_w_out[j]
            h = h + swiglu(rms_norm(h, ln_ffn[i]), ffn_w1[j], ffn_w3[j], ffn_w2[j])
        else:
            z = jax.nn.gelu(hn @ c_w_in[j], approximate=False)
            u, vv = jnp.split(z, 2, axis=-1)
            vv = layer_norm(vv, c_ln_g[j], c_ln_b[j])
            h = h + spatial_gating(u, vv, c_w_s[j], c_b_s[j]) @ c_w_out[j]
            h = h + moe_swiglu(rms_norm(h, ln_ffn[i]), router_w[j], moe_w1[j], moe_w3[j], moe_w2[j])
        gate = jax.nn.sigmoid(rms_norm(h, ln_ple[i]) @ ple_gate[i])
        h = h + gate * (p[i] @ ple_proj[i])
    return rms_norm(h, final_norm)


HEAD_DIM = 64
D_MIX = D_MODEL
N_MIXERS = 4
N_GROUP_HEADS = D_MIX // (N_MIXERS * HEAD_DIM)
QB = 128
NEG = -1e30
TINY = 1e-30
BIG = 1e9

SWA_HEADS = N_GROUP_HEADS
SWA_KV_HEADS = 2
SWA_WINDOW = 128
MLA_HEADS = N_GROUP_HEADS
MLA_Q_RANK = 3 * D_MODEL // 16
MLA_KV_RANK = D_MODEL // 8
MLA_NOPE = 64
MLA_ROPE = 32
MLA_V = 64
ROPE_THETA_2 = 10000.0
NSA_HEADS = N_GROUP_HEADS
NSA_CMP_LEN = 32
NSA_CMP_STRIDE = 16
NSA_CMP_HIDDEN = 128
NSA_SEL_BLOCK = 64
NSA_TOPN = 16
NSA_WINDOW = 512
NSA_N_BRANCH = 3
MOBA_HEADS = N_GROUP_HEADS
MOBA_BLOCK = 256
MOBA_TOPK = 3
D_FF_2 = 4 * D_MODEL
N_ALIBI = SWA_HEADS + NSA_HEADS + MOBA_HEADS
N_ADA = 6

SWA_COLS = (SWA_HEADS + 2 * SWA_KV_HEADS) * HEAD_DIM
MLA_COLS = MLA_Q_RANK + MLA_KV_RANK + MLA_ROPE
NSA_COLS = NSA_HEADS * HEAD_DIM + 2 * NSA_N_BRANCH * HEAD_DIM + NSA_N_BRANCH * NSA_HEADS
MOBA_COLS = 3 * MOBA_HEADS * HEAD_DIM
D_IN = SWA_COLS + MLA_COLS + NSA_COLS + MOBA_COLS


def alibi_slopes():
    s = np.array([2.0 ** (-8.0 * (i + 1) / N_ALIBI) for i in range(N_ALIBI)], np.float32)
    return jnp.asarray(s[0::3]), jnp.asarray(s[1::3]), jnp.asarray(s[2::3])

def split_last(a, sizes):
    offs = np.cumsum([0] + list(sizes))
    return [a[..., int(offs[i]):int(offs[i + 1])] for i in range(len(sizes))]

def heads(t, n):
    B, S, W = t.shape
    return t.reshape(B, S, n, W // n).transpose(0, 2, 1, 3)

def merge_heads(t):
    B, H, S, d = t.shape
    return t.transpose(0, 2, 1, 3).reshape(B, S, H * d)

def unblock(o):
    nq, B, H, qb, d = o.shape
    return o.transpose(1, 2, 0, 3, 4).reshape(B, H, nq * qb, d)

def rmsnorm(x, g):
    xf = x.astype(jnp.float32)
    y = xf * lax.rsqrt(jnp.mean(xf * xf, axis=-1, keepdims=True) + RMS_EPS)
    return (y * g.astype(jnp.float32)).astype(x.dtype)

def rope(x, pos):
    half = x.shape[-1] // 2
    freqs = ROPE_THETA_2 ** (-jnp.arange(half, dtype=jnp.float32) / half)
    ang = pos[:, None] * freqs[None, :]
    cos, sin = jnp.cos(ang), jnp.sin(ang)
    x1 = x[..., :half].astype(jnp.float32)
    x2 = x[..., half:].astype(jnp.float32)
    return jnp.concatenate([x1 * cos - x2 * sin, x1 * sin + x2 * cos], axis=-1).astype(x.dtype)

def masked_softmax(s, mask, sink=None):
    s = jnp.where(mask, s.astype(jnp.float32), NEG)
    m = jnp.max(s, axis=-1, keepdims=True)
    if sink is not None:
        m = jnp.maximum(m, sink)
    e = jnp.where(mask, jnp.exp(s - m), 0.0)
    den = jnp.sum(e, axis=-1, keepdims=True)
    if sink is not None:
        den = den + jnp.exp(sink - m)
    return e / jnp.maximum(den, TINY)

def banded_attention(q, k, v, window, slopes, sink=None):
    B, KVH, G, S, d = q.shape
    nq = S // QB
    nb = window // QB
    kw = (nb + 1) * QB

    def band(t):
        tb = t.reshape(B, KVH, nq, QB, d)
        tp = jnp.pad(tb, ((0, 0), (0, 0), (nb, 0), (0, 0), (0, 0)))
        return jnp.concatenate([tp[:, :, i:i + nq] for i in range(nb + 1)], axis=3)

    kb, vb = band(k), band(v)
    qb = q.reshape(B, KVH, G, nq, QB, d)
    s = jnp.einsum('bkgnqd,bknsd->bkgnqs', qb, kb) * (d ** -0.5)
    dist = nb * QB + jnp.arange(QB)[:, None] - jnp.arange(kw)[None, :]
    key_pos = (jnp.arange(nq)[:, None] - nb) * QB + jnp.arange(kw)[None, :]
    mask = ((dist >= 0) & (dist < window))[None, :, :] & (key_pos >= 0)[:, None, :]
    bias = -slopes.astype(jnp.float32)[:, :, None, None, None] * dist
    sink_b = None if sink is None else sink.astype(jnp.float32)[None, :, :, None, None, None]
    p = masked_softmax(s.astype(jnp.float32) + bias, mask, sink_b).astype(v.dtype)
    o = jnp.einsum('bkgnqs,bknsd->bkgnqd', p, vb)
    return o.reshape(B, KVH * G, S, d)

def causal_attention_blocks(q, k, v, scale):
    B, H, S, dq = q.shape
    nq = S // QB
    qb = q.reshape(B, H, nq, QB, dq).transpose(2, 0, 1, 3, 4)
    kpos = jnp.arange(S)

    def one(args):
        qi, n = args
        tq = n * QB + jnp.arange(QB)
        s = jnp.einsum('bhqd,bhsd->bhqs', qi, k) * scale
        p = masked_softmax(s, kpos[None, :] <= tq[:, None]).astype(v.dtype)
        return jnp.einsum('bhqs,bhsd->bhqd', p, v)

    return unblock(lax.map(one, (qb, jnp.arange(nq))))

def swa_mixer(z, sinks, slopes):
    G = SWA_HEADS // SWA_KV_HEADS
    q, k, v = split_last(z, [SWA_HEADS * HEAD_DIM, SWA_KV_HEADS * HEAD_DIM, SWA_KV_HEADS * HEAD_DIM])
    q = heads(q, SWA_HEADS)
    B, _, S, d = q.shape
    q = q.reshape(B, SWA_KV_HEADS, G, S, d)
    o = banded_attention(q, heads(k, SWA_KV_HEADS), heads(v, SWA_KV_HEADS), SWA_WINDOW,
                         slopes.reshape(SWA_KV_HEADS, G), sinks.reshape(SWA_KV_HEADS, G))
    return merge_heads(o)

def mla_mixer(z, q_norm_g, kv_norm_g, w_uq, w_ukv):
    cq, ckv, k_pe = split_last(z, [MLA_Q_RANK, MLA_KV_RANK, MLA_ROPE])
    B, S, _ = z.shape
    pos = jnp.arange(S, dtype=jnp.float32)
    q = heads(rmsnorm(cq, q_norm_g) @ w_uq, MLA_HEADS)
    kv = heads(rmsnorm(ckv, kv_norm_g) @ w_ukv, MLA_HEADS)
    q = jnp.concatenate([q[..., :MLA_NOPE], rope(q[..., MLA_NOPE:], pos)], axis=-1)
    k_pe = jnp.broadcast_to(rope(k_pe, pos)[:, None], (B, MLA_HEADS, S, MLA_ROPE))
    k = jnp.concatenate([kv[..., :MLA_NOPE], k_pe], axis=-1)
    v = kv[..., MLA_NOPE:]
    o = causal_attention_blocks(q, k, v, (MLA_NOPE + MLA_ROPE) ** -0.5)
    return merge_heads(o)

def nsa_mixer(z, slopes, pos_k, pos_v, ck_w1, ck_w2, cv_w1, cv_w2):
    d, H = HEAD_DIM, NSA_HEADS
    q, kc, vc, ks, vs, kw, vw, gl = split_last(z, [H * d, d, d, d, d, d, d, NSA_N_BRANCH * H])
    B, S, _ = z.shape
    q = heads(q, H)
    scale = d ** -0.5
    ratio = NSA_CMP_LEN // NSA_CMP_STRIDE
    n_cmp = S // NSA_CMP_STRIDE - ratio + 1

    def compress(t, pos_emb, w1, w2):
        ch = t.reshape(B, S // NSA_CMP_STRIDE, NSA_CMP_STRIDE, d)
        blk = jnp.concatenate([ch[:, i:i + n_cmp] for i in range(ratio)], axis=2) + pos_emb
        return jax.nn.gelu(blk.reshape(B, n_cmp, NSA_CMP_LEN * d) @ w1) @ w2

    k_cmp = compress(kc, pos_k, ck_w1, ck_w2)
    v_cmp = compress(vc, pos_v, cv_w1, cv_w2)
    cmp_end = jnp.arange(n_cmp) * NSA_CMP_STRIDE + NSA_CMP_LEN - 1
    n_sel = S // NSA_SEL_BLOCK
    topn = min(NSA_TOPN, n_sel)
    sel_ratio = NSA_SEL_BLOCK // NSA_CMP_STRIDE
    n_off = sel_ratio + ratio - 1
    k_sel = ks.reshape(B, n_sel, NSA_SEL_BLOCK, d)
    v_sel = vs.reshape(B, n_sel, NSA_SEL_BLOCK, d)
    nq = S // QB
    qb = q.reshape(B, H, nq, QB, d).transpose(2, 0, 1, 3, 4)
    m = slopes.astype(jnp.float32)[None, :, None, None]
    blk_ids = jnp.arange(n_sel)
    bi = jnp.arange(B)[:, None, None]
    nk = topn * NSA_SEL_BLOCK

    def one(args):
        qi, n = args
        tq = n * QB + jnp.arange(QB)
        dist_c = tq[:, None] - cmp_end[None, :]
        s_c = jnp.einsum('bhqd,bcd->bhqc', qi, k_cmp) * scale
        p_c = masked_softmax(s_c.astype(jnp.float32) - m * dist_c, dist_c >= 0)
        o_c = jnp.einsum('bhqc,bcd->bhqd', p_c.astype(v_cmp.dtype), v_cmp)
        pp = jnp.pad(p_c.sum(axis=1), ((0, 0), (0, 0), (ratio - 1, sel_ratio)))
        imp = sum(pp[..., o::sel_ratio][..., :n_sel] for o in range(n_off))
        cur = tq // NSA_SEL_BLOCK
        cand = blk_ids[None, :] <= cur[:, None]
        forced = (blk_ids[None, :] == 0) | (blk_ids[None, :] == cur[:, None]) | (blk_ids[None, :] == cur[:, None] - 1)
        imp = jnp.where(cand, jnp.where(forced, BIG, imp), NEG)
        _, idx = lax.top_k(imp, topn)
        valid = jnp.take_along_axis(jnp.broadcast_to(cand, imp.shape), idx, axis=-1)
        kg = k_sel[bi, idx].reshape(B, QB, nk, d)
        vg = v_sel[bi, idx].reshape(B, QB, nk, d)
        key_pos = (idx[..., None] * NSA_SEL_BLOCK + jnp.arange(NSA_SEL_BLOCK)).reshape(B, QB, nk)
        dist_s = tq[None, :, None] - key_pos
        mask_s = (jnp.repeat(valid, NSA_SEL_BLOCK, axis=-1) & (dist_s >= 0))[:, None]
        s_s = jnp.einsum('bhqd,bqkd->bhqk', qi, kg) * scale
        p_s = masked_softmax(s_s.astype(jnp.float32) - m * dist_s[:, None], mask_s)
        o_s = jnp.einsum('bhqk,bqkd->bhqd', p_s.astype(vg.dtype), vg)
        return o_c, o_s

    o_c, o_s = lax.map(one, (qb, jnp.arange(nq)))
    o_c, o_s = unblock(o_c), unblock(o_s)
    o_w = banded_attention(q[:, None], heads(kw, 1), heads(vw, 1), NSA_WINDOW, slopes[None, :], None)
    g = jax.nn.sigmoid(gl.astype(jnp.float32)).reshape(B, S, NSA_N_BRANCH, H).transpose(0, 3, 1, 2).astype(q.dtype)
    o = g[..., 0:1] * o_c + g[..., 1:2] * o_s + g[..., 2:3] * o_w
    return merge_heads(o)

def moba_mixer(z, slopes):
    d, H = HEAD_DIM, MOBA_HEADS
    q, k, v = [heads(t, H) for t in split_last(z, [H * d] * 3)]
    B, _, S, _ = q.shape
    scale = d ** -0.5
    n_blk = -(-S // MOBA_BLOCK)
    pad = n_blk * MOBA_BLOCK - S
    kp = jnp.pad(k, ((0, 0), (0, 0), (0, pad), (0, 0)))
    vp = jnp.pad(v, ((0, 0), (0, 0), (0, pad), (0, 0)))
    k_blk = kp.reshape(B, H, n_blk, MOBA_BLOCK, d)
    v_blk = vp.reshape(B, H, n_blk, MOBA_BLOCK, d)
    k_mean = jnp.mean(k_blk, axis=3)
    topk = min(MOBA_TOPK, n_blk)
    nq = S // QB
    qb = q.reshape(B, H, nq, QB, d).transpose(2, 0, 1, 3, 4)
    m = slopes.astype(jnp.float32)[None, :, None, None]
    bi = jnp.arange(B)[:, None, None, None]
    hi = jnp.arange(H)[None, :, None, None]
    blk_ids = jnp.arange(n_blk)
    ng = topk * MOBA_BLOCK

    def one(args):
        qi, n = args
        tq = n * QB + jnp.arange(QB)
        cur = (n * QB) // MOBA_BLOCK
        gate = jnp.einsum('bhqd,bhjd->bhqj', qi, k_mean).astype(jnp.float32)
        gate = jnp.where(blk_ids < cur, gate, NEG)
        _, idx = lax.top_k(gate, topk)
        valid = idx < cur
        kg = k_blk[bi, hi, idx].reshape(B, H, QB, ng, d)
        vg = v_blk[bi, hi, idx].reshape(B, H, QB, ng, d)
        key_pos = (idx[..., None] * MOBA_BLOCK + jnp.arange(MOBA_BLOCK)).reshape(B, H, QB, ng)
        s_g = jnp.einsum('bhqd,bhqkd->bhqk', qi, kg) * scale - m * (tq[:, None] - key_pos)
        mask_g = jnp.repeat(valid, MOBA_BLOCK, axis=-1)
        start = cur * MOBA_BLOCK
        k_own = lax.dynamic_slice_in_dim(kp, start, MOBA_BLOCK, axis=2)
        v_own = lax.dynamic_slice_in_dim(vp, start, MOBA_BLOCK, axis=2)
        dist_own = tq[:, None] - (start + jnp.arange(MOBA_BLOCK))[None, :]
        s_o = jnp.einsum('bhqd,bhsd->bhqs', qi, k_own) * scale - m * dist_own
        mask_o = jnp.broadcast_to(dist_own >= 0, s_o.shape)
        p = masked_softmax(jnp.concatenate([s_g, s_o], axis=-1),
                           jnp.concatenate([mask_g, mask_o], axis=-1)).astype(v.dtype)
        return (jnp.einsum('bhqk,bhqkd->bhqd', p[..., :ng], vg)
                + jnp.einsum('bhqs,bhsd->bhqd', p[..., ng:], v_own))

    return merge_heads(unblock(lax.map(one, (qb, jnp.arange(nq)))))

def second_inputs(seed: int = 0) -> dict:
    key = jax.random.key(seed)
    ks = jax.random.split(key, 24)
    f32 = jnp.float32

    def nrm(k, shape, s):
        return jax.random.normal(k, shape, f32) * s

    return {
        'x': nrm(ks[0], (BATCH, SEQ, D_MODEL), 1.0),
        'c': nrm(ks[1], (BATCH, D_MODEL), 1.0),
        'norm_mix_g': 1.0 + nrm(ks[2], (DEPTH, D_MODEL), 0.02),
        'norm_mlp_g': 1.0 + nrm(ks[3], (DEPTH, D_MODEL), 0.02),
        'w_ada': nrm(ks[4], (DEPTH, D_MODEL, N_ADA * D_MODEL), 0.5 * D_MODEL ** -0.5),
        'b_ada': nrm(ks[5], (DEPTH, N_ADA * D_MODEL), 0.01),
        'w_in': nrm(ks[6], (DEPTH, D_MODEL, D_IN), D_MODEL ** -0.5),
        'w_out': nrm(ks[7], (DEPTH, D_MIX, D_MODEL), D_MIX ** -0.5),
        'swa_sinks': nrm(ks[8], (DEPTH, SWA_HEADS), 1.0),
        'mla_q_norm_g': 1.0 + nrm(ks[9], (DEPTH, MLA_Q_RANK), 0.02),
        'mla_kv_norm_g': 1.0 + nrm(ks[10], (DEPTH, MLA_KV_RANK), 0.02),
        'mla_w_uq': nrm(ks[11], (DEPTH, MLA_Q_RANK, MLA_HEADS * (MLA_NOPE + MLA_ROPE)), MLA_Q_RANK ** -0.5),
        'mla_w_ukv': nrm(ks[12], (DEPTH, MLA_KV_RANK, MLA_HEADS * (MLA_NOPE + MLA_V)), MLA_KV_RANK ** -0.5),
        'nsa_cmp_pos_k': nrm(ks[13], (DEPTH, NSA_CMP_LEN, HEAD_DIM), 0.02),
        'nsa_cmp_pos_v': nrm(ks[14], (DEPTH, NSA_CMP_LEN, HEAD_DIM), 0.02),
        'nsa_cmp_k_w1': nrm(ks[15], (DEPTH, NSA_CMP_LEN * HEAD_DIM, NSA_CMP_HIDDEN), (NSA_CMP_LEN * HEAD_DIM) ** -0.5),
        'nsa_cmp_k_w2': nrm(ks[16], (DEPTH, NSA_CMP_HIDDEN, HEAD_DIM), NSA_CMP_HIDDEN ** -0.5),
        'nsa_cmp_v_w1': nrm(ks[17], (DEPTH, NSA_CMP_LEN * HEAD_DIM, NSA_CMP_HIDDEN), (NSA_CMP_LEN * HEAD_DIM) ** -0.5),
        'nsa_cmp_v_w2': nrm(ks[18], (DEPTH, NSA_CMP_HIDDEN, HEAD_DIM), NSA_CMP_HIDDEN ** -0.5),
        'w_up': nrm(ks[19], (DEPTH, D_MODEL, D_FF_2), D_MODEL ** -0.5),
        'w_down': nrm(ks[20], (DEPTH, D_FF_2, D_MODEL), D_FF_2 ** -0.5),
        'final_norm_g': 1.0 + nrm(ks[21], (D_MODEL,), 0.02),
    }

def second_block(x, c, norm_mix_g, norm_mlp_g, w_ada, b_ada, w_in, w_out, swa_sinks,
              mla_q_norm_g, mla_kv_norm_g, mla_w_uq, mla_w_ukv,
              nsa_cmp_pos_k, nsa_cmp_pos_v, nsa_cmp_k_w1, nsa_cmp_k_w2, nsa_cmp_v_w1, nsa_cmp_v_w2,
              w_up, w_down, final_norm_g):
    slopes_a, slopes_c, slopes_d = alibi_slopes()
    c_act = jax.nn.silu(c)
    for l in range(DEPTH):
        mod = c_act @ w_ada[l] + b_ada[l]
        sh1, sc1, g1, sh2, sc2, g2 = [t[:, None, :] for t in jnp.split(mod, N_ADA, axis=-1)]
        h = rmsnorm(x, norm_mix_g[l]) * (1.0 + sc1) + sh1
        z = h @ w_in[l]
        za, zb, zc, zd = split_last(z, [SWA_COLS, MLA_COLS, NSA_COLS, MOBA_COLS])
        o = jnp.concatenate([
            swa_mixer(za, swa_sinks[l], slopes_a),
            mla_mixer(zb, mla_q_norm_g[l], mla_kv_norm_g[l], mla_w_uq[l], mla_w_ukv[l]),
            nsa_mixer(zc, slopes_c, nsa_cmp_pos_k[l], nsa_cmp_pos_v[l],
                      nsa_cmp_k_w1[l], nsa_cmp_k_w2[l], nsa_cmp_v_w1[l], nsa_cmp_v_w2[l]),
            moba_mixer(zd, slopes_d),
        ], axis=-1)
        x = x + g1 * (o @ w_out[l])
        h = rmsnorm(x, norm_mlp_g[l]) * (1.0 + sc2) + sh2
        x = x + g2 * (jnp.square(jax.nn.relu(h @ w_up[l])) @ w_down[l])
    return rmsnorm(x, final_norm_g)


def setup_inputs(seed=0):
    out = dict(first_inputs(seed))
    for name, value in second_inputs(seed + 1).items():
        if name != "x":
            out[name + "_2"] = value
    return out


def reference(
    x, p, positions, ln_mix, ln_ffn, ln_ple, a_w_in, a_lambda, a_subln, a_conv_w, a_w_out,
    ffn_w1, ffn_w3, ffn_w2, c_w_in, c_ln_g, c_ln_b, c_w_s, c_b_s, c_w_out, router_w, moe_w1,
    moe_w3, moe_w2, ple_gate, ple_proj, final_norm, c_2, norm_mix_g_2, norm_mlp_g_2, w_ada_2,
    b_ada_2, w_in_2, w_out_2, swa_sinks_2, mla_q_norm_g_2, mla_kv_norm_g_2, mla_w_uq_2,
    mla_w_ukv_2, nsa_cmp_pos_k_2, nsa_cmp_pos_v_2, nsa_cmp_k_w1_2, nsa_cmp_k_w2_2,
    nsa_cmp_v_w1_2, nsa_cmp_v_w2_2, w_up_2, w_down_2, final_norm_g_2,
):
    x = first_block(
        x, p, positions, ln_mix, ln_ffn, ln_ple, a_w_in, a_lambda, a_subln, a_conv_w, a_w_out,
        ffn_w1, ffn_w3, ffn_w2, c_w_in, c_ln_g, c_ln_b, c_w_s, c_b_s, c_w_out, router_w, moe_w1,
        moe_w3, moe_w2, ple_gate, ple_proj, final_norm,
    )
    return second_block(
        x, c_2, norm_mix_g_2, norm_mlp_g_2, w_ada_2, b_ada_2, w_in_2, w_out_2, swa_sinks_2,
        mla_q_norm_g_2, mla_kv_norm_g_2, mla_w_uq_2, mla_w_ukv_2, nsa_cmp_pos_k_2,
        nsa_cmp_pos_v_2, nsa_cmp_k_w1_2, nsa_cmp_k_w2_2, nsa_cmp_v_w1_2, nsa_cmp_v_w2_2, w_up_2,
        w_down_2, final_norm_g_2,
    )


_drawn_inputs = setup_inputs


def setup_inputs(seed=0):
    import zlib

    import numpy as np

    out = dict(_drawn_inputs(seed))
    spreads = {}
    factors = {'ln_ple': 3.44,
     'c_ln_b': 4.944,
     'norm_mix_g_2': 8.0,
     'norm_mlp_g_2': 4.542,
     'b_ada_2': 2.674,
     'swa_sinks_2': 28.112,
     'mla_q_norm_g_2': 8.0,
     'mla_kv_norm_g_2': 8.0,
     'nsa_cmp_pos_k_2': 8.0,
     'nsa_cmp_pos_v_2': 31.15,
     'nsa_cmp_k_w1_2': 4.334,
     'nsa_cmp_k_w2_2': 4.198,
     'final_norm_g_2': 8.293}
    for name, (base, spread) in spreads.items():
        noise = np.random.default_rng([zlib.crc32(name.encode()), seed]).standard_normal(out[name].shape)
        drawn = base * np.exp(spread * noise) if base else spread * noise
        out[name] = jnp.asarray(drawn.astype(out[name].dtype))
    for name, factor in factors.items():
        out[name] = (out[name] * factor).astype(out[name].dtype)
    return out
```

```python
import math
from contextlib import ExitStack

import numpy as np
import concourse.bass as bass
from concourse import mybir

F32 = mybir.dt.float32
I32 = mybir.dt.int32
U32 = mybir.dt.uint32
ALU = mybir.AluOpType
ACT = mybir.ActivationFunctionType
AX = mybir.AxisListType

P = 128
D = 1024
S = 256
KT = D // P
QB = S // P
BANK = 512
SLOT = 2048
RING = 11
F1 = 2816
NE = 8
J1 = F1 // 256
F2 = 4 * D
J2 = F2 // 256
NCMP = S // 16 - 1
RMS_EPS = 1e-6
LN_EPS = 1e-5
NEG = -1e30
GUARD = -1e20
TINY = 1e-30
LAMBDA_INIT = 0.8 - 0.6 * math.exp(-0.3 * 0)
SLOPES = [float(np.float32(2.0 ** (-8.0 * (i + 1) / 12))) for i in range(12)]
NT = 18
(T_SWAQ, T_SWAK, T_CKV, T_CQ, T_KPE, T_GATE, T_NSAQ, T_KC, T_VC, T_KS, T_KW, T_MOBQ,
 T_MOBK) = (0, 2, 3, 4, 6, 7, 8, 10, 11, 12, 13, 14, 16)

W_QK = 0
W_BCH = W_QK + 4
W_V = W_BCH + 6
W_OUT0 = W_V + 2
W_FFN0 = W_OUT0 + 4
W_PLE0 = W_FFN0 + 3 * J1
W_CIN = W_PLE0 + 5
W_COUT = W_CIN + 8
W_MOE = W_COUT + 4
W_PLE1 = W_MOE + 3 * J1 * NE
W_BLK = W_PLE1 + 5
B_ADAC, B_ADAR, B_IN, B_V, B_CMP, B_SMALL, B_OUT, B_MLP = 0, 16, 24, 33, 35, 37, 38, 42
B_ALL = B_MLP + 2 * J2
SLOTS = W_BLK + 2 * B_ALL

COLS = {}
_at = 0
for _n, _w in [("gain", 80), ("subln", 1), ("conv", 12), ("invf", 1), ("bs", 8), ("router", 64),
               ("iota", 8), ("c", 8), ("bada", 64), ("mlag", 6), ("pos", 64), ("nsac", 2 * NCMP),
               ("ident", P), ("rot0", P), ("rotm", P), ("cosm", S), ("sinm", S),
               ("alibi", 2 * S), ("causal", 2 * S), ("window", 2 * S), ("ple", 4 * S)]:
    COLS[_n] = (_at, _at + _w)
    _at += _w
NCOLS = _at

NORMS = ["mix0", "ffn0", "ple0", "mix1", "ffn1", "ple1", "b0mix", "b0mlp", "b1mix", "b1mlp"]


def attention_groups(block_layer):
    if block_layer is None:
        return [("diff", qb, hg) for qb in range(QB) for hg in range(2)]
    return [(kind, qb, 0) for qb in range(QB) for kind in ("swa", "moba", "nsac", "nsas", "nsaw", "mla")]


def head_of(kind, u):
    return 2 * (u % 2) + u // 2 if kind in ("moba", "nsac", "nsas", "nsaw") else u


GROUP_BASE = [0, 4, 16]


def swiglu_up(j):
    return 3 * j if j else 1


def mlp_up(j):
    return 2 * j - 1 if j else 0


def build(nc, a, out):
    stream, consts, pos, lam_in, ln_rows, w_s, sinks, bada_rows, fin_row, x_in = (
        a[n] for n in ("stream", "consts", "pos", "lam", "ln_rows", "w_s", "sinks", "bada_rows", "fin_row", "x"))
    with ExitStack() as ctx:
        def sb(name, shape, dt=F32):
            return ctx.enter_context(nc.sbuf_tensor(name, shape, dt))

        def sem(name):
            return ctx.enter_context(nc.semaphore(name))

        ps = ctx.enter_context(nc.psum_tensor("ps", [P, 8, BANK], F32))
        ring = sb("ring", [P, RING, SLOT])
        resid = sb("resid", [P, QB, D])
        xT = sb("xT", [P, KT, S])
        rows = sb("rows", [P, QB, D])
        catT = sb("catT", [P, KT, S])
        arena = sb("arena", [P, 8192])
        score = sb("score", [P, 2, 4, S + 1])
        probT = sb("probT", [P, 2, 8, P])
        grow = sb("grow", [P, 2, D])
        c_all = sb("c_all", [P, KT, P])
        con = sb("con", [P, NCOLS])
        ones = sb("ones", [P, P])
        zeros = sb("zeros", [P, P])
        stat = sb("stat", [P, 16])
        neghalf = sb("neghalf", [P, 8])
        soft = sb("soft", [P, 2, 4, 4])
        csilu = sb("csilu", [P, KT])
        ada = sb("ada", [P, 32])
        modg = sb("modg", [P, 2, 8])
        lam = sb("lam", [P, 8])
        lamv = sb("lamv", [P, 4 * 64])
        sink = sb("sink", [P, 2, 4])
        sub8 = sb("sub8", [P, 1])
        bn = sb("bn", [P, 2, 2, 6])
        mv = sb("mv", [P, 2, 2])
        posi = sb("posi", [P, S], I32)
        gates = sb("gates", [P, QB, 16])
        top = sb("top", [P, QB, 8])
        topi = sb("topi", [P, QB, 8], U32)
        route = sb("route", [P, QB, 4, 8])
        logit = sb("logit", [P, QB, 8])
        hidc = sb("hidc", [P, 2, 16])
        kcmp = sb("kcmp", [P, 16])
        vcmp = sb("vcmp", [P, 64])

        def col(name, a=0, n=None):
            lo, hi = COLS[name]
            return con[:, lo + a:(lo + a + n if n is not None else hi)]

        ident = col("ident")
        zqk = arena[:, 0:2048].rearrange("p (t s) -> p t s", s=S)
        zbch = arena[:, 2048:5120].rearrange("p (t s) -> p t s", s=S)
        v1 = arena[:, 5120:6144].rearrange("p (b n) -> p b n", b=QB)
        cos0, sin0 = arena[:, 6144:6400], arena[:, 6400:6656]
        ang, turns = arena[:, 6656:6912], arena[:, 6912:7168]
        u_rows = arena[:, 0:2048].rearrange("p (b n) -> p b n", b=QB)
        v_rows = arena[:, 2048:4096].rearrange("p (b n) -> p b n", b=QB)
        ln_g, ln_b = arena[:, 4096:5120], arena[:, 5120:6144]
        ws = arena[:, 6144:7168].rearrange("p (g t) -> p g t", g=8)
        egate = arena[:, 0:2048].rearrange("p (e s) -> p e s", e=NE)
        ediag = arena[:, 2048:4096].rearrange("p (b e s) -> p b e s", b=QB, e=NE)
        zT = arena[:, 0:NT * S].rearrange("p (t s) -> p t s", s=S)
        v2 = arena[:, 4608:5632].rearrange("p (b n) -> p b n", b=QB)
        qm = arena[:, 5632:6656].rearrange("p (h s) -> p h s", h=4)
        km = arena[:, 6656:7680].rearrange("p (h s) -> p h s", h=4)
        vm = arena[:, 7680:8192].rearrange("p (b n) -> p b n", b=QB)
        flat0 = score[:, 0].rearrange("p a b -> p (a b)")
        flat1 = score[:, 1].rearrange("p a b -> p (a b)")
        blk = flat1[:, 0:2 * 16 * NCMP].rearrange("p (v l n) -> p v l n", v=2, n=NCMP)
        acth = catT[:, 0:4].rearrange("p (q a) s -> p q (a s)", q=2)
        hidT = catT[:, 4:8].rearrange("p (q a) s -> p q (a s)", q=2)

        def bank(b, n=1):
            return ps[:, b:b + n, :].rearrange("p b n -> p (b n)")

        landed = [sem(f"landed{r}") for r in range(RING)]
        slot_done = sem("slot_done")
        consts_in = sem("consts_in")
        ln_in = sem("ln_in")
        fin_in = sem("fin_in")
        bada_in = sem("bada_in")
        out_done = sem("out_done")
        consts_made = sem("consts_made")
        root_asked = sem("root_asked")
        root_ready = sem("root_ready")
        rows_scaled = sem("rows_scaled")
        rowsT_ready = sem("rowsT_ready")
        normed = sem("normed")
        projT_kept = sem("projT_kept")
        vrows_kept = sem("vrows_kept")
        angles_ready = sem("angles_ready")
        sines_ready = sem("sines_ready")
        rot_ready = sem("rot_ready")
        roped = sem("roped")
        conv_ready = sem("conv_ready")
        lam_asked = sem("lam_asked")
        lam_exp = sem("lam_exp")
        scores_ready = sem("scores_ready")
        shifted = sem("shifted")
        exp_ready = sem("exp_ready")
        probT_ready = sem("probT_ready")
        probT_kept = sem("probT_kept")
        mixed_ready = sem("mixed_ready")
        mixed_kept = sem("mixed_kept")
        heads_ready = sem("heads_ready")
        catT_ready = sem("catT_ready")
        catT_kept = sem("catT_kept")
        resid_ready = sem("resid_ready")
        act_ready = sem("act_ready")
        hid_ready = sem("hid_ready")
        ple_gated = sem("ple_gated")
        gelu_done = sem("gelu_done")
        vn_ready = sem("vn_ready")
        ws_masked = sem("ws_masked")
        spatial_ready = sem("spatial_ready")
        spatial_gated = sem("spatial_gated")
        logits_ready = sem("logits_ready")
        route_asked = sem("route_asked")
        route_exp = sem("route_exp")
        ediag_ready = sem("ediag_ready")
        egate_ready = sem("egate_ready")
        egate_kept = sem("egate_kept")
        egated = sem("egated")
        moe_ready = sem("moe_ready")
        csilu_ready = sem("csilu_ready")
        mod_ready = sem("mod_ready")
        grow_ready = sem("grow_ready")
        squares_ready = sem("squares_ready")
        latsum_ready = sem("latsum_ready")
        latms_ready = sem("latms_ready")
        latroot_ready = sem("latroot_ready")
        latent_ready = sem("latent_ready")
        mlaheads_ready = sem("mlaheads_ready")
        mlaheads_kept = sem("mlaheads_kept")
        mlarot_ready = sem("mlarot_ready")
        mla_ready = sem("mla_ready")
        cmpblk_ready = sem("cmpblk_ready")
        cmpact_ready = sem("cmpact_ready")
        cmp_kept = sem("cmp_kept")
        gateT_ready = sem("gateT_ready")
        gates_ready = sem("gates_ready")
        sink_ready = sem("sink_ready")
        dve_step = sem("dve_step")
        act_step = sem("act_step")
        pool_step = sem("pool_step")

        def bc(ap, n):
            return ap.unsqueeze(2).broadcast_to([ap.shape[0], ap.shape[1], n])

        def rep(ap, n):
            return ap.unsqueeze(1).broadcast_to([ap.shape[0], n, ap.shape[1]])

        block = ctx.enter_context(nc.Block())

        @block.sync
        def _(sp):
            for r in range(RING):
                sp.dma_start(ring[:, r, :], stream[r]).then_inc(landed[r], 16)
            laps = SLOTS // RING
            with sp.Fori(1, laps) as lap:
                for r in range(RING):
                    sp.wait_ge(slot_done, lap * RING + (r + 1 - RING))
                    sp.dma_start(ring[:, r, :], stream[bass.ds(lap * RING + r, 1)].rearrange("a p n -> (a p) n"))\
                        .then_inc(landed[r], 16)
            for n in range(laps * RING, SLOTS):
                sp.wait_ge(slot_done, n + 1 - RING)
                sp.dma_start(ring[:, n % RING, :], stream[n]).then_inc(landed[n % RING], 16)
            sp.wait_ge(resid_ready, 12)
            sp.dma_start(out.rearrange("(b p) n -> p b n", p=P), rows[:, :, :]).then_inc(out_done, 16)
            sp.wait_ge(out_done, 16)

        @block.tensor
        def _(pe):
            def slot(n):
                pe.wait_ge(landed[n % RING], 16 * (n // RING + 1))
                return ring[:, n % RING, :]

            def rowsT(k):
                for t in range(QB):
                    pe.wait_ge(rows_scaled, QB * (k + (k >= 6)) + t + 1)
                    for half in range(2):
                        for i in range(4):
                            f = 4 * half + i
                            last = pe.transpose(ps[:, 4 + 2 * t + half, i * P:(i + 1) * P],
                                                rows[:, t, f * P:(f + 1) * P], ident)
                        last.then_inc(rowsT_ready, 1)
                pe.wait_ge(normed, 4 * (k + 1))

            def tiles(n0, count, job0, fresh):
                for s in range(count):
                    w = slot(n0 + s).rearrange("p (k n) -> p k n", k=KT)
                    if s >= 4 or not fresh:
                        pe.wait_ge(projT_kept, job0 + s - 3)
                    for i in range(2):
                        for k in range(KT):
                            last = pe.matmul(ps[:, s % 4, i * S:(i + 1) * S], w[:, k, i * P:(i + 1) * P],
                                             xT[:, k, :], start=k == 0, stop=k == KT - 1)
                    last.then_inc(slot_done, 1)

            def row_product(n0, src, b0):
                for s in range(4):
                    w = slot(n0 + s).rearrange("p (k n) -> p k n", k=2)
                    for kk in range(2):
                        for t in range(QB):
                            for half in range(2):
                                k = 2 * s + kk
                                last = pe.matmul(ps[:, b0 + 2 * t + half, :], src[:, k, t * P:(t + 1) * P],
                                                 w[:, kk, half * BANK:(half + 1) * BANK],
                                                 start=k == 0, stop=k == KT - 1)
                    last.then_inc(slot_done, 1)

            def value_rows(n0):
                for s in range(2):
                    w = slot(n0 + s).rearrange("p (k n) -> p k n", k=4)
                    for kk in range(4):
                        for t in range(QB):
                            k = 4 * s + kk
                            last = pe.matmul(ps[:, 4 + t, :], xT[:, k, t * P:(t + 1) * P], w[:, kk, :],
                                             start=k == 0, stop=k == KT - 1)
                    last.then_inc(slot_done, 1)

            def cat_transpose(tiles_):
                for t in range(QB):
                    for half in range(tiles_ // 4):
                        for i in range(4):
                            f = 4 * half + i
                            last = pe.transpose(ps[:, 4 + 2 * t + half, i * P:(i + 1) * P],
                                                rows[:, t, f * P:(f + 1) * P], ident)
                        last.then_inc(catT_ready, 1)

            def attention(layer):
                groups = attention_groups(layer)
                base = GROUP_BASE[0 if layer is None else layer + 1]

                def scores(i):
                    kind, qb, hg = groups[i]
                    g = base + i
                    if i >= 2:
                        pe.wait_ge(shifted, g - 1)
                    kw = NCMP if kind == "nsac" else P * (qb + 1)
                    qs = slice(qb * P, (qb + 1) * P)
                    for u in range(4):
                        if kind == "diff":
                            r, h = 64 * (u // 2), 2 * hg + u % 2
                            q, k = zqk[r:r + 64, h, qs], zqk[r:r + 64, 4 + h, 0:kw]
                        elif kind == "swa":
                            r = 64 * (u // 2)
                            q, k = zT[r:r + 64, T_SWAQ + u % 2, qs], zT[r:r + 64, T_SWAK, 0:kw]
                        elif kind == "moba":
                            r = 64 * (u // 2)
                            q, k = zT[r:r + 64, T_MOBQ + u % 2, qs], zT[r:r + 64, T_MOBK + u % 2, 0:kw]
                        elif kind == "mla":
                            q, k = qm[:, u, qs], km[:, u, 0:kw]
                        else:
                            r = 64 * (u // 2)
                            q = zT[r:r + 64, T_NSAQ + u % 2, qs]
                            k = {"nsac": kcmp[r:r + 64, 0:NCMP], "nsas": zT[r:r + 64, T_KS, 0:kw],
                                 "nsaw": zT[r:r + 64, T_KW, 0:kw]}[kind]
                        last = pe.matmul(ps[:, 2 * (g % 2) + u // 2, (u % 2) * S:(u % 2) * S + kw], q, k,
                                         start=True, stop=True)
                    last.then_inc(scores_ready, 1)

                def transposes(i):
                    kind, qb, hg = groups[i]
                    g = base + i
                    pe.wait_ge(exp_ready, g + 1)
                    pe.wait_ge(probT_kept, g)
                    nkb = 1 if kind == "nsac" else qb + 1
                    kp = NCMP if kind == "nsac" else P
                    for u in range(4):
                        for kb in range(nkb):
                            n = u * nkb + kb
                            last = pe.transpose(ps[0:kp, 4 + n // 4, (n % 4) * P:(n % 4 + 1) * P],
                                                score[:, g % 2, u, kb * P:kb * P + kp], ident)
                    last.then_inc(probT_ready, 1)

                def mix(i):
                    kind, qb, hg = groups[i]
                    g = base + i
                    pe.wait_ge(probT_kept, g + 1)
                    if i >= 2:
                        pe.wait_ge(mixed_kept, g - 1)
                    nkb = 1 if kind == "nsac" else qb + 1
                    kp = NCMP if kind == "nsac" else P
                    vw = P if kind == "diff" else 64
                    for u in range(4):
                        o = head_of(kind, u)
                        for kb in range(nkb):
                            if kind == "diff":
                                h = 2 * hg + u % 2
                                v = v1[:, kb, h * P:(h + 1) * P]
                            elif kind == "swa":
                                v = v2[:, kb, (o // 2) * 64:(o // 2) * 64 + 64]
                            elif kind == "nsas":
                                v = v2[:, kb, 128:192]
                            elif kind == "nsaw":
                                v = v2[:, kb, 192:256]
                            elif kind == "moba":
                                v = v2[:, kb, 256 + o * 64:256 + o * 64 + 64]
                            elif kind == "mla":
                                v = vm[:, kb, o * 64:o * 64 + 64]
                            else:
                                v = vcmp[0:kp, :]
                            last = pe.matmul(ps[:, 6 + g % 2, o * vw:(o + 1) * vw],
                                             probT[0:kp, g % 2, u * nkb + kb, :], v,
                                             start=kb == 0, stop=kb == nkb - 1)
                    last.then_inc(mixed_ready, 1)

                scores(0)
                for i in range(len(groups)):
                    if i + 1 < len(groups):
                        scores(i + 1)
                    transposes(i)
                    mix(i)

            def up(slots, j, ready):
                if j >= 2:
                    pe.wait_ge(hid_ready, ready(j - 2))
                for get, b in slots:
                    w = get()
                    for i in range(2):
                        for k in range(KT):
                            last = pe.matmul(ps[:, b, i * S:(i + 1) * S], w[:, k, i * P:(i + 1) * P],
                                             xT[:, k, :], start=k == 0, stop=k == KT - 1)
                    last.then_inc(slot_done, 1)

            def down(get, j, ready, first, final):
                pe.wait_ge(hid_ready, ready(j))
                w = get()
                for kk in range(2):
                    for t in range(QB):
                        for half in range(2):
                            last = pe.matmul(ps[:, 4 + 2 * t + half, :],
                                             hidT[:, j % 2, kk * S + t * P:kk * S + (t + 1) * P],
                                             w[:, kk, half * BANK:(half + 1) * BANK],
                                             start=first and kk == 0, stop=final and kk == 1,
                                             skip_group_check=not first and not final and open_group[0])
                last.then_inc(slot_done, 1)

            open_group = [False]

            def wslot(r, gen, k):
                def get():
                    pe.wait_ge(landed[r], gen)
                    return ring[:, r, :].rearrange("p (k n) -> p k n", k=k)
                return get

            def swiglu(n0, turn, step0, first, final):
                def at(n, k):
                    return wslot(n % RING, (turn * (3 * J1 // RING) + (n // RING + 1)) * 16, k)

                def ready(j):
                    return turn * J1 + (step0 + j + 1)

                n = n0
                for j in range(J1 + 1):
                    if j < J1:
                        up([(at(n, KT), 2 * (j % 2)), (at(n + 1, KT), 2 * (j % 2) + 1)], j, ready)
                        n += 2
                    if j >= 1:
                        down(at(n, 2), j - 1, ready, first and j == 1, final and j == J1)
                        n += 1

            pe.wait_ge(consts_in, 16 * 6)
            pe.wait_ge(consts_made, 1)
            rowsT(0)
            tiles(W_QK, 4, 0, True)
            tiles(W_BCH, 6, 4, False)
            value_rows(W_V)
            pe.wait_ge(projT_kept, 10)
            for t in range(8):
                last = pe.matmul(ps[:, t // 2, (t % 2) * S:(t % 2 + 1) * S], col("rot0"), zqk[:, t, :],
                                 start=True, stop=True)
            last.then_inc(rot_ready, 1)
            pe.wait_ge(roped, 1)
            pe.wait_ge(vrows_kept, 1)
            attention(None)
            pe.wait_ge(heads_ready, 1)
            cat_transpose(4)
            pe.wait_ge(catT_kept, 2)
            pe.wait_ge(conv_ready, 1)
            row_product(W_OUT0, catT, 4)
            rowsT(1)
            swiglu(W_FFN0, 0, 0, True, True)

            def ple(layer, n0):
                row_product(n0, xT, 4)
                w = slot(n0 + 4).rearrange("p (k n) -> p k n", k=2)
                for k in range(2):
                    for t in range(QB):
                        for half in range(2):
                            a = (2 * layer + k) * S + t * P
                            last = pe.matmul(ps[:, 2 * t + half, :], col("ple", a, P),
                                             w[:, k, half * BANK:(half + 1) * BANK], start=k == 0, stop=k == 1)
                last.then_inc(slot_done, 1)

            rowsT(2)
            ple(0, W_PLE0)
            rowsT(3)
            row_product(W_CIN, xT, 0)
            row_product(W_CIN + 4, xT, 4)
            pe.wait_ge(ws_masked, 1)
            for t in range(QB):
                pe.wait_ge(vn_ready, t + 1)
                for half in range(2):
                    for i in range(4):
                        g = 4 * half + i
                        last = pe.matmul(ps[:, 2 * t + half, i * P:(i + 1) * P], ws[:, g, :],
                                         v_rows[:, t, g * P:(g + 1) * P], start=True, stop=True)
                    last.then_inc(spatial_ready, 1)
            pe.wait_ge(heads_ready, 2)
            cat_transpose(8)
            pe.wait_ge(catT_kept, 6)
            row_product(W_COUT, catT, 4)
            rowsT(4)
            for t in range(QB):
                for k in range(KT):
                    last = pe.matmul(ps[:, 0, t * 8:(t + 1) * 8], xT[:, k, t * P:(t + 1) * P],
                                     col("router", k * 8, 8), start=k == 0, stop=k == KT - 1)
            last.then_inc(logits_ready, 1)
            pe.wait_ge(ediag_ready, 1)
            for t in range(QB):
                for half in range(2):
                    last = pe.matmul(ps[:, 2 * t + half, :], ones[:, :],
                                     ediag[:, t, 4 * half:4 * half + 4, :].rearrange("p e s -> p (e s)"),
                                     start=True, stop=True)
            last.then_inc(egate_ready, 1)
            pe.wait_ge(egate_kept, 4)
            for b in range(4, 8):
                pe.matmul(ps[:, b, :], zeros[:, :], xT[:, 0:2, :].rearrange("p a b -> p (a b)"),
                          start=True, stop=False, skip_group_check=True)
            open_group[0] = True
            with pe.Fori(0, NE) as e:
                swiglu(W_MOE, e, J1, False, False)
            for b in range(4, 8):
                last = pe.matmul(ps[:, b, :], zeros[:, :], xT[:, 0:2, :].rearrange("p a b -> p (a b)"),
                                 start=False, stop=True, skip_group_check=True)
            last.then_inc(moe_ready, 1)
            rowsT(5)
            ple(1, W_PLE1)
            for l in range(2):
                n0 = W_BLK + l * B_ALL
                pe.wait_ge(csilu_ready, 2)
                pe.wait_ge(resid_ready, 7 + 2 * l)
                for s in range(16):
                    w = slot(n0 + B_ADAC + s).rearrange("p (k n) -> p k n", k=KT)
                    for i in range(2):
                        for k in range(KT):
                            last = pe.matmul(ps[:, 0, 2 * s + i:2 * s + i + 1], w[:, k, i * P:(i + 1) * P],
                                             csilu[:, k:k + 1], start=k == 0, stop=k == KT - 1)
                    last.then_inc(slot_done, 1)
                for s in range(8):
                    w = slot(n0 + B_ADAR + s).rearrange("p (k n) -> p k n", k=2)
                    for kk in range(2):
                        for half in range(2):
                            k = 2 * (s % 4) + kk
                            last = pe.matmul(ps[:, 4 + 2 * (s // 4) + half, :], c_all[:, k, :],
                                             w[:, kk, half * BANK:(half + 1) * BANK],
                                             start=k == 0, stop=k == KT - 1)
                    last.then_inc(slot_done, 1)
                pe.wait_ge(grow_ready, l + 1)
                rowsT(6 + 2 * l)
                job0 = 10 + 9 * l
                tiles(n0 + B_IN, 9, job0, True)
                value_rows(n0 + B_V)
                pe.wait_ge(projT_kept, job0 + 9)
                pe.wait_ge(squares_ready, l + 1)
                sq = flat0
                pe.matmul(ps[:, 0, 0:S], ones[:, :], sq[:, 0:S], start=True, stop=True)
                for k in range(2):
                    last = pe.matmul(ps[:, 0, S:2 * S], ones[:, :], sq[:, (k + 1) * S:(k + 2) * S],
                                     start=k == 0, stop=k == 1)
                last.then_inc(latsum_ready, 1)
                for t in range(QB):
                    last = pe.transpose(ps[:, 1, t * P:(t + 1) * P], zT[:, T_GATE, t * P:(t + 1) * P], ident)
                last.then_inc(gateT_ready, 1)
                pe.wait_ge(cmpblk_ready, l + 1)
                for which in range(2):
                    w = slot(n0 + B_CMP + which).rearrange("p (l n) -> p l n", l=16)
                    for j in range(16):
                        last = pe.matmul(ps[:, 7, which * 16:which * 16 + NCMP], w[:, j, :], blk[:, which, j, :],
                                         start=j == 0, stop=j == 15)
                    last.then_inc(slot_done, 1)
                w = slot(n0 + B_SMALL)
                uq = w[:, 0:1024].rearrange("p (k n) -> p k n", k=2)
                ukk, ukv, ck2, cv2 = w[:, 1024:1280], w[:, 1280:1536], w[:, 1536:1664], w[:, 1664:1728]
                pe.wait_ge(vrows_kept, 2 + l)
                pe.wait_ge(latent_ready, l + 1)
                for h in range(4):
                    for k in range(2):
                        pe.matmul(ps[:, 2 + h // 2, (h % 2) * S:(h % 2 + 1) * S], uq[:, k, h * P:(h + 1) * P],
                                  zT[:, T_CQ + k, :], start=k == 0, stop=k == 1)
                for h in range(4):
                    pe.matmul(ps[0:64, 4 + h // 2, (h % 2) * S:(h % 2 + 1) * S], ukk[:, h * 64:(h + 1) * 64],
                              zT[:, T_CKV, :], start=True, stop=True)
                for t in range(QB):
                    last = pe.matmul(ps[:, 6, t * S:(t + 1) * S], zT[:, T_CKV, t * P:(t + 1) * P], ukv,
                                     start=True, stop=True)
                last.then_inc(mlaheads_ready, 1)
                pe.wait_ge(cmpact_ready, l + 1)
                pe.matmul(ps[:, 7, 32:32 + NCMP], ck2, hidc[:, 0, 0:NCMP], start=True, stop=True)
                pe.matmul(ps[0:NCMP, 7, 64:128], hidc[:, 1, 0:NCMP], cv2, start=True, stop=True)\
                    .then_inc(slot_done, 1)
                pe.wait_ge(mlaheads_kept, l + 1)
                pe.wait_ge(gates_ready, l + 1)
                for h in range(4):
                    pe.matmul(ps[:, 2 + h // 2, (h % 2) * S:(h % 2 + 1) * S], col("rotm"), qm[:, h, :],
                              start=True, stop=True)
                last = pe.matmul(ps[:, 1, 0:S], col("rotm"), zT[:, T_KPE, :], start=True, stop=True)
                last.then_inc(mlarot_ready, 1)
                pe.wait_ge(mla_ready, l + 1)
                pe.wait_ge(cmp_kept, l + 1)
                attention(l)
                pe.wait_ge(mixed_kept, GROUP_BASE[1 + l] + 12)
                cat_transpose(8)
                pe.wait_ge(catT_kept, 10 + 4 * l)
                row_product(n0 + B_OUT, catT, 4)
                rowsT(7 + 2 * l)
                step0 = J1 + NE * J1 + l * J2

                def ready(j):
                    return step0 + j + 1

                open_group[0] = False
                n = n0 + B_MLP
                for j in range(J2 + 1):
                    if j < J2:
                        up([(wslot(n % RING, 16 * (n // RING + 1), KT), j % 2)], j, ready)
                        n += 1
                    if j >= 1:
                        down(wslot(n % RING, 16 * (n // RING + 1), 2), j - 1, ready, j == 1, j == J2)
                        n += 1

        @block.vector
        def _(dve):
            steps = [0]

            def link(ins):
                steps[0] += 1
                ins.then_inc(dve_step, 1)
                dve.wait_ge(dve_step, steps[0])

            roots = [0]

            def root(src, n, scale, eps):
                dve.tensor_scalar(stat[:, 0:n], src, scale, eps, ALU.mult, ALU.add).then_inc(root_asked, 1)
                roots[0] += 1
                dve.wait_ge(root_ready, roots[0])

            def norm_rows():
                for t in range(QB):
                    link(dve.tensor_tensor_reduce(out=rows[:, t, :], in0=resid[:, t, :], in1=resid[:, t, :],
                                                  scale=1.0, scalar=0.0, op0=ALU.mult, op1=ALU.add,
                                                  accum_out=stat[:, 8 + t:9 + t]))
                root(stat[:, 8:10], 2, 1.0 / D, RMS_EPS)
                for t in range(QB):
                    dve.tensor_scalar(rows[:, t, :], resid[:, t, :], stat[:, t:t + 1], None, ALU.mult)\
                        .then_inc(rows_scaled, 1)

            def norm(k, gain, shift=None):
                norm_rows()
                for t in range(QB):
                    for half in range(2):
                        b = 2 * t + half
                        dve.wait_ge(rowsT_ready, 4 * k + b + 1)
                        src = ps[:, 4 + b, :].rearrange("p (f s) -> p f s", f=4)
                        dst = xT[:, 4 * half:4 * half + 4, t * P:(t + 1) * P]
                        ins = dve.tensor_tensor(dst, src, bc(gain[:, 4 * half:4 * half + 4], P), ALU.mult)
                        if shift is not None:
                            link(ins)
                            ins = dve.tensor_tensor(dst, dst, bc(shift[:, 4 * half:4 * half + 4], P), ALU.add)
                        ins.then_inc(normed, 1)

            def gain(k):
                return col("gain", 8 * k, 8)

            def add_branch(gate=None):
                for t in range(QB):
                    for half in range(2):
                        c = slice(half * BANK, (half + 1) * BANK)
                        src = ps[:, 4 + 2 * t + half, :]
                        if gate is not None:
                            link(dve.tensor_tensor(rows[:, t, c], src, gate[:, c], ALU.mult))
                            src = rows[:, t, c]
                        ins = dve.tensor_tensor(resid[:, t, c], resid[:, t, c], src, ALU.add)
                        if (t, half) == (1, 1):
                            ins.then_inc(resid_ready, 1)
                        else:
                            link(ins)

            def attention(layer):
                groups = attention_groups(layer)
                base = GROUP_BASE[0 if layer is None else layer + 1]

                def soften(i):
                    kind, qb, hg = groups[i]
                    g = base + i
                    kw = NCMP if kind == "nsac" else P * (qb + 1)
                    src = bank(2 * (g % 2), 2).rearrange("p (u k) -> p u k", u=4)[:, :, 0:kw]
                    sc = score[:, g % 2, :, 0:kw]
                    m = soft[:, g % 2, 0, :]
                    dve.wait_ge(scores_ready, g + 1)
                    if i >= 2:
                        dve.wait_ge(probT_ready, g - 1)
                    if kind in ("diff", "mla"):
                        link(dve.tensor_tensor(sc, src, rep(col("causal", qb * S, kw), 4), ALU.add))
                    else:
                        table = {"swa": col("window", qb * S, kw), "nsac": col("nsac", qb * NCMP, NCMP)}
                        first = {"swa": 0, "moba": 2}.get(kind, 1)
                        for u in range(4):
                            ins = dve.scalar_tensor_tensor(
                                out=sc[:, u, :], in0=table.get(kind, col("alibi", qb * S, kw)),
                                scalar=SLOPES[first + 3 * head_of(kind, u)] * 8.0, in1=src[:, u, :], op0=ALU.mult, op1=ALU.add)
                        link(ins)
                    if kind == "swa":
                        sc = score[:, g % 2, :, 0:kw + 1]
                        link(dve.tensor_scalar(sc[:, :, kw:kw + 1].rearrange("p u o -> p (u o)"), sink[:, layer, :],
                                               8.0, None, ALU.mult))
                    link(dve.tensor_reduce(m, sc, AX.X, ALU.max))
                    if kind == "nsac":
                        link(dve.tensor_scalar(m, m, GUARD, None, ALU.max))
                    dve.tensor_tensor(sc, sc, bc(m, sc.shape[2]), ALU.subtract).then_inc(shifted, 1)

                def finish(i):
                    kind, qb, hg = groups[i]
                    g = base + i
                    kw = NCMP if kind == "nsac" else P * (qb + 1) + (kind == "swa")
                    den, rden, coef = (soft[:, g % 2, n, :] for n in (1, 2, 3))
                    dve.wait_ge(exp_ready, g + 1)
                    to = den.rearrange("p (i r) -> p r i", i=2) if head_of(kind, 1) == 2 else \
                        den.rearrange("p (r i) -> p r i", r=2)
                    link(dve.tensor_reduce(to, score[:, g % 2, :, 0:kw].rearrange("p (r i) k -> p r i k", r=2),
                                           AX.X, ALU.add))
                    link(dve.tensor_scalar(den, den, TINY, None, ALU.max))
                    link(dve.reciprocal(rden, den))
                    w = P if kind == "diff" else 64
                    src = ps[:, 6 + g % 2, 0:4 * w].rearrange("p (u n) -> p u n", u=4)
                    if kind == "diff":
                        link(dve.tensor_tensor(coef, rden, lam[:, 4:8], ALU.mult))
                        dve.wait_ge(mixed_ready, g + 1)
                        tmp = xT[:, 0:2, :].rearrange("p a (b n) -> p (a b) n", b=2)
                        link_kept(dve.tensor_tensor(tmp, src, bc(coef, P), ALU.mult), g)
                        link(dve.tensor_tensor(rows[:, qb, hg * S:(hg + 1) * S], xT[:, 0, :], xT[:, 1, :], ALU.add))
                        return
                    m0 = {"swa": 0, "mla": 256, "moba": 768}.get(kind, 512)
                    dst = rows[:, qb, m0:m0 + 256].rearrange("p (u n) -> p u n", u=4)
                    if kind.startswith("nsa"):
                        b = "csw".index(kind[3])
                        if (kind, qb) == ("nsac", 0):
                            dve.wait_ge(gates_ready, layer + 1)
                        link(dve.tensor_tensor(coef, rden, gates[:, qb, 4 * b:4 * b + 4], ALU.mult))
                        dve.wait_ge(mixed_ready, g + 1)
                        if kind == "nsac":
                            link_kept(dve.tensor_tensor(dst, src, bc(coef, 64), ALU.mult), g)
                        else:
                            tmp = catT[:, 0, :].rearrange("p (u n) -> p u n", u=4)
                            link_kept(dve.tensor_tensor(tmp, src, bc(coef, 64), ALU.mult), g)
                            link(dve.tensor_tensor(dst, dst, tmp, ALU.add))
                    else:
                        dve.wait_ge(mixed_ready, g + 1)
                        link_kept(dve.tensor_tensor(dst, src, bc(rden, 64), ALU.mult), g)

                soften(0)
                for i in range(len(groups)):
                    if i + 1 < len(groups):
                        soften(i + 1)
                    finish(i)

            def link_kept(ins, g):
                ins.then_inc(mixed_kept, 1)
                dve.wait_ge(mixed_kept, g + 1)

            def hidden(j, ready, paired, gate=None):
                dve.wait_ge(act_ready, ready(j))
                p = j % 2
                other = ps[:, 2 * p + 1, :] if paired else acth[:, p, :]
                if gate is None:
                    dve.tensor_tensor(hidT[:, p, :], acth[:, p, :], other, ALU.mult).then_inc(hid_ready, 1)
                else:
                    dve.tensor_tensor(acth[:, p, :], acth[:, p, :], other, ALU.mult).then_inc(egated, 1)
                    dve.wait_ge(egated, gate[1](j))
                    dve.tensor_tensor(hidT[:, p, :].rearrange("p (a s) -> p a s", a=2),
                                      acth[:, p, :].rearrange("p (a s) -> p a s", a=2),
                                      rep(gate[0], 2), ALU.mult).then_inc(hid_ready, 1)

            dve.memset(ones[:, :], 1.0)
            dve.memset(zeros[:, :], 0.0).then_inc(consts_made, 1)
            dve.wait_ge(consts_in, 16 * 6)
            link(dve.tensor_copy(ang, posi[:, :]))
            link(dve.tensor_scalar(ang, ang, col("invf"), None, ALU.mult))
            magic = 1.5 * 2.0 ** 23
            link(dve.tensor_scalar(turns, ang, 1.0 / (2 * math.pi), magic, ALU.mult, ALU.add))
            link(dve.tensor_scalar(turns, turns, -magic, None, ALU.add))
            c1 = 6.28125
            c2 = math.floor((2 * math.pi - c1) * 2 ** 21) / 2 ** 21
            c3 = 2 * math.pi - c1 - c2
            for c in (c1, c2, c3):
                link(dve.scalar_tensor_tensor(out=ang, in0=turns, scalar=-c, in1=ang, op0=ALU.mult, op1=ALU.add))
            lim = float(np.nextafter(np.float32(math.pi), np.float32(0)))
            link(dve.tensor_scalar(ang, ang, -lim, lim, ALU.max, ALU.min))
            link(dve.tensor_scalar(turns, ang, -1.0, None, ALU.mult))
            link(dve.tensor_tensor(turns, turns, ang, ALU.max))
            dve.tensor_scalar(turns, turns, -1.0, math.pi / 2, ALU.mult, ALU.add).then_inc(angles_ready, 1)
            for i in range(2):
                link(dve.tensor_tensor_reduce(out=rows[:, 0, 0:64], in0=lamv[:, 128 * i:128 * i + 64],
                                              in1=lamv[:, 128 * i + 64:128 * i + 128], scale=1.0, scalar=0.0,
                                              op0=ALU.mult, op1=ALU.add, accum_out=lam[:, i:i + 1]))
            dve.memset(lam[:, 4:8], 1.0).then_inc(lam_asked, 1)
            dve.wait_ge(lam_exp, 1)
            link(dve.tensor_tensor(lam[:, 0:1], lam[:, 3:4], lam[:, 2:3], ALU.subtract))
            link(dve.tensor_scalar(lam[:, 0:1], lam[:, 0:1], -LAMBDA_INIT, None, ALU.add))
            for i in (6, 7):
                dve.tensor_copy(lam[:, i:i + 1], lam[:, 0:1])
            link(dve.tensor_scalar(sub8[:, :], col("subln"), 1.0 - LAMBDA_INIT, None, ALU.mult))
            dve.wait_ge(csilu_ready, 1)
            dve.tensor_copy(c_all[:, :, :], bc(csilu[:, :], P)).then_inc(csilu_ready, 1)

            norm(0, gain(0))
            dve.wait_ge(rot_ready, 1)
            dve.wait_ge(sines_ready, 2)
            rot = bank(0, 4).rearrange("p (t s) -> p t s", s=S)
            rtmp = rows[:, :, :].rearrange("p b (t s) -> p (b t) s", s=S)
            link(dve.tensor_tensor(rtmp, rot, rep(sin0, 8), ALU.mult))
            link(dve.tensor_tensor(zqk, zqk, rep(cos0, 8), ALU.mult))
            dve.tensor_tensor(zqk, zqk, rtmp, ALU.add).then_inc(roped, 1)
            zb, zc, zh = zbch[:, 0:4, :], zbch[:, 4:8, :], zbch[:, 8:12, :]
            link(dve.tensor_tensor(zc, zc, zh, ALU.mult))
            for i in range(4):
                ins = dve.tensor_scalar(zh[:, i, :], zc[:, i, :], col("conv", 3 * i + 2, 1), None, ALU.mult)
            link(ins)
            for tap in (1, 0):
                lag = 2 - tap
                for i in range(4):
                    ins = dve.scalar_tensor_tensor(out=zh[:, i, lag:S], in0=zc[:, i, 0:S - lag],
                                                   scalar=col("conv", 3 * i + tap, 1), in1=zh[:, i, lag:S],
                                                   op0=ALU.mult, op1=ALU.add)
                link(ins)
            dve.tensor_tensor(catT[:, 4:8, :], zh, zb, ALU.mult).then_inc(conv_ready, 1)
            attention(None)
            heads = rows[:, :, 0:512].rearrange("p b (h n) -> p b h n", h=4)
            sq = xT[:, 0:4, :].rearrange("p (b a) (h n) -> p b (a h) n", b=2, h=2)
            for t in range(QB):
                link(dve.tensor_tensor(sq[:, t], heads[:, t], heads[:, t], ALU.mult))
            link(dve.tensor_reduce(stat[:, 8:16], sq.rearrange("p b h n -> p (b h) n"), AX.X, ALU.add))
            root(stat[:, 8:16], 8, 1.0 / P, RMS_EPS)
            for t in range(QB):
                ins = dve.tensor_tensor(heads[:, t], heads[:, t], bc(stat[:, 4 * t:4 * t + 4], P), ALU.mult)
                if t == 0:
                    link(ins)
            ins.then_inc(heads_ready, 1)
            dve.wait_ge(slot_done, W_OUT0 + 4)
            add_branch()
            dve.wait_ge(resid_ready, 1)
            norm(1, gain(1))
            for j in range(J1):
                hidden(j, lambda j: j + 1, True)
            dve.wait_ge(slot_done, W_FFN0 + 3 * J1)
            add_branch()
            dve.wait_ge(resid_ready, 2)

            def ple(layer, n):
                for t in range(QB):
                    for half in range(2):
                        c = slice(half * BANK, (half + 1) * BANK)
                        dve.wait_ge(ple_gated, 4 * layer + 2 * t + half + 1)
                        link(dve.tensor_tensor(rows[:, t, c], rows[:, t, c], ps[:, 2 * t + half, :], ALU.mult))
                        ins = dve.tensor_tensor(resid[:, t, c], resid[:, t, c], rows[:, t, c], ALU.add)
                        if (t, half) == (1, 1):
                            ins.then_inc(resid_ready, 1)
                            dve.wait_ge(resid_ready, n)
                        else:
                            link(ins)

            norm(2, gain(2))
            ple(0, 3)
            norm(3, gain(3))
            for t in range(QB):
                dve.wait_ge(gelu_done, 4 + 2 * t + 2)
                for half in range(2):
                    ins = dve.bn_stats(bn[:, t, half, :], v_rows[:, t, half * BANK:(half + 1) * BANK])
                link(ins)
                link(dve.bn_aggr(mv[:, t, :], bn[:, t].rearrange("p a b -> p (a b)")))
                link(dve.tensor_copy(stat[:, 8 + t:9 + t], mv[:, t, 1:2]))
            root(stat[:, 8:10], 2, 1.0, LN_EPS)
            dve.wait_ge(ln_in, 16 * 3)
            for t in range(QB):
                link(dve.tensor_scalar(v_rows[:, t, :], v_rows[:, t, :], mv[:, t, 0:1], stat[:, t:t + 1],
                                       ALU.subtract, ALU.mult))
                link(dve.tensor_tensor(v_rows[:, t, :], v_rows[:, t, :], ln_g, ALU.mult))
                dve.tensor_tensor(v_rows[:, t, :], v_rows[:, t, :], ln_b, ALU.add).then_inc(vn_ready, 1)
            for t in range(QB):
                for half in range(2):
                    dve.wait_ge(spatial_ready, 2 * t + half + 1)
                    for i in range(4):
                        g = 4 * half + i
                        ins = dve.scalar_tensor_tensor(out=rows[:, t, g * P:(g + 1) * P],
                                                       in0=ps[:, 2 * t + half, i * P:(i + 1) * P],
                                                       scalar=col("bs", g, 1), in1=u_rows[:, t, g * P:(g + 1) * P],
                                                       op0=ALU.add, op1=ALU.mult)
            ins.then_inc(heads_ready, 1)
            dve.wait_ge(slot_done, W_COUT + 4)
            add_branch()
            dve.wait_ge(resid_ready, 4)
            norm(4, gain(4))
            dve.wait_ge(logits_ready, 1)
            link(dve.tensor_copy(logit[:, :, :].rearrange("p b e -> p (b e)"), ps[:, 0, 0:16]))
            for t in range(QB):
                link(dve.max(top[:, t, :], logit[:, t, :]))
                link(dve.max_index(topi[:, t, :], top[:, t, :], logit[:, t, :]))
                link(dve.tensor_copy(route[:, t, 0, :], topi[:, t, :]))
                ins = dve.tensor_tensor(route[:, t, 1, 0:1], top[:, t, 1:2], top[:, t, 0:1], ALU.subtract)
                if t == 0:
                    link(ins)
            ins.then_inc(route_asked, 1)
            dve.wait_ge(route_exp, 2)
            for t in range(QB):
                e = route[:, t, 1, 1:2]
                link(dve.tensor_scalar(route[:, t, 1, 2:3], e, 1.0, None, ALU.add))
                link(dve.reciprocal(route[:, t, 1, 3:4], route[:, t, 1, 2:3]))
                link(dve.tensor_tensor(route[:, t, 1, 4:5], e, route[:, t, 1, 3:4], ALU.mult))
                for n in range(2):
                    link(dve.tensor_scalar(route[:, t, 2 + n, :], col("iota"), route[:, t, 0, n:n + 1],
                                           route[:, t, 1, 3 + n:4 + n], ALU.is_equal, ALU.mult))
                link(dve.tensor_tensor(route[:, t, 2, :], route[:, t, 2, :], route[:, t, 3, :], ALU.add))
                ins = dve.tensor_tensor(ediag[:, t], rep(ident, NE), bc(route[:, t, 2, :], P), ALU.mult)
            ins.then_inc(ediag_ready, 1)
            dve.wait_ge(egate_ready, 1)
            for t in range(QB):
                for half in range(2):
                    dve.tensor_copy(egate[:, 4 * half:4 * half + 4, t * P:(t + 1) * P],
                                    ps[:, 2 * t + half, :].rearrange("p (e s) -> p e s", e=4)).then_inc(egate_kept, 1)
            dve.wait_ge(egate_kept, 4)
            with dve.Fori(0, NE) as e:
                for j in range(J1):
                    hidden(j, lambda j: e * J1 + (J1 + j + 1), True,
                           (arena[:, bass.ds(e * S, S)], lambda j: e * J1 + (j + 1)))
            dve.wait_ge(moe_ready, 1)
            add_branch()
            dve.wait_ge(resid_ready, 5)
            norm(5, gain(5))
            ple(1, 6)
            norm_rows()
            dve.wait_ge(rows_scaled, 14)
            dve.wait_ge(fin_in, 16)
            for t in range(QB):
                ins = dve.tensor_tensor(resid[:, t, :], rows[:, t, :], ln_g, ALU.mult)
                if t == 0:
                    link(ins)
            ins.then_inc(resid_ready, 1)
            dve.wait_ge(resid_ready, 7)
            for l in range(2):
                n0 = W_BLK + l * B_ALL
                dve.wait_ge(slot_done, n0 + B_ADAR)
                link(dve.tensor_tensor(ada[:, :], ps[:, 0, 0:32], col("bada", 32 * l, 32), ALU.add))
                for i in range(2):
                    ins = dve.scalar_tensor_tensor(out=modg[:, i, :], in0=ada[:, 16 * i + 8:16 * i + 16], scalar=1.0,
                                                   in1=gain(6 + 2 * l + i), op0=ALU.add, op1=ALU.mult)
                link(ins)
                dve.wait_ge(slot_done, n0 + B_IN)
                dve.wait_ge(bada_in, 16 * (l + 1))
                ins = dve.tensor_tensor(grow[:, :, :].rearrange("p a n -> p (a n)"),
                                        grow[:, :, :].rearrange("p a n -> p (a n)"), bank(4, 4), ALU.add)
                ins.then_inc(grow_ready, 1)
                norm(6 + 2 * l, modg[:, 0, :], ada[:, 0:8])
                dve.wait_ge(projT_kept, 10 + 9 * l + 9)
                dve.tensor_tensor(flat0[:, 0:3 * S], arena[:, T_CKV * S:(T_CKV + 3) * S],
                                  arena[:, T_CKV * S:(T_CKV + 3) * S], ALU.mult).then_inc(squares_ready, 1)
                for which in range(2):
                    for par in range(2):
                        z = zT[64 * par:64 * par + 64, T_KC + which, :].rearrange("p (n l) -> p l n", l=16)
                        for hi in range(2):
                            ins = dve.tensor_tensor(
                                blk[64 * par:64 * par + 64, which, 8 * hi:8 * hi + 8, :],
                                z[:, par:16:2, hi:hi + NCMP],
                                bc(col("pos", 32 * l + 16 * which + 8 * hi, 8)[64 * par:64 * par + 64], NCMP), ALU.add)
                ins.then_inc(cmpblk_ready, 1)
                dve.wait_ge(latsum_ready, l + 1)
                lat = flat0[:, 0:2 * S]
                dve.wait_ge(cmpblk_ready, l + 1)
                link(dve.tensor_scalar(lat[:, 0:S], ps[:, 0, 0:S], 1.0 / 128, RMS_EPS, ALU.mult, ALU.add))
                dve.tensor_scalar(lat[:, S:2 * S], ps[:, 0, S:2 * S], 1.0 / 192, RMS_EPS, ALU.mult, ALU.add)\
                    .then_inc(latms_ready, 1)
                dve.wait_ge(latroot_ready, l + 1)
                link(dve.reciprocal(flat0[:, 2 * S:4 * S], lat))
                for t, r, g in ((T_CKV, 2, 0), (T_CQ, 3, 1), (T_CQ + 1, 3, 2)):
                    ins = dve.scalar_tensor_tensor(out=zT[:, t, :], in0=zT[:, t, :], scalar=col("mlag", 3 * l + g, 1),
                                                   in1=flat0[:, r * S:(r + 1) * S], op0=ALU.mult, op1=ALU.mult)
                ins.then_inc(latent_ready, 1)
                dve.wait_ge(mlarot_ready, l + 1)
                cm, sm = col("cosm"), col("sinm")
                tmp = flat0[:, 0:4 * S].rearrange("p (h s) -> p h s", h=4)
                link(dve.tensor_tensor(tmp, bank(2, 2).rearrange("p (h s) -> p h s", h=4), rep(sm, 4), ALU.mult))
                link(dve.tensor_tensor(qm, qm, rep(cm, 4), ALU.mult))
                link(dve.tensor_tensor(qm, qm, tmp, ALU.add))
                kpe = zT[:, T_KPE, :]
                link(dve.tensor_tensor(flat0[:, 0:S], ps[:, 1, 0:S], sm, ALU.mult))
                link(dve.tensor_tensor(kpe, kpe, cm, ALU.mult))
                link(dve.tensor_tensor(kpe, kpe, flat0[:, 0:S], ALU.add))
                dve.tensor_copy(km[64:128, :, :], rep(kpe[64:128], 4)).then_inc(mla_ready, 1)
                attention(l)
                dve.wait_ge(slot_done, n0 + B_OUT + 4)
                add_branch(grow[:, 0, :])
                dve.wait_ge(resid_ready, 8 + 2 * l)
                norm(7 + 2 * l, modg[:, 1, :], ada[:, 16:24])
                base = J1 + NE * J1 + l * J2
                for j in range(J2):
                    hidden(j, lambda j: base + j + 1, False)
                dve.wait_ge(slot_done, n0 + B_ALL)
                add_branch(grow[:, 1, :])
                dve.wait_ge(resid_ready, 9 + 2 * l)
            norm_rows()
            dve.wait_ge(rows_scaled, 24)
            dve.wait_ge(fin_in, 32)
            fin = catT[:, 0:4, :].rearrange("p a s -> p (a s)")
            for t in range(QB):
                ins = dve.tensor_tensor(rows[:, t, :], rows[:, t, :], fin, ALU.mult)
                if t == 0:
                    link(ins)
            ins.then_inc(resid_ready, 1)

        @block.scalar
        def _(act):
            steps = [0]

            def link(ins):
                steps[0] += 1
                ins.then_inc(act_step, 1)
                act.wait_ge(act_step, steps[0])

            act.dma_start(con[:, :], consts).then_inc(consts_in, 16)
            act.dma_start(resid[:, :, :], x_in.rearrange("(b p) n -> p b n", p=P)).then_inc(consts_in, 16)
            act.dma_start(posi[:, :], pos.partition_broadcast(P)).then_inc(consts_in, 16)
            act.dma_start(lamv[:, :], lam_in.partition_broadcast(P)).then_inc(consts_in, 16)
            for l in range(2):
                act.dma_start(sink[:, l, :], sinks[l].partition_broadcast(P)).then_inc(consts_in, 16)
            act.dma_start(grow[:, :, :].rearrange("p a n -> p (a n)"), bada_rows[0].partition_broadcast(P))\
                .then_inc(bada_in, 16)
            act.wait_ge(consts_in, 16 * 6)
            act.activation(csilu[:, :], col("c"), ACT.Silu).then_inc(csilu_ready, 1)
            act.wait_ge(angles_ready, 1)
            act.activation(sin0, ang, ACT.Sin).then_inc(sines_ready, 1)
            act.activation(cos0, turns, ACT.Sin).then_inc(sines_ready, 1)
            act.wait_ge(lam_asked, 1)
            act.activation(lam[:, 2:4], lam[:, 0:2], ACT.Exp).then_inc(lam_exp, 1)

            def keep_tiles(dst, count, n0):
                for s in range(count):
                    act.wait_ge(slot_done, n0 + s + 1)
                    act.activation(dst[:, 2 * s:2 * s + 2, :].rearrange("p a s -> p (a s)"),
                                   ps[:, s % 4, :], ACT.Copy).then_inc(projT_kept, 1)

            def attention(layer):
                groups = attention_groups(layer)
                base = GROUP_BASE[0 if layer is None else layer + 1]

                def exps(i):
                    kind, qb, hg = groups[i]
                    g = base + i
                    kw = NCMP if kind == "nsac" else P * (qb + 1) + (kind == "swa")
                    sc = score[:, g % 2, :, 0:kw]
                    act.wait_ge(shifted, g + 1)
                    act.activation(sc, sc, ACT.Exp, scale=96.0 ** -0.5 if kind == "mla" else 0.125)\
                        .then_inc(exp_ready, 1)

                def keep(i):
                    kind, qb, hg = groups[i]
                    g = base + i
                    nkb = 1 if kind == "nsac" else qb + 1
                    kp = NCMP if kind == "nsac" else P
                    act.wait_ge(probT_ready, g + 1)
                    if i >= 2:
                        act.wait_ge(mixed_ready, g - 1)
                    act.activation(probT[0:kp, g % 2, 0:4 * nkb, :].rearrange("p a b -> p (a b)"),
                                   bank(4, 2)[0:kp, 0:4 * nkb * P], ACT.Copy).then_inc(probT_kept, 1)

                exps(0)
                for i in range(len(groups)):
                    keep(i)
                    if i + 1 < len(groups):
                        exps(i + 1)

            def keep_cat(count, before, gain=None):
                for n in range(count):
                    act.wait_ge(catT_ready, before + n + 1)
                    t, half = (n, 0) if count == 2 else (n // 2, n % 2)
                    act.activation(catT[:, 4 * half:4 * half + 4, t * P:(t + 1) * P],
                                   ps[:, 4 + 2 * t + half, :].rearrange("p (f s) -> p f s", f=4),
                                   ACT.Copy, scale=1.0 if gain is None else gain).then_inc(catT_kept, 1)

            def activations(j, done, func, paired):
                act.wait_ge(slot_done, done)
                act.activation(acth[:, j % 2, :], ps[:, (2 if paired else 1) * (j % 2), :], func)\
                    .then_inc(act_ready, 1)

            keep_tiles(zqk, 4, W_QK)
            keep_tiles(zbch, 6, W_BCH)
            act.wait_ge(slot_done, W_V + 2)
            act.activation(v1.rearrange("p b n -> p (b n)"), bank(4, 2), ACT.Copy).then_inc(vrows_kept, 1)
            attention(None)
            keep_cat(2, 0, sub8[:, 0:1])
            for j in range(J1):
                activations(j, W_FFN0 + swiglu_up(j) + 1, ACT.Silu, True)
            act.wait_ge(slot_done, W_OUT0)
            act.dma_start(ln_g, ln_rows[0].partition_broadcast(P)).then_inc(ln_in, 16)
            act.dma_start(ln_b, ln_rows[1].partition_broadcast(P)).then_inc(ln_in, 16)
            act.dma_start(ws, w_s).then_inc(ln_in, 16)

            def ple(layer):
                act.wait_ge(slot_done, (W_PLE0, W_PLE1)[layer] + 5)
                for b in range(4):
                    act.activation(rows[:, b // 2, (b % 2) * BANK:(b % 2 + 1) * BANK], ps[:, 4 + b, :], ACT.Sigmoid)\
                        .then_inc(ple_gated, 1)

            ple(0)
            for part, dst in enumerate((u_rows, v_rows)):
                act.wait_ge(slot_done, W_CIN + 4 * part + 4)
                for b in range(4):
                    act.activation(dst[:, b // 2, (b % 2) * BANK:(b % 2 + 1) * BANK], ps[:, 4 * part + b, :], ACT.Gelu)\
                        .then_inc(gelu_done, 1)
            keep_cat(4, 2)
            act.wait_ge(route_asked, 1)
            for t in range(QB):
                act.activation(route[:, t, 1, 1:2], route[:, t, 1, 0:1], ACT.Exp).then_inc(route_exp, 1)
            with act.Fori(0, NE) as e:
                for j in range(J1):
                    activations(j, e * (3 * J1) + (W_MOE + swiglu_up(j) + 1), ACT.Silu, True)
            act.dma_start(ln_g, fin_row[0].partition_broadcast(P)).then_inc(fin_in, 16)
            ple(1)
            for l in range(2):
                if l == 1:
                    act.wait_ge(resid_ready, 9)
                    act.dma_start(grow[:, :, :].rearrange("p a n -> p (a n)"), bada_rows[1].partition_broadcast(P))\
                        .then_inc(bada_in, 16)
                n0 = W_BLK + l * B_ALL
                keep_tiles(zT, 9, n0 + B_IN)
                act.wait_ge(slot_done, n0 + B_CMP)
                act.activation(v2.rearrange("p b n -> p (b n)"), bank(4, 2), ACT.Copy).then_inc(vrows_kept, 1)
                act.wait_ge(latms_ready, l + 1)
                act.activation(flat0[:, 0:2 * S], flat0[:, 0:2 * S], ACT.Sqrt).then_inc(latroot_ready, 1)
                act.wait_ge(gateT_ready, l + 1)
                act.activation(gates[:, :, 0:12], ps[:, 1, 0:2 * P].rearrange("p (b n) -> p b n", b=2)[:, :, 0:12],
                               ACT.Sigmoid).then_inc(gates_ready, 1)
                act.wait_ge(mlaheads_ready, l + 1)
                link(act.activation(qm.rearrange("p h s -> p (h s)"), bank(2, 2), ACT.Copy))
                link(act.activation(km[0:64].rearrange("p h s -> p (h s)"), bank(4, 2)[0:64], ACT.Copy))
                act.activation(vm.rearrange("p b n -> p (b n)"), bank(6), ACT.Copy).then_inc(mlaheads_kept, 1)
                act.wait_ge(slot_done, n0 + B_SMALL)
                act.activation(hidc[:, :, 0:NCMP], ps[:, 7, 0:32].rearrange("p (v n) -> p v n", v=2)[:, :, 0:NCMP],
                               ACT.Gelu_apprx_tanh).then_inc(cmpact_ready, 1)
                act.wait_ge(slot_done, n0 + B_OUT)
                link(act.activation(kcmp[:, 0:NCMP], ps[:, 7, 32:32 + NCMP], ACT.Copy))
                act.activation(vcmp[0:NCMP, :], ps[0:NCMP, 7, 64:128], ACT.Copy).then_inc(cmp_kept, 1)
                attention(l)
                keep_cat(4, 6 + 4 * l)
                for j in range(J2):
                    activations(j, n0 + B_MLP + mlp_up(j) + 1, ACT.Relu, False)
            act.wait_ge(slot_done, SLOTS)
            act.dma_start(catT[:, 0:4, :].rearrange("p a s -> p (a s)"), fin_row[1].partition_broadcast(P))\
                .then_inc(fin_in, 16)

        @block.gpsimd
        def _(pool):
            pool.memset(neghalf[:, :], -0.5).then_inc(pool_step, 1)
            pool.wait_ge(pool_step, 1)
            widths = [2, 8] + [2] * 12
            for n, w in enumerate(widths):
                if n == 5:
                    pool.wait_ge(ln_in, 16 * 3)
                    pool.affine_select(out=ws, in_=ws, pattern=[[0, 8], [1, P]], compare_op=ALU.is_ge, fill=0.0,
                                       base=0, channel_multiplier=-1).then_inc(ws_masked, 1)
                pool.wait_ge(root_asked, n + 1)
                pool.tensor_tensor(stat[:, 0:w], stat[:, 0:w], neghalf[:, 0:w], ALU.pow).then_inc(root_ready, 1)


def row_tiles(w, k):
    n = w.shape[-1]
    return np.ascontiguousarray(w.reshape(k, P, n).transpose(1, 0, 2)).reshape(P, k * n)


def column_slots(w):
    return [row_tiles(w[:, j:j + 256], KT) for j in range(0, w.shape[1], 256)]


def row_slots(w):
    return [row_tiles(w[j:j + 256], 2) for j in range(0, w.shape[0], 256)]


def swiglu_slots(w1, w3, w2):
    a, b, c = column_slots(w1), column_slots(w3), row_slots(w2)
    out = []
    for j in range(J1 + 1):
        if j < J1:
            out += [a[j], b[j]]
        if j >= 1:
            out.append(c[j - 1])
    return out


def lay_out(i):
    f = np.float32
    slots = []
    w = np.asarray(i["a_w_in"])[0]
    slots += column_slots(w[:, 0:1024]) + column_slots(w[:, 1536:3072])
    wv = w[:, 1024:1536]
    slots += [row_tiles(wv[0:512], 4), row_tiles(wv[512:1024], 4)]
    slots += row_slots(np.asarray(i["a_w_out"])[0])
    slots += swiglu_slots(*(np.asarray(i[n])[0] for n in ("ffn_w1", "ffn_w3", "ffn_w2")))
    pg, pp = np.asarray(i["ple_gate"]), np.asarray(i["ple_proj"])
    slots += row_slots(pg[0]) + row_slots(pp[0])
    w = np.asarray(i["c_w_in"])[0]
    slots += row_slots(w[:, 0:1024]) + row_slots(w[:, 1024:2048])
    slots += row_slots(np.asarray(i["c_w_out"])[0])
    m1, m3, m2 = (np.asarray(i[n])[0] for n in ("moe_w1", "moe_w3", "moe_w2"))
    for e in range(NE):
        slots += swiglu_slots(m1[e], m3[e], m2[e])
    slots += row_slots(pg[1]) + row_slots(pp[1])
    for l in range(2):
        w = np.asarray(i["w_ada_2"])[l]
        sh1, sc1, g1, sh2, sc2, g2 = (w[:, n * D:(n + 1) * D] for n in range(6))
        for part in (sh1, sc1, sh2, sc2):
            slots += column_slots(part)
        slots += row_slots(g1) + row_slots(g2)
        w = np.asarray(i["w_in_2"])[l]
        z = {}
        at = 0
        for name, n in (("swaq", 256), ("swak", 128), ("swav", 128), ("cq", 192), ("ckv", 128), ("kpe", 32),
                        ("nsaq", 256), ("kc", 64), ("vc", 64), ("ks", 64), ("vs", 64), ("kw", 64), ("vw", 64),
                        ("gl", 12), ("mobq", 256), ("mobk", 256), ("mobv", 256)):
            z[name] = w[:, at:at + n]
            at += n

        def pad(n):
            return np.zeros((D, n), f)

        sq = z["swaq"]
        cols = [sq[:, 0:64], sq[:, 128:192], sq[:, 64:128], sq[:, 192:256], z["swak"], z["ckv"], z["cq"], pad(64),
                pad(64), z["kpe"], pad(32), z["gl"], pad(116), z["nsaq"]]
        for name in ("kc", "vc", "ks", "kw"):
            cols += [z[name], z[name]]
        cols += [z["mobq"], z["mobk"]]
        slots += column_slots(np.concatenate(cols, 1))
        wv = np.concatenate([z["swav"], z["vs"], z["vw"], z["mobv"]], 1)
        slots += [row_tiles(wv[0:512], 4), row_tiles(wv[512:1024], 4)]
        for n in ("nsa_cmp_k_w1_2", "nsa_cmp_v_w1_2"):
            slots.append(row_tiles(np.asarray(i[n])[l], 16))
        uq = np.asarray(i["mla_w_uq_2"])[l].reshape(192, 4, 96)
        uqp = np.zeros((256, 4, 128), f)
        uqp[0:192, :, 0:96] = uq
        ukv = np.asarray(i["mla_w_ukv_2"])[l].reshape(128, 4, 128)
        ck2, cv2 = np.asarray(i["nsa_cmp_k_w2_2"])[l], np.asarray(i["nsa_cmp_v_w2_2"])[l]
        small = np.zeros((P, SLOT), f)
        small[:, 0:1024] = row_tiles(uqp.reshape(256, 512), 2)
        small[:, 1024:1280] = ukv[:, :, 0:64].reshape(128, 256)
        small[:, 1280:1536] = ukv[:, :, 64:128].reshape(128, 256)
        small[:, 1536:1600] = ck2
        small[:, 1600:1664] = ck2
        small[:, 1664:1728] = cv2
        slots.append(small)
        slots += row_slots(np.asarray(i["w_out_2"])[l])
        a, b = column_slots(np.asarray(i["w_up_2"])[l]), row_slots(np.asarray(i["w_down_2"])[l])
        for j in range(J2 + 1):
            if j < J2:
                slots.append(a[j])
            if j >= 1:
                slots.append(b[j - 1])
    assert len(slots) == SLOTS, (len(slots), SLOTS)
    stream = np.stack(slots)
    del slots

    def colvec(v):
        return np.asarray(v).reshape(-1, P).T

    con = {}
    lm, lf, lp = (np.asarray(i[n]) for n in ("ln_mix", "ln_ffn", "ln_ple"))
    nm, nl = np.asarray(i["norm_mix_g_2"]), np.asarray(i["norm_mlp_g_2"])
    con["gain"] = np.concatenate([colvec(v) for v in (lm[0], lf[0], lp[0], lm[1], lf[1], lp[1], nm[0], nl[0],
                                                      nm[1], nl[1])], 1)
    con["subln"] = colvec(np.asarray(i["a_subln"])[0])
    con["conv"] = np.asarray(i["a_conv_w"])[0].reshape(4, P, 3).transpose(1, 0, 2).reshape(P, 12)
    half = 8
    inv = np.float32(500000.0) ** (-np.arange(0, 16, 2, dtype=f) / np.float32(16))
    invf = np.zeros((2, 64), f)
    invf[:, 0:half] = inv
    invf[:, half:2 * half] = inv
    con["invf"] = invf.reshape(P, 1)
    con["bs"] = np.asarray(i["c_b_s"])[0].T
    con["router"] = row_tiles(np.asarray(i["router_w"])[0], KT)
    con["iota"] = np.tile(np.arange(8, dtype=f), (P, 1))
    con["c"] = colvec(np.asarray(i["c_2"])[0])
    ba = np.asarray(i["b_ada_2"])
    con["bada"] = np.concatenate([colvec(ba[l, n * D:(n + 1) * D]) for l in range(2) for n in (0, 1, 3, 4)], 1)
    qg, kg = np.asarray(i["mla_q_norm_g_2"]), np.asarray(i["mla_kv_norm_g_2"])
    mlag = np.zeros((P, 6), f)
    for l in range(2):
        mlag[:, 3 * l] = kg[l]
        mlag[:, 3 * l + 1] = qg[l, 0:128]
        mlag[0:64, 3 * l + 2] = qg[l, 128:192]
    con["mlag"] = mlag
    con["pos"] = np.concatenate([np.asarray(i[n])[l].reshape(16, P).T for l in range(2)
                                 for n in ("nsa_cmp_pos_k_2", "nsa_cmp_pos_v_2")], 1)
    t = np.arange(S)
    cend = np.arange(NCMP) * 16 + 31
    dc = (t[:, None] - cend[None, :]).astype(f)
    con["nsac"] = np.where(dc >= 0, -dc, f(NEG)).reshape(2, P, NCMP).transpose(1, 0, 2).reshape(P, -1)
    con["ident"] = np.eye(P, dtype=f)
    rot0, rotm = np.zeros((P, P), f), np.zeros((P, P), f)
    for h in range(2):
        for d in range(half):
            rot0[64 * h + d + half, 64 * h + d] = -1
            rot0[64 * h + d, 64 * h + d + half] = 1
    for d in range(16):
        rotm[64 + d + 16, 64 + d] = -1
        rotm[64 + d, 64 + d + 16] = 1
    con["rot0"], con["rotm"] = rot0, rotm
    fr = np.float32(10000.0) ** (-np.arange(16, dtype=f) / np.float32(16))
    ang = (t.astype(f)[:, None] * fr[None, :]).astype(np.float64)
    cosm, sinm = np.ones((P, S), f), np.zeros((P, S), f)
    for r in (64, 80):
        cosm[r:r + 16] = np.cos(ang).T
        sinm[r:r + 16] = np.sin(ang).T
    con["cosm"], con["sinm"] = cosm, sinm
    dist = (t[:, None] - t[None, :]).astype(f)

    def by_block(m):
        return m.astype(f).reshape(2, P, S).transpose(1, 0, 2).reshape(P, 2 * S)

    con["alibi"] = by_block(np.where(dist >= 0, -dist, f(NEG)))
    con["causal"] = by_block(np.where(dist >= 0, f(0), f(NEG)))
    con["window"] = by_block(np.where((dist >= 0) & (dist < 128), -dist, f(NEG)))
    p = np.asarray(i["p"])
    con["ple"] = np.concatenate([row_tiles(np.ascontiguousarray(p[l, 0].T), 2) for l in range(2)], 1)
    consts = np.concatenate([con[n] for n in COLS], 1)
    assert consts.shape == (P, NCOLS), consts.shape
    return {
        "stream": stream,
        "x": np.ascontiguousarray(np.asarray(i["x"])[0]),
        "consts": np.ascontiguousarray(consts.astype(f, copy=False)),
        "pos": np.ascontiguousarray(np.asarray(i["positions"])[0]),
        "lam": np.ascontiguousarray(np.asarray(i["a_lambda"])[0].reshape(-1)),
        "ln_rows": np.stack([np.asarray(i["c_ln_g"])[0], np.asarray(i["c_ln_b"])[0]]),
        "w_s": np.ascontiguousarray(np.asarray(i["c_w_s"])[0].transpose(2, 0, 1)),
        "sinks": np.ascontiguousarray(np.asarray(i["swa_sinks_2"])),
        "bada_rows": np.ascontiguousarray(np.concatenate([ba[:, 2 * D:3 * D], ba[:, 5 * D:6 * D]], 1)),
        "fin_row": np.stack([np.asarray(i["final_norm"]), np.asarray(i["final_norm_g_2"])]),
    }


def kernel(**inputs):
    import concourse.bacc as bacc
    from concourse.bass_utils import run_bass_kernel_spmd

    nc = bacc.Bacc("TRN2", target_bir_lowering=False, num_devices=1)
    arrays = lay_out(inputs)
    aps = {n: nc.dram_tensor(f"in_{n}", a.shape, mybir.dt.from_np(a.dtype), kind="ExternalInput").ap()
           for n, a in arrays.items()}
    out = nc.dram_tensor("out", (S, D), F32, kind="ExternalOutput").ap()
    build(nc, aps, out)
    r = run_bass_kernel_spmd(nc, [{f"in_{n}": a for n, a in arrays.items()}], core_ids=[0])
    return r.results[0]["out"].reshape(1, S, D)
```

```python
import math
from contextlib import ExitStack

import numpy as np
import concourse.bass as bass
from concourse import mybir

F32 = mybir.dt.float32
I32 = mybir.dt.int32
U32 = mybir.dt.uint32
ALU = mybir.AluOpType
ACT = mybir.ActivationFunctionType
AX = mybir.AxisListType

P = 128
D = 1024
S = 256
KT = D // P
QB = S // P
BANK = 512
SLOT = 2048
RING = 11
F1 = 2816
NE = 8
J1 = F1 // 256
F2 = 4 * D
J2 = F2 // 256
NCMP = S // 16 - 1
RMS_EPS = 1e-6
LN_EPS = 1e-5
NEG = -1e30
GUARD = -1e20
TINY = 1e-30
LAMBDA_INIT = 0.8 - 0.6 * math.exp(-0.3 * 0)
SLOPES = [float(np.float32(2.0 ** (-8.0 * (i + 1) / 12))) for i in range(12)]
NT = 18
(T_SWAQ, T_SWAK, T_CKV, T_CQ, T_KPE, T_GATE, T_NSAQ, T_KC, T_VC, T_KS, T_KW, T_MOBQ,
 T_MOBK) = (0, 2, 3, 4, 6, 7, 8, 10, 11, 12, 13, 14, 16)

W_QK = 0
W_BCH = W_QK + 4
W_V = W_BCH + 6
W_OUT0 = W_V + 2
W_FFN0 = W_OUT0 + 4
W_PLE0 = W_FFN0 + 3 * J1
W_CIN = W_PLE0 + 5
W_COUT = W_CIN + 8
W_MOE = W_COUT + 4
W_PLE1 = W_MOE + 3 * J1 * NE
W_BLK = W_PLE1 + 5
B_ADAC, B_ADAR, B_IN, B_V, B_CMP, B_SMALL, B_OUT, B_MLP = 0, 16, 24, 33, 35, 37, 38, 42
B_ALL = B_MLP + 2 * J2
SLOTS = W_BLK + 2 * B_ALL

COLS = {}
_at = 0
for _n, _w in [("gain", 80), ("subln", 1), ("conv", 12), ("invf", 1), ("bs", 8), ("router", 64),
               ("iota", 8), ("c", 8), ("bada", 64), ("mlag", 6), ("pos", 64), ("nsac", 2 * NCMP),
               ("ident", P), ("before", P), ("slot", 2 * P), ("rot0", P), ("rotm", P), ("cosm", S), ("sinm", S),
               ("alibi", 2 * S), ("causal", 2 * S), ("window", 2 * S), ("ple", 4 * S)]:
    COLS[_n] = (_at, _at + _w)
    _at += _w
NCOLS = _at

NORMS = ["mix0", "ffn0", "ple0", "mix1", "ffn1", "ple1", "b0mix", "b0mlp", "b1mix", "b1mlp"]


def attention_groups(block_layer):
    if block_layer is None:
        return [("diff", qb, hg) for qb in range(QB) for hg in range(2)]
    return [(kind, qb, 0) for qb in range(QB) for kind in ("swa", "moba", "nsac", "nsas", "nsaw", "mla")]


def head_of(kind, u):
    return 2 * (u % 2) + u // 2 if kind in ("moba", "nsac", "nsas", "nsaw") else u


GROUP_BASE = [0, 4, 16]


def swiglu_up(j):
    return 3 * j if j else 1


def mlp_up(j):
    return 2 * j - 1 if j else 0


def build(nc, a, out):
    stream, consts, pos, lam_in, ln_rows, w_s, sinks, bada_rows, fin_row, x_in = (
        a[n] for n in ("stream", "consts", "pos", "lam", "ln_rows", "w_s", "sinks", "bada_rows", "fin_row", "x"))
    with ExitStack() as ctx:
        def sb(name, shape, dt=F32):
            return ctx.enter_context(nc.sbuf_tensor(name, shape, dt))

        def sem(name):
            return ctx.enter_context(nc.semaphore(name))

        ps = ctx.enter_context(nc.psum_tensor("ps", [P, 8, BANK], F32))
        ring = sb("ring", [P, RING, SLOT])
        resid = sb("resid", [P, QB, D])
        xT = sb("xT", [P, KT, S])
        rows = sb("rows", [P, QB, D])
        catT = sb("catT", [P, KT, S])
        arena = sb("arena", [P, 8192])
        score = sb("score", [P, 2, 4, S + 1])
        probT = sb("probT", [P, 2, 8, P])
        grow = sb("grow", [P, 2, D])
        c_all = sb("c_all", [P, KT, P])
        con = sb("con", [P, NCOLS])
        ones = sb("ones", [P, P])
        stat = sb("stat", [P, 16])
        neghalf = sb("neghalf", [P, 8])
        soft = sb("soft", [P, 2, 4, 4])
        csilu = sb("csilu", [P, KT])
        ada = sb("ada", [P, 32])
        modg = sb("modg", [P, 2, 8])
        lam = sb("lam", [P, 8])
        lamv = sb("lamv", [P, 4 * 64])
        sink = sb("sink", [P, 2, 4])
        sub8 = sb("sub8", [P, 1])
        bn = sb("bn", [P, 2, 2, 6])
        mv = sb("mv", [P, 2, 2])
        posi = sb("posi", [P, S], I32)
        gates = sb("gates", [P, QB, 16])
        top = sb("top", [P, QB, 8])
        topi = sb("topi", [P, QB, 8], U32)
        route = sb("route", [P, QB, 4, 8])
        logit = sb("logit", [P, QB, 8])
        member = sb("member", [P, QB, NE])
        place = sb("place", [P, QB, NE])
        most = sb("most", [P, 8])
        most_i = sb("most_i", [P, 1], I32)
        hidc = sb("hidc", [P, 2, 16])
        kcmp = sb("kcmp", [P, 16])
        vcmp = sb("vcmp", [P, 64])

        def col(name, a=0, n=None):
            lo, hi = COLS[name]
            return con[:, lo + a:(lo + a + n if n is not None else hi)]

        ident = col("ident")
        zqk = arena[:, 0:2048].rearrange("p (t s) -> p t s", s=S)
        zbch = arena[:, 2048:5120].rearrange("p (t s) -> p t s", s=S)
        v1 = arena[:, 5120:6144].rearrange("p (b n) -> p b n", b=QB)
        cos0, sin0 = arena[:, 6144:6400], arena[:, 6400:6656]
        ang, turns = arena[:, 6656:6912], arena[:, 6912:7168]
        u_rows = arena[:, 0:2048].rearrange("p (b n) -> p b n", b=QB)
        v_rows = arena[:, 2048:4096].rearrange("p (b n) -> p b n", b=QB)
        ln_g, ln_b = arena[:, 4096:5120], arena[:, 5120:6144]
        ws = arena[:, 6144:7168].rearrange("p (g t) -> p g t", g=8)
        sel = arena[:, 0:256].rearrange("p (b c) -> p b c", b=QB)
        selg = arena[:, 256:512].rearrange("p (b c) -> p b c", b=QB)
        selT = arena[:, 512:768].rearrange("p (b s) -> p b s", b=QB)
        y_rows = arena[:, 1024:2048]
        act_rows = arena[:, 2048:2560].rearrange("p (q n) -> p q n", q=2)
        hid_rows = arena[:, 2560:3072].rearrange("p (q n) -> p q n", q=2)
        hidE = arena[:, 3072:3584].rearrange("p (q k c) -> p q k c", q=2, k=2)
        zT = arena[:, 0:NT * S].rearrange("p (t s) -> p t s", s=S)
        v2 = arena[:, 4608:5632].rearrange("p (b n) -> p b n", b=QB)
        qm = arena[:, 5632:6656].rearrange("p (h s) -> p h s", h=4)
        km = arena[:, 6656:7680].rearrange("p (h s) -> p h s", h=4)
        vm = arena[:, 7680:8192].rearrange("p (b n) -> p b n", b=QB)
        flat0 = score[:, 0].rearrange("p a b -> p (a b)")
        flat1 = score[:, 1].rearrange("p a b -> p (a b)")
        blk = flat1[:, 0:2 * 16 * NCMP].rearrange("p (v l n) -> p v l n", v=2, n=NCMP)
        acth = catT[:, 0:4].rearrange("p (q a) s -> p q (a s)", q=2)
        hidT = catT[:, 4:8].rearrange("p (q a) s -> p q (a s)", q=2)

        def bank(b, n=1):
            return ps[:, b:b + n, :].rearrange("p b n -> p (b n)")

        landed = [sem(f"landed{r}") for r in range(RING)]
        slot_done = sem("slot_done")
        consts_in = sem("consts_in")
        ln_in = sem("ln_in")
        fin_in = sem("fin_in")
        bada_in = sem("bada_in")
        out_done = sem("out_done")
        consts_made = sem("consts_made")
        root_asked = sem("root_asked")
        root_ready = sem("root_ready")
        rows_scaled = sem("rows_scaled")
        rowsT_ready = sem("rowsT_ready")
        normed = sem("normed")
        projT_kept = sem("projT_kept")
        vrows_kept = sem("vrows_kept")
        angles_ready = sem("angles_ready")
        sines_ready = sem("sines_ready")
        rot_ready = sem("rot_ready")
        roped = sem("roped")
        conv_ready = sem("conv_ready")
        lam_asked = sem("lam_asked")
        lam_exp = sem("lam_exp")
        scores_ready = sem("scores_ready")
        shifted = sem("shifted")
        exp_ready = sem("exp_ready")
        probT_ready = sem("probT_ready")
        probT_kept = sem("probT_kept")
        mixed_ready = sem("mixed_ready")
        mixed_kept = sem("mixed_kept")
        heads_ready = sem("heads_ready")
        catT_ready = sem("catT_ready")
        catT_kept = sem("catT_kept")
        resid_ready = sem("resid_ready")
        act_ready = sem("act_ready")
        hid_ready = sem("hid_ready")
        ple_gated = sem("ple_gated")
        gelu_done = sem("gelu_done")
        vn_ready = sem("vn_ready")
        ws_masked = sem("ws_masked")
        spatial_ready = sem("spatial_ready")
        spatial_gated = sem("spatial_gated")
        logits_ready = sem("logits_ready")
        route_asked = sem("route_asked")
        route_exp = sem("route_exp")
        member_ready = sem("member_ready")
        ranks_ready = sem("ranks_ready")
        routed = sem("routed")
        moe_done = sem("moe_done")

        class Pass:

            def __init__(self, name, chunk, landed, done, first_slot):
                self.chunk, self.landed, self.done, self.first = chunk, landed, done, first_slot
                self.sel_ready = sem(name + "sel_ready")
                self.gather_ready = sem(name + "gather_ready")
                self.gathered = sem(name + "gathered")
                self.selT_ready = sem(name + "selT_ready")
                self.selT_kept = sem(name + "selT_kept")
                self.act_ready = sem(name + "act_ready")
                self.hid_ready = sem(name + "hid_ready")
                self.hidT_ready = sem(name + "hidT_ready")
                self.hidT_kept = sem(name + "hidT_kept")
                self.y_kept = sem(name + "y_kept")
                self.scattered = sem(name + "scattered")
                self.merged = sem(name + "merged")

        more_landed = [sem(f"more_landed{r}") for r in range(RING)]
        more_done = sem("more_done")
        csilu_ready = sem("csilu_ready")
        mod_ready = sem("mod_ready")
        grow_ready = sem("grow_ready")
        squares_ready = sem("squares_ready")
        latsum_ready = sem("latsum_ready")
        latms_ready = sem("latms_ready")
        latroot_ready = sem("latroot_ready")
        latent_ready = sem("latent_ready")
        mlaheads_ready = sem("mlaheads_ready")
        mlaheads_kept = sem("mlaheads_kept")
        mlarot_ready = sem("mlarot_ready")
        mla_ready = sem("mla_ready")
        cmpblk_ready = sem("cmpblk_ready")
        cmpact_ready = sem("cmpact_ready")
        cmp_kept = sem("cmp_kept")
        gateT_ready = sem("gateT_ready")
        gates_ready = sem("gates_ready")
        sink_ready = sem("sink_ready")
        dve_step = sem("dve_step")
        act_step = sem("act_step")
        pool_step = sem("pool_step")

        first_pass = Pass("moe_", 0, landed, slot_done, W_MOE)
        second_pass = Pass("more_", 1, more_landed, more_done, 0)

        def overflowing(eng):
            eng.wait_ge(routed, 1)
            return eng.value_load(most_i[0:1, 0:1], min_val=0, max_val=S) > P

        def bc(ap, n):
            return ap.unsqueeze(2).broadcast_to([ap.shape[0], ap.shape[1], n])

        def rep(ap, n):
            return ap.unsqueeze(1).broadcast_to([ap.shape[0], n, ap.shape[1]])

        block = ctx.enter_context(nc.Block())

        @block.sync
        def _(sp):
            for r in range(RING):
                sp.dma_start(ring[:, r, :], stream[r]).then_inc(landed[r], 16)
            laps = SLOTS // RING
            moe0, moe1 = W_MOE // RING, (W_MOE + 3 * J1 * NE) // RING
            assert W_MOE % RING == 0 and (3 * J1) % RING == 0

            def laps_of(start, end):
                with sp.Fori(start, end) as lap:
                    for r in range(RING):
                        sp.wait_ge(slot_done, lap * RING + (r + 1 - RING))
                        sp.dma_start(ring[:, r, :],
                                     stream[bass.ds(lap * RING + r, 1)].rearrange("a p n -> (a p) n"))\
                            .then_inc(landed[r], 16)

            laps_of(1, moe1)
            with sp.If(overflowing(sp)):
                sp.wait_ge(slot_done, moe1 * RING)
                for r in range(RING):
                    sp.dma_start(ring[:, r, :], stream[W_MOE + r]).then_inc(more_landed[r], 16)
                with sp.Fori(1, moe1 - moe0) as lap:
                    for r in range(RING):
                        sp.wait_ge(more_done, lap * RING + (r + 1 - RING))
                        sp.dma_start(ring[:, r, :],
                                     stream[bass.ds(lap * RING + (W_MOE + r), 1)].rearrange("a p n -> (a p) n"))\
                            .then_inc(more_landed[r], 16)
                sp.wait_ge(more_done, (moe1 - moe0) * RING)
            laps_of(moe1, laps)
            for n in range(laps * RING, SLOTS):
                sp.wait_ge(slot_done, n + 1 - RING)
                sp.dma_start(ring[:, n % RING, :], stream[n]).then_inc(landed[n % RING], 16)
            sp.wait_ge(resid_ready, 12)
            sp.dma_start(out.rearrange("(b p) n -> p b n", p=P), rows[:, :, :]).then_inc(out_done, 16)
            sp.wait_ge(out_done, 16)

        @block.tensor
        def _(pe):
            def slot(n):
                pe.wait_ge(landed[n % RING], 16 * (n // RING + 1))
                return ring[:, n % RING, :]

            def rowsT(k):
                for t in range(QB):
                    pe.wait_ge(rows_scaled, QB * (k + (k >= 6)) + t + 1)
                    for half in range(2):
                        for i in range(4):
                            f = 4 * half + i
                            last = pe.transpose(ps[:, 4 + 2 * t + half, i * P:(i + 1) * P],
                                                rows[:, t, f * P:(f + 1) * P], ident)
                        last.then_inc(rowsT_ready, 1)
                pe.wait_ge(normed, 4 * (k + 1))

            def tiles(n0, count, job0, fresh):
                for s in range(count):
                    w = slot(n0 + s).rearrange("p (k n) -> p k n", k=KT)
                    if s >= 4 or not fresh:
                        pe.wait_ge(projT_kept, job0 + s - 3)
                    for i in range(2):
                        for k in range(KT):
                            last = pe.matmul(ps[:, s % 4, i * S:(i + 1) * S], w[:, k, i * P:(i + 1) * P],
                                             xT[:, k, :], start=k == 0, stop=k == KT - 1)
                    last.then_inc(slot_done, 1)

            def row_product(n0, src, b0):
                for s in range(4):
                    w = slot(n0 + s).rearrange("p (k n) -> p k n", k=2)
                    for kk in range(2):
                        for t in range(QB):
                            for half in range(2):
                                k = 2 * s + kk
                                last = pe.matmul(ps[:, b0 + 2 * t + half, :], src[:, k, t * P:(t + 1) * P],
                                                 w[:, kk, half * BANK:(half + 1) * BANK],
                                                 start=k == 0, stop=k == KT - 1)
                    last.then_inc(slot_done, 1)

            def value_rows(n0):
                for s in range(2):
                    w = slot(n0 + s).rearrange("p (k n) -> p k n", k=4)
                    for kk in range(4):
                        for t in range(QB):
                            k = 4 * s + kk
                            last = pe.matmul(ps[:, 4 + t, :], xT[:, k, t * P:(t + 1) * P], w[:, kk, :],
                                             start=k == 0, stop=k == KT - 1)
                    last.then_inc(slot_done, 1)

            def cat_transpose(tiles_):
                for t in range(QB):
                    for half in range(tiles_ // 4):
                        for i in range(4):
                            f = 4 * half + i
                            last = pe.transpose(ps[:, 4 + 2 * t + half, i * P:(i + 1) * P],
                                                rows[:, t, f * P:(f + 1) * P], ident)
                        last.then_inc(catT_ready, 1)

            def attention(layer):
                groups = attention_groups(layer)
                base = GROUP_BASE[0 if layer is None else layer + 1]

                def scores(i):
                    kind, qb, hg = groups[i]
                    g = base + i
                    if i >= 2:
                        pe.wait_ge(shifted, g - 1)
                    kw = NCMP if kind == "nsac" else P * (qb + 1)
                    qs = slice(qb * P, (qb + 1) * P)
                    for u in range(4):
                        if kind == "diff":
                            r, h = 64 * (u // 2), 2 * hg + u % 2
                            q, k = zqk[r:r + 64, h, qs], zqk[r:r + 64, 4 + h, 0:kw]
                        elif kind == "swa":
                            r = 64 * (u // 2)
                            q, k = zT[r:r + 64, T_SWAQ + u % 2, qs], zT[r:r + 64, T_SWAK, 0:kw]
                        elif kind == "moba":
                            r = 64 * (u // 2)
                            q, k = zT[r:r + 64, T_MOBQ + u % 2, qs], zT[r:r + 64, T_MOBK + u % 2, 0:kw]
                        elif kind == "mla":
                            q, k = qm[:, u, qs], km[:, u, 0:kw]
                        else:
                            r = 64 * (u // 2)
                            q = zT[r:r + 64, T_NSAQ + u % 2, qs]
                            k = {"nsac": kcmp[r:r + 64, 0:NCMP], "nsas": zT[r:r + 64, T_KS, 0:kw],
                                 "nsaw": zT[r:r + 64, T_KW, 0:kw]}[kind]
                        last = pe.matmul(ps[:, 2 * (g % 2) + u // 2, (u % 2) * S:(u % 2) * S + kw], q, k,
                                         start=True, stop=True)
                    last.then_inc(scores_ready, 1)

                def transposes(i):
                    kind, qb, hg = groups[i]
                    g = base + i
                    pe.wait_ge(exp_ready, g + 1)
                    pe.wait_ge(probT_kept, g)
                    nkb = 1 if kind == "nsac" else qb + 1
                    kp = NCMP if kind == "nsac" else P
                    for u in range(4):
                        for kb in range(nkb):
                            n = u * nkb + kb
                            last = pe.transpose(ps[0:kp, 4 + n // 4, (n % 4) * P:(n % 4 + 1) * P],
                                                score[:, g % 2, u, kb * P:kb * P + kp], ident)
                    last.then_inc(probT_ready, 1)

                def mix(i):
                    kind, qb, hg = groups[i]
                    g = base + i
                    pe.wait_ge(probT_kept, g + 1)
                    if i >= 2:
                        pe.wait_ge(mixed_kept, g - 1)
                    nkb = 1 if kind == "nsac" else qb + 1
                    kp = NCMP if kind == "nsac" else P
                    vw = P if kind == "diff" else 64
                    for u in range(4):
                        o = head_of(kind, u)
                        for kb in range(nkb):
                            if kind == "diff":
                                h = 2 * hg + u % 2
                                v = v1[:, kb, h * P:(h + 1) * P]
                            elif kind == "swa":
                                v = v2[:, kb, (o // 2) * 64:(o // 2) * 64 + 64]
                            elif kind == "nsas":
                                v = v2[:, kb, 128:192]
                            elif kind == "nsaw":
                                v = v2[:, kb, 192:256]
                            elif kind == "moba":
                                v = v2[:, kb, 256 + o * 64:256 + o * 64 + 64]
                            elif kind == "mla":
                                v = vm[:, kb, o * 64:o * 64 + 64]
                            else:
                                v = vcmp[0:kp, :]
                            last = pe.matmul(ps[:, 6 + g % 2, o * vw:(o + 1) * vw],
                                             probT[0:kp, g % 2, u * nkb + kb, :], v,
                                             start=kb == 0, stop=kb == nkb - 1)
                    last.then_inc(mixed_ready, 1)

                scores(0)
                for i in range(len(groups)):
                    if i + 1 < len(groups):
                        scores(i + 1)
                    transposes(i)
                    mix(i)

            def up(slots, j, ready):
                if j >= 2:
                    pe.wait_ge(hid_ready, ready(j - 2))
                for get, b in slots:
                    w = get()
                    for i in range(2):
                        for k in range(KT):
                            last = pe.matmul(ps[:, b, i * S:(i + 1) * S], w[:, k, i * P:(i + 1) * P],
                                             xT[:, k, :], start=k == 0, stop=k == KT - 1)
                    last.then_inc(slot_done, 1)

            def down(get, j, ready, first, final):
                pe.wait_ge(hid_ready, ready(j))
                w = get()
                for kk in range(2):
                    for t in range(QB):
                        for half in range(2):
                            last = pe.matmul(ps[:, 4 + 2 * t + half, :],
                                             hidT[:, j % 2, kk * S + t * P:kk * S + (t + 1) * P],
                                             w[:, kk, half * BANK:(half + 1) * BANK],
                                             start=first and kk == 0, stop=final and kk == 1)
                last.then_inc(slot_done, 1)

            def wslot(n, k):
                def get():
                    return slot(n).rearrange("p (k n) -> p k n", k=k)
                return get

            def swiglu(n0):
                n = n0

                def ready(j):
                    return j + 1

                for j in range(J1 + 1):
                    if j < J1:
                        up([(wslot(n + i, KT), 2 * (j % 2) + i) for i in range(2)], j, ready)
                        n += 2
                    if j >= 1:
                        down(wslot(n, 2), j - 1, ready, j == 1, j == J1)
                        n += 1

            pe.wait_ge(consts_in, 16 * 6)
            pe.wait_ge(consts_made, 1)
            rowsT(0)
            tiles(W_QK, 4, 0, True)
            tiles(W_BCH, 6, 4, False)
            value_rows(W_V)
            pe.wait_ge(projT_kept, 10)
            for t in range(8):
                last = pe.matmul(ps[:, t // 2, (t % 2) * S:(t % 2 + 1) * S], col("rot0"), zqk[:, t, :],
                                 start=True, stop=True)
            last.then_inc(rot_ready, 1)
            pe.wait_ge(roped, 1)
            pe.wait_ge(vrows_kept, 1)
            attention(None)
            pe.wait_ge(heads_ready, 1)
            cat_transpose(4)
            pe.wait_ge(catT_kept, 2)
            pe.wait_ge(conv_ready, 1)
            row_product(W_OUT0, catT, 4)
            rowsT(1)
            swiglu(W_FFN0)

            def ple(layer, n0):
                row_product(n0, xT, 4)
                w = slot(n0 + 4).rearrange("p (k n) -> p k n", k=2)
                for k in range(2):
                    for t in range(QB):
                        for half in range(2):
                            a = (2 * layer + k) * S + t * P
                            last = pe.matmul(ps[:, 2 * t + half, :], col("ple", a, P),
                                             w[:, k, half * BANK:(half + 1) * BANK], start=k == 0, stop=k == 1)
                last.then_inc(slot_done, 1)

            rowsT(2)
            ple(0, W_PLE0)
            rowsT(3)
            row_product(W_CIN, xT, 0)
            row_product(W_CIN + 4, xT, 4)
            pe.wait_ge(ws_masked, 1)
            for t in range(QB):
                pe.wait_ge(vn_ready, t + 1)
                for half in range(2):
                    for i in range(4):
                        g = 4 * half + i
                        last = pe.matmul(ps[:, 2 * t + half, i * P:(i + 1) * P], ws[:, g, :],
                                         v_rows[:, t, g * P:(g + 1) * P], start=True, stop=True)
                    last.then_inc(spatial_ready, 1)
            pe.wait_ge(heads_ready, 2)
            cat_transpose(8)
            pe.wait_ge(catT_kept, 6)
            row_product(W_COUT, catT, 4)
            rowsT(4)
            for t in range(QB):
                for k in range(KT):
                    last = pe.matmul(ps[:, 0, t * 8:(t + 1) * 8], xT[:, k, t * P:(t + 1) * P],
                                     col("router", k * 8, 8), start=k == 0, stop=k == KT - 1)
            last.then_inc(logits_ready, 1)
            pe.wait_ge(member_ready, 1)
            pe.matmul(ps[:, 1, 0:8], col("before"), member[:, 0, :], start=True, stop=True)
            pe.matmul(ps[:, 1, 8:16], col("before"), member[:, 1, :], start=True, stop=False)
            pe.matmul(ps[:, 1, 8:16], ones[:, :], member[:, 0, :], start=False, stop=True)
            for t in range(QB):
                last = pe.matmul(ps[:, 1, 16:24], ones[:, :], member[:, t, :], start=t == 0, stop=t == 1)
            last.then_inc(ranks_ready, 1)

            def experts(w):
                with pe.Fori(0, NE) as e:
                    pe.wait_ge(w.sel_ready, e + 1)
                    for half in range(2):
                        for i in range(4):
                            f = 4 * half + i
                            for t in range(QB):
                                last = pe.matmul(ps[:, 6 + half, i * P:(i + 1) * P], rows[:, t, f * P:(f + 1) * P],
                                                 sel[:, t, :], start=t == 0, stop=t == 1)
                        last.then_inc(w.gather_ready, 1)
                    for t in range(QB):
                        last = pe.transpose(ps[:, 3, t * P:(t + 1) * P], selg[:, t, :], ident)
                    last.then_inc(w.selT_ready, 1)
                    pe.wait_ge(w.gathered, e * 2 + 2)

                    def weights(i, k):
                        pe.wait_ge(w.landed[i % RING],
                                   16 * (e * (3 * J1 // RING) + (w.first // RING + i // RING + 1)))
                        return ring[:, i % RING, :].rearrange("p (k n) -> p k n", k=k)

                    def up(i, b, n0):
                        m = weights(i, KT)
                        for k in range(KT):
                            last = pe.matmul(ps[:, b, n0:n0 + 256], xT[:, k, 0:P], m[:, k, :],
                                             start=k == 0, stop=k == KT - 1)
                        last.then_inc(w.done, 1)

                    def turn(j):
                        pe.wait_ge(w.hid_ready, e * J1 + (j + 1))
                        for i in range(2):
                            c = 256 * (j % 2) + i * P
                            last = pe.transpose(ps[:, 2, c:c + P], hid_rows[:, j % 2, i * P:(i + 1) * P], ident)
                        last.then_inc(w.hidT_ready, 1)

                    def down(i, j):
                        m = weights(i, 2)
                        pe.wait_ge(w.hidT_kept, e * J1 + (j + 1))
                        for kk in range(2):
                            for half in range(2):
                                last = pe.matmul(ps[:, 4 + half, :], hidE[:, j % 2, kk, :],
                                                 m[:, kk, half * BANK:(half + 1) * BANK],
                                                 start=j == 0 and kk == 0, stop=j == J1 - 1 and kk == 1)
                        last.then_inc(w.done, 1)

                    n = 0
                    for j in range(J1 + 1):
                        if j < J1:
                            up(n, j % 2, 0)
                        if j >= 1:
                            turn(j - 1)
                        if j < J1:
                            up(n + 1, j % 2, 256)
                            n += 2
                        if j >= 1:
                            down(n, j - 1)
                            n += 1
                    pe.wait_ge(w.selT_kept, e + 1)
                    pe.wait_ge(w.y_kept, e * 2 + 2)
                    for t in range(QB):
                        for half in range(2):
                            last = pe.matmul(ps[:, (6, 0)[t] + half, :], selT[:, t, :],
                                             y_rows[:, half * BANK:(half + 1) * BANK], start=True, stop=True)
                        last.then_inc(w.scattered, 1)

            experts(first_pass)
            with pe.If(overflowing(pe)):
                experts(second_pass)
            rowsT(5)
            ple(1, W_PLE1)
            for l in range(2):
                n0 = W_BLK + l * B_ALL
                pe.wait_ge(csilu_ready, 2)
                pe.wait_ge(resid_ready, 7 + 2 * l)
                for s in range(16):
                    w = slot(n0 + B_ADAC + s).rearrange("p (k n) -> p k n", k=KT)
                    for i in range(2):
                        for k in range(KT):
                            last = pe.matmul(ps[:, 0, 2 * s + i:2 * s + i + 1], w[:, k, i * P:(i + 1) * P],
                                             csilu[:, k:k + 1], start=k == 0, stop=k == KT - 1)
                    last.then_inc(slot_done, 1)
                for s in range(8):
                    w = slot(n0 + B_ADAR + s).rearrange("p (k n) -> p k n", k=2)
                    for kk in range(2):
                        for half in range(2):
                            k = 2 * (s % 4) + kk
                            last = pe.matmul(ps[:, 4 + 2 * (s // 4) + half, :], c_all[:, k, :],
                                             w[:, kk, half * BANK:(half + 1) * BANK],
                                             start=k == 0, stop=k == KT - 1)
                    last.then_inc(slot_done, 1)
                pe.wait_ge(grow_ready, l + 1)
                rowsT(6 + 2 * l)
                job0 = 10 + 9 * l
                tiles(n0 + B_IN, 9, job0, True)
                value_rows(n0 + B_V)
                pe.wait_ge(projT_kept, job0 + 9)
                pe.wait_ge(squares_ready, l + 1)
                sq = flat0
                pe.matmul(ps[:, 0, 0:S], ones[:, :], sq[:, 0:S], start=True, stop=True)
                for k in range(2):
                    last = pe.matmul(ps[:, 0, S:2 * S], ones[:, :], sq[:, (k + 1) * S:(k + 2) * S],
                                     start=k == 0, stop=k == 1)
                last.then_inc(latsum_ready, 1)
                for t in range(QB):
                    last = pe.transpose(ps[:, 1, t * P:(t + 1) * P], zT[:, T_GATE, t * P:(t + 1) * P], ident)
                last.then_inc(gateT_ready, 1)
                pe.wait_ge(cmpblk_ready, l + 1)
                for which in range(2):
                    w = slot(n0 + B_CMP + which).rearrange("p (l n) -> p l n", l=16)
                    for j in range(16):
                        last = pe.matmul(ps[:, 7, which * 16:which * 16 + NCMP], w[:, j, :], blk[:, which, j, :],
                                         start=j == 0, stop=j == 15)
                    last.then_inc(slot_done, 1)
                w = slot(n0 + B_SMALL)
                uq = w[:, 0:1024].rearrange("p (k n) -> p k n", k=2)
                ukk, ukv, ck2, cv2 = w[:, 1024:1280], w[:, 1280:1536], w[:, 1536:1664], w[:, 1664:1728]
                pe.wait_ge(vrows_kept, 2 + l)
                pe.wait_ge(latent_ready, l + 1)
                for h in range(4):
                    for k in range(2):
                        pe.matmul(ps[:, 2 + h // 2, (h % 2) * S:(h % 2 + 1) * S], uq[:, k, h * P:(h + 1) * P],
                                  zT[:, T_CQ + k, :], start=k == 0, stop=k == 1)
                for h in range(4):
                    pe.matmul(ps[0:64, 4 + h // 2, (h % 2) * S:(h % 2 + 1) * S], ukk[:, h * 64:(h + 1) * 64],
                              zT[:, T_CKV, :], start=True, stop=True)
                for t in range(QB):
                    last = pe.matmul(ps[:, 6, t * S:(t + 1) * S], zT[:, T_CKV, t * P:(t + 1) * P], ukv,
                                     start=True, stop=True)
                last.then_inc(mlaheads_ready, 1)
                pe.wait_ge(cmpact_ready, l + 1)
                pe.matmul(ps[:, 7, 32:32 + NCMP], ck2, hidc[:, 0, 0:NCMP], start=True, stop=True)
                pe.matmul(ps[0:NCMP, 7, 64:128], hidc[:, 1, 0:NCMP], cv2, start=True, stop=True)\
                    .then_inc(slot_done, 1)
                pe.wait_ge(mlaheads_kept, l + 1)
                pe.wait_ge(gates_ready, l + 1)
                for h in range(4):
                    pe.matmul(ps[:, 2 + h // 2, (h % 2) * S:(h % 2 + 1) * S], col("rotm"), qm[:, h, :],
                              start=True, stop=True)
                last = pe.matmul(ps[:, 1, 0:S], col("rotm"), zT[:, T_KPE, :], start=True, stop=True)
                last.then_inc(mlarot_ready, 1)
                pe.wait_ge(mla_ready, l + 1)
                pe.wait_ge(cmp_kept, l + 1)
                attention(l)
                pe.wait_ge(mixed_kept, GROUP_BASE[1 + l] + 12)
                cat_transpose(8)
                pe.wait_ge(catT_kept, 10 + 4 * l)
                row_product(n0 + B_OUT, catT, 4)
                rowsT(7 + 2 * l)
                step0 = J1 + l * J2

                def ready(j):
                    return step0 + j + 1

                n = n0 + B_MLP
                for j in range(J2 + 1):
                    if j < J2:
                        up([(wslot(n, KT), j % 2)], j, ready)
                        n += 1
                    if j >= 1:
                        down(wslot(n, 2), j - 1, ready, j == 1, j == J2)
                        n += 1

        @block.vector
        def _(dve):
            steps = [0]

            def link(ins):
                steps[0] += 1
                ins.then_inc(dve_step, 1)
                dve.wait_ge(dve_step, steps[0])

            roots = [0]

            def root(src, n, scale, eps):
                dve.tensor_scalar(stat[:, 0:n], src, scale, eps, ALU.mult, ALU.add).then_inc(root_asked, 1)
                roots[0] += 1
                dve.wait_ge(root_ready, roots[0])

            def norm_rows():
                for t in range(QB):
                    link(dve.tensor_tensor_reduce(out=rows[:, t, :], in0=resid[:, t, :], in1=resid[:, t, :],
                                                  scale=1.0, scalar=0.0, op0=ALU.mult, op1=ALU.add,
                                                  accum_out=stat[:, 8 + t:9 + t]))
                root(stat[:, 8:10], 2, 1.0 / D, RMS_EPS)
                for t in range(QB):
                    dve.tensor_scalar(rows[:, t, :], resid[:, t, :], stat[:, t:t + 1], None, ALU.mult)\
                        .then_inc(rows_scaled, 1)

            def norm(k, gain, shift=None):
                norm_rows()
                for t in range(QB):
                    for half in range(2):
                        b = 2 * t + half
                        dve.wait_ge(rowsT_ready, 4 * k + b + 1)
                        src = ps[:, 4 + b, :].rearrange("p (f s) -> p f s", f=4)
                        dst = xT[:, 4 * half:4 * half + 4, t * P:(t + 1) * P]
                        ins = dve.tensor_tensor(dst, src, bc(gain[:, 4 * half:4 * half + 4], P), ALU.mult)
                        if shift is not None:
                            link(ins)
                            ins = dve.tensor_tensor(dst, dst, bc(shift[:, 4 * half:4 * half + 4], P), ALU.add)
                        ins.then_inc(normed, 1)

            def gain(k):
                return col("gain", 8 * k, 8)

            def add_branch(gate=None):
                for t in range(QB):
                    for half in range(2):
                        c = slice(half * BANK, (half + 1) * BANK)
                        src = ps[:, 4 + 2 * t + half, :]
                        if gate is not None:
                            link(dve.tensor_tensor(rows[:, t, c], src, gate[:, c], ALU.mult))
                            src = rows[:, t, c]
                        ins = dve.tensor_tensor(resid[:, t, c], resid[:, t, c], src, ALU.add)
                        if (t, half) == (1, 1):
                            ins.then_inc(resid_ready, 1)
                        else:
                            link(ins)

            def attention(layer):
                groups = attention_groups(layer)
                base = GROUP_BASE[0 if layer is None else layer + 1]

                def soften(i):
                    kind, qb, hg = groups[i]
                    g = base + i
                    kw = NCMP if kind == "nsac" else P * (qb + 1)
                    src = bank(2 * (g % 2), 2).rearrange("p (u k) -> p u k", u=4)[:, :, 0:kw]
                    sc = score[:, g % 2, :, 0:kw]
                    m = soft[:, g % 2, 0, :]
                    dve.wait_ge(scores_ready, g + 1)
                    if i >= 2:
                        dve.wait_ge(probT_ready, g - 1)
                    if kind in ("diff", "mla"):
                        link(dve.tensor_tensor(sc, src, rep(col("causal", qb * S, kw), 4), ALU.add))
                    else:
                        table = {"swa": col("window", qb * S, kw), "nsac": col("nsac", qb * NCMP, NCMP)}
                        first = {"swa": 0, "moba": 2}.get(kind, 1)
                        for u in range(4):
                            ins = dve.scalar_tensor_tensor(
                                out=sc[:, u, :], in0=table.get(kind, col("alibi", qb * S, kw)),
                                scalar=SLOPES[first + 3 * head_of(kind, u)] * 8.0, in1=src[:, u, :], op0=ALU.mult, op1=ALU.add)
                        link(ins)
                    if kind == "swa":
                        sc = score[:, g % 2, :, 0:kw + 1]
                        link(dve.tensor_scalar(sc[:, :, kw:kw + 1].rearrange("p u o -> p (u o)"), sink[:, layer, :],
                                               8.0, None, ALU.mult))
                    link(dve.tensor_reduce(m, sc, AX.X, ALU.max))
                    if kind == "nsac":
                        link(dve.tensor_scalar(m, m, GUARD, None, ALU.max))
                    dve.tensor_tensor(sc, sc, bc(m, sc.shape[2]), ALU.subtract).then_inc(shifted, 1)

                def finish(i):
                    kind, qb, hg = groups[i]
                    g = base + i
                    kw = NCMP if kind == "nsac" else P * (qb + 1) + (kind == "swa")
                    den, rden, coef = (soft[:, g % 2, n, :] for n in (1, 2, 3))
                    dve.wait_ge(exp_ready, g + 1)
                    to = den.rearrange("p (i r) -> p r i", i=2) if head_of(kind, 1) == 2 else \
                        den.rearrange("p (r i) -> p r i", r=2)
                    link(dve.tensor_reduce(to, score[:, g % 2, :, 0:kw].rearrange("p (r i) k -> p r i k", r=2),
                                           AX.X, ALU.add))
                    link(dve.tensor_scalar(den, den, TINY, None, ALU.max))
                    link(dve.reciprocal(rden, den))
                    w = P if kind == "diff" else 64
                    src = ps[:, 6 + g % 2, 0:4 * w].rearrange("p (u n) -> p u n", u=4)
                    if kind == "diff":
                        link(dve.tensor_tensor(coef, rden, lam[:, 4:8], ALU.mult))
                        dve.wait_ge(mixed_ready, g + 1)
                        tmp = xT[:, 0:2, :].rearrange("p a (b n) -> p (a b) n", b=2)
                        link_kept(dve.tensor_tensor(tmp, src, bc(coef, P), ALU.mult), g)
                        link(dve.tensor_tensor(rows[:, qb, hg * S:(hg + 1) * S], xT[:, 0, :], xT[:, 1, :], ALU.add))
                        return
                    m0 = {"swa": 0, "mla": 256, "moba": 768}.get(kind, 512)
                    dst = rows[:, qb, m0:m0 + 256].rearrange("p (u n) -> p u n", u=4)
                    if kind.startswith("nsa"):
                        b = "csw".index(kind[3])
                        if (kind, qb) == ("nsac", 0):
                            dve.wait_ge(gates_ready, layer + 1)
                        link(dve.tensor_tensor(coef, rden, gates[:, qb, 4 * b:4 * b + 4], ALU.mult))
                        dve.wait_ge(mixed_ready, g + 1)
                        if kind == "nsac":
                            link_kept(dve.tensor_tensor(dst, src, bc(coef, 64), ALU.mult), g)
                        else:
                            tmp = catT[:, 0, :].rearrange("p (u n) -> p u n", u=4)
                            link_kept(dve.tensor_tensor(tmp, src, bc(coef, 64), ALU.mult), g)
                            link(dve.tensor_tensor(dst, dst, tmp, ALU.add))
                    else:
                        dve.wait_ge(mixed_ready, g + 1)
                        link_kept(dve.tensor_tensor(dst, src, bc(rden, 64), ALU.mult), g)

                soften(0)
                for i in range(len(groups)):
                    if i + 1 < len(groups):
                        soften(i + 1)
                    finish(i)

            def link_kept(ins, g):
                ins.then_inc(mixed_kept, 1)
                dve.wait_ge(mixed_kept, g + 1)

            def hidden(j, ready, paired):
                dve.wait_ge(act_ready, ready(j))
                p = j % 2
                other = acth[:, p, :]
                if paired:
                    dve.wait_ge(slot_done, W_FFN0 + swiglu_up(j) + 1)
                    other = ps[:, 2 * p + 1, :]
                dve.tensor_tensor(hidT[:, p, :], acth[:, p, :], other, ALU.mult).then_inc(hid_ready, 1)

            dve.memset(ones[:, :], 1.0).then_inc(consts_made, 1)
            dve.wait_ge(consts_in, 16 * 6)
            link(dve.tensor_copy(ang, posi[:, :]))
            link(dve.tensor_scalar(ang, ang, col("invf"), None, ALU.mult))
            magic = 1.5 * 2.0 ** 23
            link(dve.tensor_scalar(turns, ang, 1.0 / (2 * math.pi), magic, ALU.mult, ALU.add))
            link(dve.tensor_scalar(turns, turns, -magic, None, ALU.add))
            c1 = 6.28125
            c2 = math.floor((2 * math.pi - c1) * 2 ** 21) / 2 ** 21
            c3 = 2 * math.pi - c1 - c2
            for c in (c1, c2, c3):
                link(dve.scalar_tensor_tensor(out=ang, in0=turns, scalar=-c, in1=ang, op0=ALU.mult, op1=ALU.add))
            lim = float(np.nextafter(np.float32(math.pi), np.float32(0)))
            link(dve.tensor_scalar(ang, ang, -lim, lim, ALU.max, ALU.min))
            link(dve.tensor_scalar(turns, ang, -1.0, None, ALU.mult))
            link(dve.tensor_tensor(turns, turns, ang, ALU.max))
            dve.tensor_scalar(turns, turns, -1.0, math.pi / 2, ALU.mult, ALU.add).then_inc(angles_ready, 1)
            for i in range(2):
                link(dve.tensor_tensor_reduce(out=rows[:, 0, 0:64], in0=lamv[:, 128 * i:128 * i + 64],
                                              in1=lamv[:, 128 * i + 64:128 * i + 128], scale=1.0, scalar=0.0,
                                              op0=ALU.mult, op1=ALU.add, accum_out=lam[:, i:i + 1]))
            dve.memset(lam[:, 4:8], 1.0).then_inc(lam_asked, 1)
            dve.wait_ge(lam_exp, 1)
            link(dve.tensor_tensor(lam[:, 0:1], lam[:, 3:4], lam[:, 2:3], ALU.subtract))
            link(dve.tensor_scalar(lam[:, 0:1], lam[:, 0:1], -LAMBDA_INIT, None, ALU.add))
            for i in (6, 7):
                dve.tensor_copy(lam[:, i:i + 1], lam[:, 0:1])
            link(dve.tensor_scalar(sub8[:, :], col("subln"), 1.0 - LAMBDA_INIT, None, ALU.mult))
            dve.wait_ge(csilu_ready, 1)
            dve.tensor_copy(c_all[:, :, :], bc(csilu[:, :], P)).then_inc(csilu_ready, 1)

            norm(0, gain(0))
            dve.wait_ge(rot_ready, 1)
            dve.wait_ge(sines_ready, 2)
            rot = bank(0, 4).rearrange("p (t s) -> p t s", s=S)
            rtmp = rows[:, :, :].rearrange("p b (t s) -> p (b t) s", s=S)
            link(dve.tensor_tensor(rtmp, rot, rep(sin0, 8), ALU.mult))
            link(dve.tensor_tensor(zqk, zqk, rep(cos0, 8), ALU.mult))
            dve.tensor_tensor(zqk, zqk, rtmp, ALU.add).then_inc(roped, 1)
            zb, zc, zh = zbch[:, 0:4, :], zbch[:, 4:8, :], zbch[:, 8:12, :]
            link(dve.tensor_tensor(zc, zc, zh, ALU.mult))
            for i in range(4):
                ins = dve.tensor_scalar(zh[:, i, :], zc[:, i, :], col("conv", 3 * i + 2, 1), None, ALU.mult)
            link(ins)
            for tap in (1, 0):
                lag = 2 - tap
                for i in range(4):
                    ins = dve.scalar_tensor_tensor(out=zh[:, i, lag:S], in0=zc[:, i, 0:S - lag],
                                                   scalar=col("conv", 3 * i + tap, 1), in1=zh[:, i, lag:S],
                                                   op0=ALU.mult, op1=ALU.add)
                link(ins)
            dve.tensor_tensor(catT[:, 4:8, :], zh, zb, ALU.mult).then_inc(conv_ready, 1)
            attention(None)
            heads = rows[:, :, 0:512].rearrange("p b (h n) -> p b h n", h=4)
            sq = xT[:, 0:4, :].rearrange("p (b a) (h n) -> p b (a h) n", b=2, h=2)
            for t in range(QB):
                link(dve.tensor_tensor(sq[:, t], heads[:, t], heads[:, t], ALU.mult))
            link(dve.tensor_reduce(stat[:, 8:16], sq.rearrange("p b h n -> p (b h) n"), AX.X, ALU.add))
            root(stat[:, 8:16], 8, 1.0 / P, RMS_EPS)
            for t in range(QB):
                ins = dve.tensor_tensor(heads[:, t], heads[:, t], bc(stat[:, 4 * t:4 * t + 4], P), ALU.mult)
                if t == 0:
                    link(ins)
            ins.then_inc(heads_ready, 1)
            dve.wait_ge(slot_done, W_OUT0 + 4)
            add_branch()
            dve.wait_ge(resid_ready, 1)
            norm(1, gain(1))
            for j in range(J1):
                hidden(j, lambda j: j + 1, True)
            dve.wait_ge(slot_done, W_FFN0 + 3 * J1)
            add_branch()
            dve.wait_ge(resid_ready, 2)

            def ple(layer, n):
                for t in range(QB):
                    for half in range(2):
                        c = slice(half * BANK, (half + 1) * BANK)
                        dve.wait_ge(ple_gated, 4 * layer + 2 * t + half + 1)
                        link(dve.tensor_tensor(rows[:, t, c], rows[:, t, c], ps[:, 2 * t + half, :], ALU.mult))
                        ins = dve.tensor_tensor(resid[:, t, c], resid[:, t, c], rows[:, t, c], ALU.add)
                        if (t, half) == (1, 1):
                            ins.then_inc(resid_ready, 1)
                            dve.wait_ge(resid_ready, n)
                        else:
                            link(ins)

            norm(2, gain(2))
            ple(0, 3)
            norm(3, gain(3))
            for t in range(QB):
                dve.wait_ge(gelu_done, 4 + 2 * t + 2)
                for half in range(2):
                    ins = dve.bn_stats(bn[:, t, half, :], v_rows[:, t, half * BANK:(half + 1) * BANK])
                link(ins)
                link(dve.bn_aggr(mv[:, t, :], bn[:, t].rearrange("p a b -> p (a b)")))
                link(dve.tensor_copy(stat[:, 8 + t:9 + t], mv[:, t, 1:2]))
            root(stat[:, 8:10], 2, 1.0, LN_EPS)
            dve.wait_ge(ln_in, 16 * 3)
            for t in range(QB):
                link(dve.tensor_scalar(v_rows[:, t, :], v_rows[:, t, :], mv[:, t, 0:1], stat[:, t:t + 1],
                                       ALU.subtract, ALU.mult))
                link(dve.tensor_tensor(v_rows[:, t, :], v_rows[:, t, :], ln_g, ALU.mult))
                dve.tensor_tensor(v_rows[:, t, :], v_rows[:, t, :], ln_b, ALU.add).then_inc(vn_ready, 1)
            for t in range(QB):
                for half in range(2):
                    dve.wait_ge(spatial_ready, 2 * t + half + 1)
                    for i in range(4):
                        g = 4 * half + i
                        ins = dve.scalar_tensor_tensor(out=rows[:, t, g * P:(g + 1) * P],
                                                       in0=ps[:, 2 * t + half, i * P:(i + 1) * P],
                                                       scalar=col("bs", g, 1), in1=u_rows[:, t, g * P:(g + 1) * P],
                                                       op0=ALU.add, op1=ALU.mult)
            ins.then_inc(heads_ready, 1)
            dve.wait_ge(slot_done, W_COUT + 4)
            add_branch()
            dve.wait_ge(resid_ready, 4)
            norm(4, gain(4))
            dve.wait_ge(logits_ready, 1)
            link(dve.tensor_copy(logit[:, :, :].rearrange("p b e -> p (b e)"), ps[:, 0, 0:16]))
            for t in range(QB):
                link(dve.max(top[:, t, :], logit[:, t, :]))
                link(dve.max_index(topi[:, t, :], top[:, t, :], logit[:, t, :]))
                link(dve.tensor_copy(route[:, t, 0, :], topi[:, t, :]))
                ins = dve.tensor_tensor(route[:, t, 1, 0:1], top[:, t, 1:2], top[:, t, 0:1], ALU.subtract)
                if t == 0:
                    link(ins)
            ins.then_inc(route_asked, 1)
            dve.wait_ge(route_exp, 2)
            for t in range(QB):
                e = route[:, t, 1, 1:2]
                link(dve.tensor_scalar(route[:, t, 1, 2:3], e, 1.0, None, ALU.add))
                link(dve.reciprocal(route[:, t, 1, 3:4], route[:, t, 1, 2:3]))
                link(dve.tensor_tensor(route[:, t, 1, 4:5], e, route[:, t, 1, 3:4], ALU.mult))
                for n in range(2):
                    link(dve.tensor_scalar(route[:, t, 2 + n, :], col("iota"), route[:, t, 0, n:n + 1],
                                           None, ALU.is_equal))
                ins = dve.tensor_tensor(member[:, t, :], route[:, t, 2, :], route[:, t, 3, :], ALU.add)
                link(ins)
                for n in range(2):
                    link(dve.tensor_scalar(route[:, t, 2 + n, :], route[:, t, 2 + n, :], route[:, t, 1, 3 + n:4 + n],
                                           None, ALU.mult))
                link(dve.tensor_tensor(route[:, t, 2, :], route[:, t, 2, :], route[:, t, 3, :], ALU.add))
            dve.memset(most[:, 0:1], 0.0).then_inc(member_ready, 1)
            dve.wait_ge(ranks_ready, 1)
            link(dve.tensor_copy(place[:, :, :].rearrange("p b e -> p (b e)"), ps[:, 1, 0:16]))
            link(dve.tensor_reduce(most[:, 0:1], ps[:, 1, 16:24], AX.X, ALU.max))
            link(dve.tensor_copy(most_i[:, :], most[:, 0:1]))
            link(dve.tensor_scalar(member[:, :, :], member[:, :, :], -1000.0, 1000.0, ALU.mult, ALU.add))
            dve.tensor_tensor(place[:, :, :], place[:, :, :], member[:, :, :], ALU.add).then_inc(routed, 1)
            dve.wait_ge(routed, 1)

            def experts(w):
                with dve.Fori(0, NE) as e:
                    rank = col("slot", w.chunk * P, P)
                    for t in range(QB):
                        pl = place[:, t, bass.ds(e, 1)]
                        dve.tensor_scalar(sel[:, t, :], rank, pl, None, ALU.is_equal)
                        ins = dve.tensor_scalar(selg[:, t, :], rank, pl, route[:, t, 2, bass.ds(e, 1)],
                                                ALU.is_equal, ALU.mult)
                    ins.then_inc(w.sel_ready, 1)
                    for half in range(2):
                        dve.wait_ge(w.gather_ready, e * 2 + (half + 1))
                        dve.tensor_tensor(xT[:, 4 * half:4 * half + 4, 0:P],
                                          ps[:, 6 + half, :].rearrange("p (f c) -> p f c", f=4),
                                          bc(gain(4)[:, 4 * half:4 * half + 4], P), ALU.mult).then_inc(w.gathered, 1)
                    for j in range(J1):
                        dve.wait_ge(w.act_ready, e * J1 + (j + 1))
                        dve.tensor_tensor(hid_rows[:, j % 2, :], act_rows[:, j % 2, :], ps[:, j % 2, 256:512], ALU.mult)\
                            .then_inc(w.hid_ready, 1)
                    for t in range(QB):
                        dve.wait_ge(w.scattered, e * 2 + (t + 1))
                        ins = dve.tensor_tensor(resid[:, t, :], resid[:, t, :], bank((6, 0)[t], 2), ALU.add)
                    ins.then_inc(w.merged, 1)
                    dve.wait_ge(w.merged, e + 1)

            experts(first_pass)
            with dve.If(overflowing(dve)):
                experts(second_pass)
            dve.memset(most[:, 1:2], 0.0).then_inc(resid_ready, 1)
            dve.wait_ge(resid_ready, 5)
            norm(5, gain(5))
            ple(1, 6)
            norm_rows()
            dve.wait_ge(rows_scaled, 14)
            dve.wait_ge(fin_in, 16)
            for t in range(QB):
                ins = dve.tensor_tensor(resid[:, t, :], rows[:, t, :], ln_g, ALU.mult)
                if t == 0:
                    link(ins)
            ins.then_inc(resid_ready, 1)
            dve.wait_ge(resid_ready, 7)
            for l in range(2):
                n0 = W_BLK + l * B_ALL
                dve.wait_ge(slot_done, n0 + B_ADAR)
                link(dve.tensor_tensor(ada[:, :], ps[:, 0, 0:32], col("bada", 32 * l, 32), ALU.add))
                for i in range(2):
                    ins = dve.scalar_tensor_tensor(out=modg[:, i, :], in0=ada[:, 16 * i + 8:16 * i + 16], scalar=1.0,
                                                   in1=gain(6 + 2 * l + i), op0=ALU.add, op1=ALU.mult)
                link(ins)
                dve.wait_ge(slot_done, n0 + B_IN)
                dve.wait_ge(bada_in, 16 * (l + 1))
                ins = dve.tensor_tensor(grow[:, :, :].rearrange("p a n -> p (a n)"),
                                        grow[:, :, :].rearrange("p a n -> p (a n)"), bank(4, 4), ALU.add)
                ins.then_inc(grow_ready, 1)
                norm(6 + 2 * l, modg[:, 0, :], ada[:, 0:8])
                dve.wait_ge(projT_kept, 10 + 9 * l + 9)
                dve.tensor_tensor(flat0[:, 0:3 * S], arena[:, T_CKV * S:(T_CKV + 3) * S],
                                  arena[:, T_CKV * S:(T_CKV + 3) * S], ALU.mult).then_inc(squares_ready, 1)
                for which in range(2):
                    for par in range(2):
                        z = zT[64 * par:64 * par + 64, T_KC + which, :].rearrange("p (n l) -> p l n", l=16)
                        for hi in range(2):
                            ins = dve.tensor_tensor(
                                blk[64 * par:64 * par + 64, which, 8 * hi:8 * hi + 8, :],
                                z[:, par:16:2, hi:hi + NCMP],
                                bc(col("pos", 32 * l + 16 * which + 8 * hi, 8)[64 * par:64 * par + 64], NCMP), ALU.add)
                ins.then_inc(cmpblk_ready, 1)
                dve.wait_ge(latsum_ready, l + 1)
                lat = flat0[:, 0:2 * S]
                dve.wait_ge(cmpblk_ready, l + 1)
                link(dve.tensor_scalar(lat[:, 0:S], ps[:, 0, 0:S], 1.0 / 128, RMS_EPS, ALU.mult, ALU.add))
                dve.tensor_scalar(lat[:, S:2 * S], ps[:, 0, S:2 * S], 1.0 / 192, RMS_EPS, ALU.mult, ALU.add)\
                    .then_inc(latms_ready, 1)
                dve.wait_ge(latroot_ready, l + 1)
                link(dve.reciprocal(flat0[:, 2 * S:4 * S], lat))
                for t, r, g in ((T_CKV, 2, 0), (T_CQ, 3, 1), (T_CQ + 1, 3, 2)):
                    ins = dve.scalar_tensor_tensor(out=zT[:, t, :], in0=zT[:, t, :], scalar=col("mlag", 3 * l + g, 1),
                                                   in1=flat0[:, r * S:(r + 1) * S], op0=ALU.mult, op1=ALU.mult)
                ins.then_inc(latent_ready, 1)
                dve.wait_ge(mlarot_ready, l + 1)
                cm, sm = col("cosm"), col("sinm")
                tmp = flat0[:, 0:4 * S].rearrange("p (h s) -> p h s", h=4)
                link(dve.tensor_tensor(tmp, bank(2, 2).rearrange("p (h s) -> p h s", h=4), rep(sm, 4), ALU.mult))
                link(dve.tensor_tensor(qm, qm, rep(cm, 4), ALU.mult))
                link(dve.tensor_tensor(qm, qm, tmp, ALU.add))
                kpe = zT[:, T_KPE, :]
                link(dve.tensor_tensor(flat0[:, 0:S], ps[:, 1, 0:S], sm, ALU.mult))
                link(dve.tensor_tensor(kpe, kpe, cm, ALU.mult))
                link(dve.tensor_tensor(kpe, kpe, flat0[:, 0:S], ALU.add))
                dve.tensor_copy(km[64:128, :, :], rep(kpe[64:128], 4)).then_inc(mla_ready, 1)
                attention(l)
                dve.wait_ge(slot_done, n0 + B_OUT + 4)
                add_branch(grow[:, 0, :])
                dve.wait_ge(resid_ready, 8 + 2 * l)
                norm(7 + 2 * l, modg[:, 1, :], ada[:, 16:24])
                base = J1 + l * J2
                for j in range(J2):
                    hidden(j, lambda j: base + j + 1, False)
                dve.wait_ge(slot_done, n0 + B_ALL)
                add_branch(grow[:, 1, :])
                dve.wait_ge(resid_ready, 9 + 2 * l)
            norm_rows()
            dve.wait_ge(rows_scaled, 24)
            dve.wait_ge(fin_in, 32)
            fin = catT[:, 0:4, :].rearrange("p a s -> p (a s)")
            for t in range(QB):
                ins = dve.tensor_tensor(rows[:, t, :], rows[:, t, :], fin, ALU.mult)
                if t == 0:
                    link(ins)
            ins.then_inc(resid_ready, 1)

        @block.scalar
        def _(act):
            steps = [0]

            def link(ins):
                steps[0] += 1
                ins.then_inc(act_step, 1)
                act.wait_ge(act_step, steps[0])

            act.dma_start(con[:, :], consts).then_inc(consts_in, 16)
            act.dma_start(resid[:, :, :], x_in.rearrange("(b p) n -> p b n", p=P)).then_inc(consts_in, 16)
            act.dma_start(posi[:, :], pos.partition_broadcast(P)).then_inc(consts_in, 16)
            act.dma_start(lamv[:, :], lam_in.partition_broadcast(P)).then_inc(consts_in, 16)
            for l in range(2):
                act.dma_start(sink[:, l, :], sinks[l].partition_broadcast(P)).then_inc(consts_in, 16)
            act.dma_start(grow[:, :, :].rearrange("p a n -> p (a n)"), bada_rows[0].partition_broadcast(P))\
                .then_inc(bada_in, 16)
            act.wait_ge(consts_in, 16 * 6)
            act.activation(csilu[:, :], col("c"), ACT.Silu).then_inc(csilu_ready, 1)
            act.wait_ge(angles_ready, 1)
            act.activation(sin0, ang, ACT.Sin).then_inc(sines_ready, 1)
            act.activation(cos0, turns, ACT.Sin).then_inc(sines_ready, 1)
            act.wait_ge(lam_asked, 1)
            act.activation(lam[:, 2:4], lam[:, 0:2], ACT.Exp).then_inc(lam_exp, 1)

            def keep_tiles(dst, count, n0):
                for s in range(count):
                    act.wait_ge(slot_done, n0 + s + 1)
                    act.activation(dst[:, 2 * s:2 * s + 2, :].rearrange("p a s -> p (a s)"),
                                   ps[:, s % 4, :], ACT.Copy).then_inc(projT_kept, 1)

            def attention(layer):
                groups = attention_groups(layer)
                base = GROUP_BASE[0 if layer is None else layer + 1]

                def exps(i):
                    kind, qb, hg = groups[i]
                    g = base + i
                    kw = NCMP if kind == "nsac" else P * (qb + 1) + (kind == "swa")
                    sc = score[:, g % 2, :, 0:kw]
                    act.wait_ge(shifted, g + 1)
                    act.activation(sc, sc, ACT.Exp, scale=96.0 ** -0.5 if kind == "mla" else 0.125)\
                        .then_inc(exp_ready, 1)

                def keep(i):
                    kind, qb, hg = groups[i]
                    g = base + i
                    nkb = 1 if kind == "nsac" else qb + 1
                    kp = NCMP if kind == "nsac" else P
                    act.wait_ge(probT_ready, g + 1)
                    if i >= 2:
                        act.wait_ge(mixed_ready, g - 1)
                    act.activation(probT[0:kp, g % 2, 0:4 * nkb, :].rearrange("p a b -> p (a b)"),
                                   bank(4, 2)[0:kp, 0:4 * nkb * P], ACT.Copy).then_inc(probT_kept, 1)

                exps(0)
                for i in range(len(groups)):
                    keep(i)
                    if i + 1 < len(groups):
                        exps(i + 1)

            def keep_cat(count, before, gain=None):
                for n in range(count):
                    act.wait_ge(catT_ready, before + n + 1)
                    t, half = (n, 0) if count == 2 else (n // 2, n % 2)
                    act.activation(catT[:, 4 * half:4 * half + 4, t * P:(t + 1) * P],
                                   ps[:, 4 + 2 * t + half, :].rearrange("p (f s) -> p f s", f=4),
                                   ACT.Copy, scale=1.0 if gain is None else gain).then_inc(catT_kept, 1)

            def activations(j, done, func, paired):
                act.wait_ge(slot_done, done)
                act.activation(acth[:, j % 2, :], ps[:, (2 if paired else 1) * (j % 2), :], func)\
                    .then_inc(act_ready, 1)

            keep_tiles(zqk, 4, W_QK)
            keep_tiles(zbch, 6, W_BCH)
            act.wait_ge(slot_done, W_V + 2)
            act.activation(v1.rearrange("p b n -> p (b n)"), bank(4, 2), ACT.Copy).then_inc(vrows_kept, 1)
            attention(None)
            keep_cat(2, 0, sub8[:, 0:1])
            for j in range(J1):
                activations(j, W_FFN0 + swiglu_up(j) + 1, ACT.Silu, True)
            act.wait_ge(slot_done, W_OUT0)
            act.dma_start(ln_g, ln_rows[0].partition_broadcast(P)).then_inc(ln_in, 16)
            act.dma_start(ln_b, ln_rows[1].partition_broadcast(P)).then_inc(ln_in, 16)
            act.dma_start(ws, w_s).then_inc(ln_in, 16)

            def ple(layer):
                act.wait_ge(slot_done, (W_PLE0, W_PLE1)[layer] + 5)
                for b in range(4):
                    act.activation(rows[:, b // 2, (b % 2) * BANK:(b % 2 + 1) * BANK], ps[:, 4 + b, :], ACT.Sigmoid)\
                        .then_inc(ple_gated, 1)

            ple(0)
            for part, dst in enumerate((u_rows, v_rows)):
                act.wait_ge(slot_done, W_CIN + 4 * part + 4)
                for b in range(4):
                    act.activation(dst[:, b // 2, (b % 2) * BANK:(b % 2 + 1) * BANK], ps[:, 4 * part + b, :], ACT.Gelu)\
                        .then_inc(gelu_done, 1)
            keep_cat(4, 2)
            act.wait_ge(route_asked, 1)
            for t in range(QB):
                act.activation(route[:, t, 1, 1:2], route[:, t, 1, 0:1], ACT.Exp).then_inc(route_exp, 1)

            def experts(w):
                with act.Fori(0, NE) as e:
                    act.wait_ge(w.selT_ready, e + 1)
                    act.activation(selT.rearrange("p b s -> p (b s)"), ps[:, 3, 0:256], ACT.Copy)\
                        .then_inc(w.selT_kept, 1)

                    def keep_hidT(j):
                        act.wait_ge(w.hidT_ready, e * J1 + (j + 1))
                        act.activation(hidE[:, j % 2].rearrange("p k c -> p (k c)"),
                                       ps[:, 2, 256 * (j % 2):256 * (j % 2) + 256], ACT.Copy).then_inc(w.hidT_kept, 1)

                    for j in range(J1):
                        act.wait_ge(w.done, e * (3 * J1) + (w.first + swiglu_up(j) + 1))
                        act.activation(act_rows[:, j % 2, :], ps[:, j % 2, 0:256], ACT.Silu).then_inc(w.act_ready, 1)
                        if j >= 1:
                            keep_hidT(j - 1)
                    keep_hidT(J1 - 1)
                    act.wait_ge(w.done, e * (3 * J1) + (w.first + 3 * J1))
                    for half in range(2):
                        act.activation(y_rows[:, half * BANK:(half + 1) * BANK], ps[:, 4 + half, :], ACT.Copy)\
                            .then_inc(w.y_kept, 1)

            experts(first_pass)
            with act.If(overflowing(act)):
                experts(second_pass)
            act.wait_ge(resid_ready, 5)
            act.dma_start(ln_g, fin_row[0].partition_broadcast(P)).then_inc(fin_in, 16)
            ple(1)
            for l in range(2):
                if l == 1:
                    act.wait_ge(resid_ready, 9)
                    act.dma_start(grow[:, :, :].rearrange("p a n -> p (a n)"), bada_rows[1].partition_broadcast(P))\
                        .then_inc(bada_in, 16)
                n0 = W_BLK + l * B_ALL
                keep_tiles(zT, 9, n0 + B_IN)
                act.wait_ge(slot_done, n0 + B_CMP)
                act.activation(v2.rearrange("p b n -> p (b n)"), bank(4, 2), ACT.Copy).then_inc(vrows_kept, 1)
                act.wait_ge(latms_ready, l + 1)
                act.activation(flat0[:, 0:2 * S], flat0[:, 0:2 * S], ACT.Sqrt).then_inc(latroot_ready, 1)
                act.wait_ge(gateT_ready, l + 1)
                act.activation(gates[:, :, 0:12], ps[:, 1, 0:2 * P].rearrange("p (b n) -> p b n", b=2)[:, :, 0:12],
                               ACT.Sigmoid).then_inc(gates_ready, 1)
                act.wait_ge(mlaheads_ready, l + 1)
                link(act.activation(qm.rearrange("p h s -> p (h s)"), bank(2, 2), ACT.Copy))
                link(act.activation(km[0:64].rearrange("p h s -> p (h s)"), bank(4, 2)[0:64], ACT.Copy))
                act.activation(vm.rearrange("p b n -> p (b n)"), bank(6), ACT.Copy).then_inc(mlaheads_kept, 1)
                act.wait_ge(slot_done, n0 + B_SMALL)
                act.activation(hidc[:, :, 0:NCMP], ps[:, 7, 0:32].rearrange("p (v n) -> p v n", v=2)[:, :, 0:NCMP],
                               ACT.Gelu_apprx_tanh).then_inc(cmpact_ready, 1)
                act.wait_ge(slot_done, n0 + B_OUT)
                link(act.activation(kcmp[:, 0:NCMP], ps[:, 7, 32:32 + NCMP], ACT.Copy))
                act.activation(vcmp[0:NCMP, :], ps[0:NCMP, 7, 64:128], ACT.Copy).then_inc(cmp_kept, 1)
                attention(l)
                keep_cat(4, 6 + 4 * l)
                for j in range(J2):
                    activations(j, n0 + B_MLP + mlp_up(j) + 1, ACT.Relu, False)
            act.wait_ge(slot_done, SLOTS)
            act.dma_start(catT[:, 0:4, :].rearrange("p a s -> p (a s)"), fin_row[1].partition_broadcast(P))\
                .then_inc(fin_in, 16)

        @block.gpsimd
        def _(pool):
            pool.memset(neghalf[:, :], -0.5).then_inc(pool_step, 1)
            pool.wait_ge(pool_step, 1)
            widths = [2, 8] + [2] * 12
            for n, w in enumerate(widths):
                if n == 5:
                    pool.wait_ge(ln_in, 16 * 3)
                    pool.affine_select(out=ws, in_=ws, pattern=[[0, 8], [1, P]], compare_op=ALU.is_ge, fill=0.0,
                                       base=0, channel_multiplier=-1).then_inc(ws_masked, 1)
                pool.wait_ge(root_asked, n + 1)
                pool.tensor_tensor(stat[:, 0:w], stat[:, 0:w], neghalf[:, 0:w], ALU.pow).then_inc(root_ready, 1)


def row_tiles(w, k):
    n = w.shape[-1]
    return np.ascontiguousarray(w.reshape(k, P, n).transpose(1, 0, 2)).reshape(P, k * n)


def column_slots(w):
    return [row_tiles(w[:, j:j + 256], KT) for j in range(0, w.shape[1], 256)]


def row_slots(w):
    return [row_tiles(w[j:j + 256], 2) for j in range(0, w.shape[0], 256)]


def swiglu_slots(w1, w3, w2):
    a, b, c = column_slots(w1), column_slots(w3), row_slots(w2)
    out = []
    for j in range(J1 + 1):
        if j < J1:
            out += [a[j], b[j]]
        if j >= 1:
            out.append(c[j - 1])
    return out


def lay_out(i):
    f = np.float32
    slots = []
    w = np.asarray(i["a_w_in"])[0]
    slots += column_slots(w[:, 0:1024]) + column_slots(w[:, 1536:3072])
    wv = w[:, 1024:1536]
    slots += [row_tiles(wv[0:512], 4), row_tiles(wv[512:1024], 4)]
    slots += row_slots(np.asarray(i["a_w_out"])[0])
    slots += swiglu_slots(*(np.asarray(i[n])[0] for n in ("ffn_w1", "ffn_w3", "ffn_w2")))
    pg, pp = np.asarray(i["ple_gate"]), np.asarray(i["ple_proj"])
    slots += row_slots(pg[0]) + row_slots(pp[0])
    w = np.asarray(i["c_w_in"])[0]
    slots += row_slots(w[:, 0:1024]) + row_slots(w[:, 1024:2048])
    slots += row_slots(np.asarray(i["c_w_out"])[0])
    m1, m3, m2 = (np.asarray(i[n])[0] for n in ("moe_w1", "moe_w3", "moe_w2"))
    for e in range(NE):
        slots += swiglu_slots(m1[e], m3[e], m2[e])
    slots += row_slots(pg[1]) + row_slots(pp[1])
    for l in range(2):
        w = np.asarray(i["w_ada_2"])[l]
        sh1, sc1, g1, sh2, sc2, g2 = (w[:, n * D:(n + 1) * D] for n in range(6))
        for part in (sh1, sc1, sh2, sc2):
            slots += column_slots(part)
        slots += row_slots(g1) + row_slots(g2)
        w = np.asarray(i["w_in_2"])[l]
        z = {}
        at = 0
        for name, n in (("swaq", 256), ("swak", 128), ("swav", 128), ("cq", 192), ("ckv", 128), ("kpe", 32),
                        ("nsaq", 256), ("kc", 64), ("vc", 64), ("ks", 64), ("vs", 64), ("kw", 64), ("vw", 64),
                        ("gl", 12), ("mobq", 256), ("mobk", 256), ("mobv", 256)):
            z[name] = w[:, at:at + n]
            at += n

        def pad(n):
            return np.zeros((D, n), f)

        sq = z["swaq"]
        cols = [sq[:, 0:64], sq[:, 128:192], sq[:, 64:128], sq[:, 192:256], z["swak"], z["ckv"], z["cq"], pad(64),
                pad(64), z["kpe"], pad(32), z["gl"], pad(116), z["nsaq"]]
        for name in ("kc", "vc", "ks", "kw"):
            cols += [z[name], z[name]]
        cols += [z["mobq"], z["mobk"]]
        slots += column_slots(np.concatenate(cols, 1))
        wv = np.concatenate([z["swav"], z["vs"], z["vw"], z["mobv"]], 1)
        slots += [row_tiles(wv[0:512], 4), row_tiles(wv[512:1024], 4)]
        for n in ("nsa_cmp_k_w1_2", "nsa_cmp_v_w1_2"):
            slots.append(row_tiles(np.asarray(i[n])[l], 16))
        uq = np.asarray(i["mla_w_uq_2"])[l].reshape(192, 4, 96)
        uqp = np.zeros((256, 4, 128), f)
        uqp[0:192, :, 0:96] = uq
        ukv = np.asarray(i["mla_w_ukv_2"])[l].reshape(128, 4, 128)
        ck2, cv2 = np.asarray(i["nsa_cmp_k_w2_2"])[l], np.asarray(i["nsa_cmp_v_w2_2"])[l]
        small = np.zeros((P, SLOT), f)
        small[:, 0:1024] = row_tiles(uqp.reshape(256, 512), 2)
        small[:, 1024:1280] = ukv[:, :, 0:64].reshape(128, 256)
        small[:, 1280:1536] = ukv[:, :, 64:128].reshape(128, 256)
        small[:, 1536:1600] = ck2
        small[:, 1600:1664] = ck2
        small[:, 1664:1728] = cv2
        slots.append(small)
        slots += row_slots(np.asarray(i["w_out_2"])[l])
        a, b = column_slots(np.asarray(i["w_up_2"])[l]), row_slots(np.asarray(i["w_down_2"])[l])
        for j in range(J2 + 1):
            if j < J2:
                slots.append(a[j])
            if j >= 1:
                slots.append(b[j - 1])
    assert len(slots) == SLOTS, (len(slots), SLOTS)
    stream = np.stack(slots)
    del slots

    def colvec(v):
        return np.asarray(v).reshape(-1, P).T

    con = {}
    lm, lf, lp = (np.asarray(i[n]) for n in ("ln_mix", "ln_ffn", "ln_ple"))
    nm, nl = np.asarray(i["norm_mix_g_2"]), np.asarray(i["norm_mlp_g_2"])
    con["gain"] = np.concatenate([colvec(v) for v in (lm[0], lf[0], lp[0], lm[1], lf[1], lp[1], nm[0], nl[0],
                                                      nm[1], nl[1])], 1)
    con["subln"] = colvec(np.asarray(i["a_subln"])[0])
    con["conv"] = np.asarray(i["a_conv_w"])[0].reshape(4, P, 3).transpose(1, 0, 2).reshape(P, 12)
    half = 8
    inv = np.float32(500000.0) ** (-np.arange(0, 16, 2, dtype=f) / np.float32(16))
    invf = np.zeros((2, 64), f)
    invf[:, 0:half] = inv
    invf[:, half:2 * half] = inv
    con["invf"] = invf.reshape(P, 1)
    con["bs"] = np.asarray(i["c_b_s"])[0].T
    con["router"] = row_tiles(np.asarray(i["router_w"])[0], KT)
    con["iota"] = np.tile(np.arange(8, dtype=f), (P, 1))
    con["c"] = colvec(np.asarray(i["c_2"])[0])
    ba = np.asarray(i["b_ada_2"])
    con["bada"] = np.concatenate([colvec(ba[l, n * D:(n + 1) * D]) for l in range(2) for n in (0, 1, 3, 4)], 1)
    qg, kg = np.asarray(i["mla_q_norm_g_2"]), np.asarray(i["mla_kv_norm_g_2"])
    mlag = np.zeros((P, 6), f)
    for l in range(2):
        mlag[:, 3 * l] = kg[l]
        mlag[:, 3 * l + 1] = qg[l, 0:128]
        mlag[0:64, 3 * l + 2] = qg[l, 128:192]
    con["mlag"] = mlag
    con["pos"] = np.concatenate([np.asarray(i[n])[l].reshape(16, P).T for l in range(2)
                                 for n in ("nsa_cmp_pos_k_2", "nsa_cmp_pos_v_2")], 1)
    t = np.arange(S)
    cend = np.arange(NCMP) * 16 + 31
    dc = (t[:, None] - cend[None, :]).astype(f)
    con["nsac"] = np.where(dc >= 0, -dc, f(NEG)).reshape(2, P, NCMP).transpose(1, 0, 2).reshape(P, -1)
    con["ident"] = np.eye(P, dtype=f)
    con["before"] = np.triu(np.ones((P, P), f), 1)
    con["slot"] = np.tile(np.arange(2 * P, dtype=f), (P, 1))
    rot0, rotm = np.zeros((P, P), f), np.zeros((P, P), f)
    for h in range(2):
        for d in range(half):
            rot0[64 * h + d + half, 64 * h + d] = -1
            rot0[64 * h + d, 64 * h + d + half] = 1
    for d in range(16):
        rotm[64 + d + 16, 64 + d] = -1
        rotm[64 + d, 64 + d + 16] = 1
    con["rot0"], con["rotm"] = rot0, rotm
    fr = np.float32(10000.0) ** (-np.arange(16, dtype=f) / np.float32(16))
    ang = (t.astype(f)[:, None] * fr[None, :]).astype(np.float64)
    cosm, sinm = np.ones((P, S), f), np.zeros((P, S), f)
    for r in (64, 80):
        cosm[r:r + 16] = np.cos(ang).T
        sinm[r:r + 16] = np.sin(ang).T
    con["cosm"], con["sinm"] = cosm, sinm
    dist = (t[:, None] - t[None, :]).astype(f)

    def by_block(m):
        return m.astype(f).reshape(2, P, S).transpose(1, 0, 2).reshape(P, 2 * S)

    con["alibi"] = by_block(np.where(dist >= 0, -dist, f(NEG)))
    con["causal"] = by_block(np.where(dist >= 0, f(0), f(NEG)))
    con["window"] = by_block(np.where((dist >= 0) & (dist < 128), -dist, f(NEG)))
    p = np.asarray(i["p"])
    con["ple"] = np.concatenate([row_tiles(np.ascontiguousarray(p[l, 0].T), 2) for l in range(2)], 1)
    consts = np.concatenate([con[n] for n in COLS], 1)
    assert consts.shape == (P, NCOLS), consts.shape
    return {
        "stream": stream,
        "x": np.ascontiguousarray(np.asarray(i["x"])[0]),
        "consts": np.ascontiguousarray(consts.astype(f, copy=False)),
        "pos": np.ascontiguousarray(np.asarray(i["positions"])[0]),
        "lam": np.ascontiguousarray(np.asarray(i["a_lambda"])[0].reshape(-1)),
        "ln_rows": np.stack([np.asarray(i["c_ln_g"])[0], np.asarray(i["c_ln_b"])[0]]),
        "w_s": np.ascontiguousarray(np.asarray(i["c_w_s"])[0].transpose(2, 0, 1)),
        "sinks": np.ascontiguousarray(np.asarray(i["swa_sinks_2"])),
        "bada_rows": np.ascontiguousarray(np.concatenate([ba[:, 2 * D:3 * D], ba[:, 5 * D:6 * D]], 1)),
        "fin_row": np.stack([np.asarray(i["final_norm"]), np.asarray(i["final_norm_g_2"])]),
    }


def kernel(**inputs):
    import concourse.bacc as bacc
    from concourse.bass_utils import run_bass_kernel_spmd

    nc = bacc.Bacc("TRN2", target_bir_lowering=False, num_devices=1)
    arrays = lay_out(inputs)
    aps = {n: nc.dram_tensor(f"in_{n}", a.shape, mybir.dt.from_np(a.dtype), kind="ExternalInput").ap()
           for n, a in arrays.items()}
    out = nc.dram_tensor("out", (S, D), F32, kind="ExternalOutput").ap()
    build(nc, aps, out)
    r = run_bass_kernel_spmd(nc, [{f"in_{n}": a for n, a in arrays.items()}], core_ids=[0])
    return r.results[0]["out"].reshape(1, S, D)
```

```python
import math
from contextlib import ExitStack

import numpy as np
import concourse.bass as bass
from concourse import mybir

F32 = mybir.dt.float32
F32R = mybir.dt.float32r
I32 = mybir.dt.int32
U32 = mybir.dt.uint32
ALU = mybir.AluOpType
ACT = mybir.ActivationFunctionType
AX = mybir.AxisListType

P = 128
D = 1024
S = 256
KT = D // P
QB = S // P
BANK = 512
SLOT = 2048
HALF = SLOT // 2
RING = 6
PAIRS = 3
F1 = 2816
NE = 8
J1 = F1 // 256
F2 = 4 * D
J2 = F2 // 256
NCMP = S // 16 - 1
RMS_EPS = 1e-6
LN_EPS = 1e-5
NEG = -1e30
GUARD = -1e20
TINY = 1e-30
LAMBDA_INIT = 0.8 - 0.6 * math.exp(-0.3 * 0)
SLOPES = [float(np.float32(2.0 ** (-8.0 * (i + 1) / 12))) for i in range(12)]
NT = 18
(T_SWAQ, T_SWAK, T_CKV, T_CQ, T_KPE, T_GATE, T_NSAQ, T_KC, T_VC, T_KS, T_KW, T_MOBQ,
 T_MOBK) = (0, 2, 3, 4, 6, 7, 8, 10, 11, 12, 13, 14, 16)

W_QK = 0
W_BCH = W_QK + 4
W_V = W_BCH + 6
W_OUT0 = W_V + 2
W_FFN0 = W_OUT0 + 4
W_PLE0 = W_FFN0 + 3 * J1
W_CIN = W_PLE0 + 5
W_COUT = W_CIN + 8
W_MOE = W_COUT + 4
W_PLE1 = W_MOE + 3 * J1 * NE
W_BLK = W_PLE1 + 5
B_ADA, B_IN, B_V, B_SMALL, B_CMP, B_OUT, B_MLP = 0, 24, 33, 35, 36, 38, 42
B_ALL = B_MLP + 2 * J2
SLOTS = W_BLK + 2 * B_ALL

LATENT_SLOTS = 6

COLS = {}
_at = 0
for _n, _w in [("gain", 80), ("subln", 1), ("conv", 12), ("invf", 1), ("bs", 8), ("router", 64),
               ("iota", 8), ("c", 8), ("bada", 64), ("mlag", 6), ("pos", 64), ("nsac", 2 * NCMP), ("ident", P),
               ("cmpw2", 2 * 192), ("before", P), ("slot", 2 * P), ("rot0", P), ("rotm", P), ("cosm", S), ("sinm", S),
               ("alibi", 2 * S), ("causal", 2 * S), ("window", 2 * S), ("ple", 4 * S)]:
    COLS[_n] = (_at, _at + _w)
    _at += _w
NCOLS = _at
FIRST_COLS = COLS["cmpw2"][0]

NORMS = ["mix0", "ffn0", "ple0", "mix1", "ffn1", "ple1", "b0mix", "b0mlp", "b1mix", "b1mlp"]


def attention_groups(block_layer):
    if block_layer is None:
        return [("diff", qb, hg) for qb in range(QB) for hg in range(2)]
    return [(kind, qb, 0) for qb in range(QB) for kind in ("swa", "moba", "nsac", "nsas", "nsaw", "mla")]


def head_of(kind, u):
    return 2 * (u % 2) + u // 2 if kind in ("moba", "nsac", "nsas", "nsaw") else u


GROUP_BASE = [0, 4, 16]


def swiglu_up(j):
    return 3 * j if j else 1


def mlp_up(j):
    return 2 * j - 1 if j else 0


def build(nc, a, out):
    stream, consts, pos, lam_in, ln_rows, w_s, sinks, bada_rows, fin_row, x_in = (
        a[n] for n in ("stream", "consts", "pos", "lam", "ln_rows", "w_s", "sinks", "bada_rows", "fin_row", "x"))
    with ExitStack() as ctx:
        def sb(name, shape, dt=F32):
            return ctx.enter_context(nc.sbuf_tensor(name, shape, dt))

        def sem(name):
            return ctx.enter_context(nc.semaphore(name))

        ps = ctx.enter_context(nc.psum_tensor("ps", [P, 8, BANK], F32))
        ring = sb("ring", [P, RING, SLOT])
        w_hi = sb("w_hi", [P, PAIRS, HALF], F32R)
        w_lo = sb("w_lo", [P, PAIRS, HALF], F32R)
        x_hi = sb("x_hi", [P, KT, S], F32R)
        x_lo = sb("x_lo", [P, KT, S], F32R)
        h_hi = sb("h_hi", [P, 2, BANK], F32R)
        h_lo = sb("h_lo", [P, 2, BANK], F32R)
        resid = sb("resid", [P, QB, D])
        xT = sb("xT", [P, KT, S])
        rows = sb("rows", [P, QB, D])
        ff = sb("ff", [P, 3, BANK])
        arena = sb("arena", [P, 8192])
        score = sb("score", [P, 2, 4, S + 1])
        grow = sb("grow", [P, 2, D])
        con = sb("con", [P, NCOLS])
        ones = sb("ones", [P, P])
        stat = sb("stat", [P, 16])
        neghalf = sb("neghalf", [P, 8])
        soft = sb("soft", [P, 4, 4, 4])
        csilu = sb("csilu", [P, KT])
        ada = sb("ada", [P, 32])
        modg = sb("modg", [P, 2, 8])
        lam = sb("lam", [P, 8])
        lamv = sb("lamv", [P, 4 * 64])
        sink = sb("sink", [P, 2, 4])
        sub8 = sb("sub8", [P, 1])
        bn = sb("bn", [P, 2, 2, 6])
        mv = sb("mv", [P, 2, 2])
        posi = sb("posi", [P, S], I32)
        gates = sb("gates", [P, QB, 16])
        top = sb("top", [P, QB, 8])
        topi = sb("topi", [P, QB, 8], U32)
        route = sb("route", [P, QB, 4, 8])
        logit = sb("logit", [P, QB, 8])
        member = sb("member", [P, QB, NE])
        place = sb("place", [P, QB, NE + 1])
        gate = sb("gate", [P, QB, NE + 1])
        most = sb("most", [P, 8])
        most_i = sb("most_i", [P, 1], I32)
        hidc = sb("hidc", [P, 2, 16])
        kcmp = sb("kcmp", [P, 16])
        vcmp = sb("vcmp", [P, 64])

        def col(name, a=0, n=None):
            lo, hi = COLS[name]
            return con[:, lo + a:(lo + a + n if n is not None else hi)]

        ident = col("ident")
        zqk = arena[:, 0:2048].rearrange("p (t s) -> p t s", s=S)
        zbch = arena[:, 2048:5120].rearrange("p (t s) -> p t s", s=S)
        v1 = arena[:, 5120:6144].rearrange("p (b n) -> p b n", b=QB)
        cos0, sin0 = arena[:, 6144:6400], arena[:, 6400:6656]
        ang, turns = arena[:, 6656:6912], arena[:, 6912:7168]
        u_rows = arena[:, 0:2048].rearrange("p (b n) -> p b n", b=QB)
        v_rows = arena[:, 2048:4096].rearrange("p (b n) -> p b n", b=QB)
        ln_g, ln_b = arena[:, 4096:5120], arena[:, 5120:6144]
        ws = arena[:, 6144:7168].rearrange("p (g t) -> p g t", g=8)
        sel = arena[:, 0:256].rearrange("p (b c) -> p b c", b=QB)
        selg = arena[:, 256:512].rearrange("p (b c) -> p b c", b=QB)
        selT = arena[:, 512:768].rearrange("p (b s) -> p b s", b=QB)
        y_rows = arena[:, 1024:2048]
        act_rows = arena[:, 2048:2560].rearrange("p (q n) -> p q n", q=2)
        hid_rows = arena[:, 2560:3072].rearrange("p (q n) -> p q n", q=2)
        zT = arena[:, 0:NT * S].rearrange("p (t s) -> p t s", s=S)
        v2 = arena[:, 4608:5632].rearrange("p (b n) -> p b n", b=QB)
        qm = arena[:, 5632:6656].rearrange("p (h s) -> p h s", h=4)
        km = arena[:, 6656:7680].rearrange("p (h s) -> p h s", h=4)
        vm = arena[:, 7680:8192].rearrange("p (b n) -> p b n", b=QB)
        flat0 = score[:, 0].rearrange("p a b -> p (a b)")
        flat1 = score[:, 1].rearrange("p a b -> p (a b)")
        blk = flat1[:, 0:512].rearrange("p (v l n) -> p v l n", v=2, n=16)
        blk_hi, blk_lo = (v[:, :, :].rearrange("p q n -> p (q n)")[:, 0:512]
                          .rearrange("p (v l n) -> p v l n", v=2, n=16) for v in (h_hi, h_lo))
        acth = ff[:, 0:2]
        top_at = (nc.sbuf_usable_end - 2 * 4 * KT * P) // 64 * 64
        assert nc.sbuf_base <= top_at, (nc.sbuf_base, top_at)
        probT = nc.alloc_sbuf_tensor_at("probT", [P, 2, 8, P], F32, offset=top_at)
        c_hi = nc.alloc_sbuf_tensor_at("c_hi", [P, KT, P], F32R, offset=top_at)
        c_lo = nc.alloc_sbuf_tensor_at("c_lo", [P, KT, P], F32R, offset=top_at + 4 * KT * P)

        lat_hi, lat_lo = (v[:, 0:6, :].rearrange("p (v a) n -> p v (a n)", a=2) for v in (c_hi, c_lo))

        def bank(b, n=1):
            return ps[:, b:b + n, :].rearrange("p b n -> p (b n)")

        landed = [sem(f"landed{r}") for r in range(RING)]
        hi_ready = sem("hi_ready")
        lo_ready = sem("lo_ready")
        half_done = sem("half_done")
        resid_in = sem("resid_in")
        consts_in = sem("consts_in")
        params_in = sem("params_in")
        tables_in = sem("tables_in")
        ln_in = sem("ln_in")
        fin_in = sem("fin_in")
        bada_in = sem("bada_in")
        out_done = sem("out_done")
        consts_made = sem("consts_made")
        root_asked = sem("root_asked")
        root_ready = sem("root_ready")
        rows_scaled = sem("rows_scaled")
        rowsT_ready = sem("rowsT_ready")
        gained = sem("gained")
        normed_hi = sem("normed_hi")
        first_rows = sem("first_rows")
        squared = sem("squared")
        normed = sem("normed")
        projT_kept = sem("projT_kept")
        vrows_kept = sem("vrows_kept")
        angles_ready = sem("angles_ready")
        sines_ready = sem("sines_ready")
        rot_ready = sem("rot_ready")
        roped = sem("roped")
        conv_ready = sem("conv_ready")
        lam_asked = sem("lam_asked")
        lam_exp = sem("lam_exp")
        scores_ready = sem("scores_ready")
        max_ready = sem("max_ready")
        exp_ready = sem("exp_ready")
        probT_ready = sem("probT_ready")
        probT_kept = sem("probT_kept")
        mixed_ready = sem("mixed_ready")
        mixed_kept = sem("mixed_kept")
        heads_ready = sem("heads_ready")
        catT_ready = sem("catT_ready")
        catT_hi = sem("catT_hi")
        catT_kept = sem("catT_kept")
        ple_split = sem("ple_split")
        c_split = sem("c_split")
        ada_taken = sem("ada_taken")
        resid_ready = sem("resid_ready")
        act_ready = sem("act_ready")
        hid_ready = sem("hid_ready")
        ple_gated = sem("ple_gated")
        gelu_done = sem("gelu_done")
        vn_ready = sem("vn_ready")
        ws_masked = sem("ws_masked")
        spatial_ready = sem("spatial_ready")
        logits_ready = sem("logits_ready")
        route_asked = sem("route_asked")
        route_exp = sem("route_exp")
        member_ready = sem("member_ready")
        ranks_ready = sem("ranks_ready")
        routed = sem("routed")

        class Pass:

            def __init__(self, name, chunk, landed, hi_ready, lo_ready, done, first_slot):
                self.chunk, self.landed, self.first = chunk, landed, first_slot
                self.hi_ready, self.lo_ready, self.done = hi_ready, lo_ready, done
                self.sel_ready = sem(name + "sel_ready")
                self.gather_ready = sem(name + "gather_ready")
                self.gathered = sem(name + "gathered")
                self.gathered_hi = sem(name + "gathered_hi")
                self.gathered_lo = sem(name + "gathered_lo")
                self.selT_ready = sem(name + "selT_ready")
                self.selT_kept = sem(name + "selT_kept")
                self.act_ready = sem(name + "act_ready")
                self.hid_ready = sem(name + "hid_ready")
                self.hidT_ready = sem(name + "hidT_ready")
                self.hidT_hi = sem(name + "hidT_hi")
                self.hidT_lo = sem(name + "hidT_lo")
                self.y_kept = sem(name + "y_kept")
                self.scattered = sem(name + "scattered")
                self.merged = sem(name + "merged")

        more_landed = [sem(f"more_landed{r}") for r in range(RING)]
        more_hi = sem("more_hi_ready")
        more_lo = sem("more_lo_ready")
        more_done = sem("more_done")
        csilu_ready = sem("csilu_ready")
        grow_ready = sem("grow_ready")
        squares_ready = sem("squares_ready")
        latsum_ready = sem("latsum_ready")
        latms_ready = sem("latms_ready")
        latroot_ready = sem("latroot_ready")
        latent_ready = sem("latent_ready")
        mlaheads_kept = sem("mlaheads_kept")
        mlarot_ready = sem("mlarot_ready")
        mla_ready = sem("mla_ready")
        cmpblk_ready = sem("cmpblk_ready")
        cmpact_ready = sem("cmpact_ready")
        cmp_ready = sem("cmp_ready")
        cmp_kept = sem("cmp_kept")
        gateT_ready = sem("gateT_ready")
        gates_ready = sem("gates_ready")
        dve_step = sem("dve_step")
        act_step = sem("act_step")
        pool_step = sem("pool_step")

        first_pass = Pass("moe_", 0, landed, hi_ready, lo_ready, half_done, W_MOE)
        second_pass = Pass("more_", 1, more_landed, more_hi, more_lo, more_done, 0)
        EH = 2 * 3 * J1
        BODY = 2 * EH
        assert BODY // 2 % RING == 0 and BODY % PAIRS == 0 and W_MOE % RING == 0 and 2 * W_MOE % PAIRS == 0

        def overflowing(eng):
            eng.wait_ge(routed, 1)
            return eng.value_load(most_i[0:1, 0:1], min_val=0, max_val=S) > P

        def bc(ap, n):
            return ap.unsqueeze(2).broadcast_to([ap.shape[0], ap.shape[1], n])

        def rep(ap, n):
            return ap.unsqueeze(1).broadcast_to([ap.shape[0], n, ap.shape[1]])

        block = ctx.enter_context(nc.Block())

        @block.sync
        def _(sp):
            sp.dma_start(resid[:, :, :], x_in.rearrange("(b p) n -> p b n", p=P)).then_inc(resid_in, 16)
            for r in range(RING):
                sp.dma_start(ring[:, r, :], stream[r]).then_inc(landed[r], 16)
            laps = SLOTS // RING
            moe0, moe1 = W_MOE // RING, (W_MOE + 3 * J1 * NE) // RING

            def laps_of(start, end):
                with sp.Fori(start, end) as lap:
                    for r in range(RING):
                        sp.wait_ge(lo_ready, lap * (2 * RING) + 2 * (r + 1 - RING))
                        sp.dma_start(ring[:, r, :],
                                     stream[bass.ds(lap * RING + r, 1)].rearrange("a p n -> (a p) n"))\
                            .then_inc(landed[r], 16)

            laps_of(1, moe1)
            with sp.If(overflowing(sp)):
                sp.wait_ge(lo_ready, 2 * moe1 * RING)
                for r in range(RING):
                    sp.dma_start(ring[:, r, :], stream[W_MOE + r]).then_inc(more_landed[r], 16)
                with sp.Fori(1, moe1 - moe0) as lap:
                    for r in range(RING):
                        sp.wait_ge(more_lo, lap * (2 * RING) + 2 * (r + 1 - RING))
                        sp.dma_start(ring[:, r, :],
                                     stream[bass.ds(lap * RING + (W_MOE + r), 1)].rearrange("a p n -> (a p) n"))\
                            .then_inc(more_landed[r], 16)
                sp.wait_ge(more_lo, 2 * (moe1 - moe0) * RING)
            laps_of(moe1, laps)
            for n in range(laps * RING, SLOTS):
                sp.wait_ge(lo_ready, 2 * (n + 1 - RING))
                sp.dma_start(ring[:, n % RING, :], stream[n]).then_inc(landed[n % RING], 16)
            sp.wait_ge(resid_ready, 12)
            sp.dma_start(out.rearrange("(b p) n -> p b n", p=P), rows[:, :, :]).then_inc(out_done, 16)
            sp.wait_ge(out_done, 16)

        @block.tensor
        def _(pe):
            def half_slot(m, shape):
                pe.wait_ge(lo_ready, m + 1)
                return [w[:, m % PAIRS, :].rearrange("p (k n) -> p k n", k=shape) for w in (w_hi, w_lo)]

            def product(out_, lhs, rhs, start, stop):
                pe.matmul(out_, lhs[0], rhs[0], start=start, stop=False)
                pe.matmul(out_, lhs[0], rhs[1], start=False, stop=False)
                return pe.matmul(out_, lhs[1], rhs[0], start=False, stop=stop)

            unsplit = [0]

            def rowsT(k):
                for n in range(4):
                    h, t = n // 2, n % 2
                    if n < 2:
                        pe.wait_ge(rows_scaled, QB * (k + (k >= 6)) + t + 1)
                    for i in range(4):
                        f = slice((4 * h + i) * P, (4 * h + i + 1) * P)
                        last = pe.transpose(ps[:, 4 + n, i * P:(i + 1) * P], rows[:, t, f], ident)
                    last.then_inc(rowsT_ready, 1)
                pe.wait_ge(normed, 4 * k + 2)
                unsplit[0] = 4 * k + 4

            def x_tile(k):
                if k == KT // 2 and unsplit[0]:
                    pe.wait_ge(normed, unsplit[0])
                    unsplit[0] = 0

            def feature_tile(m, b, i):
                w = half_slot(m, KT)
                for k in range(KT):
                    x_tile(k)
                    last = product(ps[:, b, i * S:(i + 1) * S], [v[:, k, :] for v in w],
                                   (x_hi[:, k, :], x_lo[:, k, :]), k == 0, k == KT - 1)
                last.then_inc(half_done, 1)

            def tiles(n0, count, job0, fresh, first=0):
                for s in range(first, count):
                    if s >= 4 or not fresh:
                        pe.wait_ge(projT_kept, job0 + s - 3)
                    for i in range(2):
                        feature_tile(2 * (n0 + s) + i, s % 4, i)

            def row_tile(m, lhs, b0, start, stop, blocks=QB, branch=False):
                w = half_slot(m, 1)
                for t in range(blocks):
                    for h in range(2):
                        last = product(ps[:, b0 + 2 * t + h, :], [v[:, t * P:(t + 1) * P] for v in lhs],
                                       [v[:, 0, h * BANK:(h + 1) * BANK] for v in w], start, stop)
                    if branch and stop and t == 0:
                        last.then_inc(first_rows, 1)
                last.then_inc(half_done, 1)

            def row_product(n0, b0, branch=False):
                for k in range(KT):
                    x_tile(k)
                    row_tile(2 * n0 + k, (x_hi[:, k, :], x_lo[:, k, :]), b0, k == 0, k == KT - 1,
                             branch=branch)

            def value_rows(n0):
                for k in range(KT):
                    if k % 2 == 0:
                        w = half_slot(2 * n0 + k // 2, 2)
                    for t in range(QB):
                        last = product(ps[:, 4 + t, :], [v[:, k, t * P:(t + 1) * P] for v in (x_hi, x_lo)],
                                       [v[:, k % 2, :] for v in w], k == 0, k == KT - 1)
                    if k % 2:
                        last.then_inc(half_done, 1)

            def cat_transpose(tiles_):
                for t in range(QB):
                    for half in range(tiles_ // 4):
                        for i in range(4):
                            f = 4 * half + i
                            last = pe.transpose(ps[:, 4 + 2 * t + half, i * P:(i + 1) * P],
                                                rows[:, t, f * P:(f + 1) * P], ident)
                        last.then_inc(catT_ready, 1)

            def attention(layer):
                groups = attention_groups(layer)
                base = GROUP_BASE[0 if layer is None else layer + 1]

                def scores(i):
                    kind, qb, hg = groups[i]
                    g = base + i
                    if i >= 2:
                        pe.wait_ge(max_ready, g - 1)
                    kw = NCMP if kind == "nsac" else P * (qb + 1)
                    qs = slice(qb * P, (qb + 1) * P)
                    for u in range(4):
                        if kind == "diff":
                            r, h = 64 * (u // 2), 2 * hg + u % 2
                            q, k = zqk[r:r + 64, h, qs], zqk[r:r + 64, 4 + h, 0:kw]
                        elif kind == "swa":
                            r = 64 * (u // 2)
                            q, k = zT[r:r + 64, T_SWAQ + u % 2, qs], zT[r:r + 64, T_SWAK, 0:kw]
                        elif kind == "moba":
                            r = 64 * (u // 2)
                            q, k = zT[r:r + 64, T_MOBQ + u % 2, qs], zT[r:r + 64, T_MOBK + u % 2, 0:kw]
                        elif kind == "mla":
                            q, k = qm[:, u, qs], km[:, u, 0:kw]
                        else:
                            r = 64 * (u // 2)
                            q = zT[r:r + 64, T_NSAQ + u % 2, qs]
                            k = {"nsac": kcmp[r:r + 64, 0:NCMP], "nsas": zT[r:r + 64, T_KS, 0:kw],
                                 "nsaw": zT[r:r + 64, T_KW, 0:kw]}[kind]
                        last = pe.matmul(ps[:, 2 * (g % 2) + u // 2, (u % 2) * S:(u % 2) * S + kw], q, k,
                                         start=True, stop=True)
                    last.then_inc(scores_ready, 1)

                def transposes(i):
                    kind, qb, hg = groups[i]
                    g = base + i
                    pe.wait_ge(exp_ready, g + 1)
                    pe.wait_ge(probT_kept, g)
                    nkb = 1 if kind == "nsac" else qb + 1
                    kp = NCMP if kind == "nsac" else P
                    for u in range(4):
                        for kb in range(nkb):
                            n = u * nkb + kb
                            last = pe.transpose(ps[0:kp, 4 + n // 4, (n % 4) * P:(n % 4 + 1) * P],
                                                score[:, g % 2, u, kb * P:kb * P + kp], ident)
                    last.then_inc(probT_ready, 1)

                def mix(i):
                    kind, qb, hg = groups[i]
                    g = base + i
                    pe.wait_ge(probT_kept, g + 1)
                    if i >= 2:
                        pe.wait_ge(mixed_kept, g - 1)
                    nkb = 1 if kind == "nsac" else qb + 1
                    kp = NCMP if kind == "nsac" else P
                    vw = P if kind == "diff" else 64
                    for u in range(4):
                        o = head_of(kind, u)
                        for kb in range(nkb):
                            if kind == "diff":
                                h = 2 * hg + u % 2
                                v = v1[:, kb, h * P:(h + 1) * P]
                            elif kind == "swa":
                                v = v2[:, kb, (o // 2) * 64:(o // 2) * 64 + 64]
                            elif kind == "nsas":
                                v = v2[:, kb, 128:192]
                            elif kind == "nsaw":
                                v = v2[:, kb, 192:256]
                            elif kind == "moba":
                                v = v2[:, kb, 256 + o * 64:256 + o * 64 + 64]
                            elif kind == "mla":
                                v = vm[:, kb, o * 64:o * 64 + 64]
                            else:
                                v = vcmp[0:kp, :]
                            last = pe.matmul(ps[:, 6 + g % 2, o * vw:(o + 1) * vw],
                                             probT[0:kp, g % 2, u * nkb + kb, :], v,
                                             start=kb == 0, stop=kb == nkb - 1)
                    last.then_inc(mixed_ready, 1)

                scores(0)
                scores(1)
                for i in range(len(groups)):
                    if i + 2 < len(groups):
                        scores(i + 2)
                    transposes(i)
                    if i >= 1:
                        mix(i - 1)
                mix(len(groups) - 1)

            def up(n, banks, j, ready):
                if j >= 2:
                    pe.wait_ge(hid_ready, ready(j - 2))
                for s, b in enumerate(banks):
                    for i in range(2):
                        feature_tile(2 * (n + s) + i, b, i)

            def down(n, j, ready, first, final):
                pe.wait_ge(hid_ready, ready(j))
                for kk in range(2):
                    row_tile(2 * n + kk, [v[:, j % 2, kk * S:(kk + 1) * S] for v in (h_hi, h_lo)], 4,
                             first and kk == 0, final and kk == 1, branch=True)

            def swiglu(n0):
                n = n0

                def ready(j):
                    return j + 1

                for j in range(J1 + 1):
                    if j < J1:
                        up(n, [2 * (j % 2), 2 * (j % 2) + 1], j, ready)
                        n += 2
                    if j >= 1:
                        down(n, j - 1, ready, j == 1, j == J1)
                        n += 1

            pe.wait_ge(consts_in, 16)
            pe.wait_ge(consts_made, 1)
            rowsT(0)
            tiles(W_QK, 4, 0, True)
            tiles(W_BCH, 1, 4, False)
            pe.wait_ge(projT_kept, 4)
            pe.wait_ge(tables_in, 16)
            x_tile(KT // 2)
            for t in range(8):
                last = pe.matmul(ps[:, 4 + t // 2, (t % 2) * S:(t % 2 + 1) * S], col("rot0"), zqk[:, t, :],
                                 start=True, stop=True)
            last.then_inc(rot_ready, 1)
            tiles(W_BCH, 6, 4, False, 1)
            pe.wait_ge(roped, 1)
            value_rows(W_V)
            pe.wait_ge(projT_kept, 10)
            pe.wait_ge(vrows_kept, 1)
            attention(None)
            pe.wait_ge(heads_ready, 1)
            cat_transpose(4)
            pe.wait_ge(catT_kept, 2)
            pe.wait_ge(conv_ready, 1)
            row_product(W_OUT0, 4, branch=True)
            rowsT(1)
            swiglu(W_FFN0)

            def ple(layer, n0):
                row_product(n0, 0)
                pe.wait_ge(ple_split, layer + 1)
                for k in range(2):
                    row_tile(2 * (n0 + 4) + k, [v[:, 0, k * S:(k + 1) * S] for v in (h_hi, h_lo)], 4, k == 0, k == 1)

            rowsT(2)
            ple(0, W_PLE0)
            rowsT(3)
            row_product(W_CIN, 0)
            row_product(W_CIN + 4, 4)
            pe.wait_ge(ws_masked, 1)
            for t in range(QB):
                pe.wait_ge(vn_ready, t + 1)
                for half in range(2):
                    for i in range(4):
                        g = 4 * half + i
                        last = pe.matmul(ps[:, 2 * t + half, i * P:(i + 1) * P], ws[:, g, :],
                                         v_rows[:, t, g * P:(g + 1) * P], start=True, stop=True)
                    last.then_inc(spatial_ready, 1)
            pe.wait_ge(heads_ready, 2)
            cat_transpose(8)
            pe.wait_ge(catT_kept, 6)
            row_product(W_COUT, 4, branch=True)
            rowsT(4)
            pe.wait_ge(gained, 20)
            unsplit[0] = 0
            for t in range(QB):
                for k in range(KT):
                    last = pe.matmul(ps[:, 0, t * 8:(t + 1) * 8], xT[:, k, t * P:(t + 1) * P],
                                     col("router", k * 8, 8), start=k == 0, stop=k == KT - 1)
            last.then_inc(logits_ready, 1)
            pe.wait_ge(member_ready, 1)
            pe.matmul(ps[:, 1, 0:8], col("before"), member[:, 0, :], start=True, stop=True)
            pe.matmul(ps[:, 1, 8:16], col("before"), member[:, 1, :], start=True, stop=False)
            pe.matmul(ps[:, 1, 8:16], ones[:, :], member[:, 0, :], start=False, stop=True)
            for t in range(QB):
                last = pe.matmul(ps[:, 1, 16:24], ones[:, :], member[:, t, :], start=t == 0, stop=t == 1)
            last.then_inc(ranks_ready, 1)

            def gather(w, ready):
                pe.wait_ge(w.sel_ready, ready)
                for half_ in range(2):
                    for i in range(4):
                        f = 4 * half_ + i
                        for t in range(QB):
                            last = pe.matmul(ps[:, 6 + half_, i * P:(i + 1) * P], rows[:, t, f * P:(f + 1) * P],
                                             sel[:, t, :], start=t == 0, stop=t == 1)
                    last.then_inc(w.gather_ready, 1)

            def experts(w):
                gather(w, 1)
                with pe.Fori(0, NE // 2) as turn:
                    for x in range(2):
                        expert(w, turn, x)

            def expert(w, turn_, x):
                def e(per, plus):
                    return turn_ * (2 * per) + (x * per + plus)

                pe.wait_ge(w.gathered_lo, e(2, 2))

                def weights(i, k):
                    pe.wait_ge(w.lo_ready, turn_ * BODY + (2 * w.first + x * EH + i + 1))
                    return [v[:, (x * EH + i) % PAIRS, :].rearrange("p (k n) -> p k n", k=k) for v in (w_hi, w_lo)]

                def up(i, b, c):
                    for h in range(2):
                        m = weights(2 * i + h, 4)
                        for k in range(4):
                            last = product(ps[:, b, c:c + 256], [v[:, 4 * h + k, 0:P] for v in (x_hi, x_lo)],
                                           [v[:, k, :] for v in m], h == 0 and k == 0, h == 1 and k == 3)
                        last.then_inc(w.done, 1)

                def turn(j):
                    pe.wait_ge(w.hid_ready, e(J1, j + 1))
                    for i in range(2):
                        c = 256 * (j % 2) + i * P
                        last = pe.transpose(ps[:, 2, c:c + P], hid_rows[:, j % 2, i * P:(i + 1) * P], ident)
                    last.then_inc(w.hidT_ready, 1)

                def down(i, j):
                    pe.wait_ge(w.hidT_lo, e(J1, j + 1))
                    for kk in range(2):
                        m = weights(2 * i + kk, 1)
                        for h in range(2):
                            last = product(ps[:, 4 + h, :], [v[:, j % 2, kk * P:(kk + 1) * P] for v in (h_hi, h_lo)],
                                           [v[:, 0, h * BANK:(h + 1) * BANK] for v in m],
                                           j == 0 and kk == 0, j == J1 - 1 and kk == 1)
                        last.then_inc(w.done, 1)

                n = 0
                for j in range(J1 + 1):
                    if j < J1:
                        up(n, j % 2, 0)
                    if j == 1:
                        pe.wait_ge(w.merged, e(1, 1))
                    if j >= 1:
                        turn(j - 1)
                    if j == 2:
                        for t in range(QB):
                            last = pe.transpose(ps[:, 3, t * P:(t + 1) * P], selg[:, t, :], ident)
                        last.then_inc(w.selT_ready, 1)
                    if j < J1:
                        up(n + 1, j % 2, 256)
                        n += 2
                    if j >= 1:
                        down(n, j - 1)
                        n += 1
                gather(w, e(1, 2))
                pe.wait_ge(w.selT_kept, e(1, 1))
                pe.wait_ge(w.y_kept, e(2, 2))
                for t in range(QB):
                    for h in range(2):
                        last = pe.matmul(ps[:, (4, 2)[t] + h, :], selT[:, t, :], y_rows[:, h * BANK:(h + 1) * BANK],
                                         start=True, stop=True)
                    last.then_inc(w.scattered, 1)

            experts(first_pass)
            with pe.If(overflowing(pe)):
                experts(second_pass)
            rowsT(5)
            ple(1, W_PLE1)
            for l in range(2):
                n0 = W_BLK + l * B_ALL
                pe.wait_ge(c_split, l + 1)
                pe.wait_ge(resid_ready, 6 + 3 * l)
                for part in range(6):
                    if part == 2:
                        pe.wait_ge(resid_ready, 7 + 2 * l)
                    if part >= 4:
                        pe.wait_ge(ada_taken, 8 * l + 2 * (part - 3))
                    for k in range(KT):
                        row_tile(2 * (n0 + B_ADA) + KT * part + k, (c_hi[:, k, :], c_lo[:, k, :]),
                                 2 * (part % 4), k == 0, k == KT - 1, blocks=1)
                rowsT(6 + 2 * l)
                job0 = 10 + 9 * l
                tiles(n0 + B_IN, LATENT_SLOTS, job0, True)
                pe.wait_ge(squares_ready, l + 1)
                sq = flat0
                pe.matmul(ps[:, 6, 0:S], ones[:, :], sq[:, 0:S], start=True, stop=True)
                for k in range(2):
                    last = pe.matmul(ps[:, 6, S:2 * S], ones[:, :], sq[:, (k + 1) * S:(k + 2) * S],
                                     start=k == 0, stop=k == 1)
                last.then_inc(latsum_ready, 1)
                pe.wait_ge(projT_kept, job0 + T_GATE // 2 + 1)
                for t in range(QB):
                    last = pe.transpose(ps[:, 7, t * P:(t + 1) * P], zT[:, T_GATE, t * P:(t + 1) * P], ident)
                last.then_inc(gateT_ready, 1)
                tiles(n0 + B_IN, 9, job0, True, LATENT_SLOTS)
                value_rows(n0 + B_V)
                uq = half_slot(2 * (n0 + B_SMALL), 2)
                pe.wait_ge(projT_kept, job0 + 9)
                pe.wait_ge(vrows_kept, 2 + l)
                pe.wait_ge(latent_ready, l + 1)
                for h in range(4):
                    for k in range(2):
                        last = product(ps[:, 2 + h // 2, (h % 2) * S:(h % 2 + 1) * S],
                                       [v[:, k, h * P:(h + 1) * P] for v in uq],
                                       [v[:, 1 + k, :] for v in (lat_hi, lat_lo)], k == 0, k == 1)
                last.then_inc(half_done, 1)
                kv = half_slot(2 * (n0 + B_SMALL) + 1, 1)
                for h in range(4):
                    product(ps[:, 4 + h // 2, (h % 2) * S:(h % 2 + 1) * S], [v[:, 0, h * P:(h + 1) * P] for v in kv],
                            [v[:, 0, :] for v in (lat_hi, lat_lo)], True, True)
                for t in range(QB):
                    last = product(ps[:, 6, t * S:(t + 1) * S], [v[:, 0, t * P:(t + 1) * P] for v in (lat_hi, lat_lo)],
                                   [v[:, 0, 512:768] for v in kv], True, True)
                last.then_inc(half_done, 1)
                pe.wait_ge(cmpblk_ready, l + 1)
                pe.wait_ge(gates_ready, l + 1)
                for which in range(2):
                    if which == 1:
                        pe.wait_ge(mlaheads_kept, l + 1)
                        for h in range(4):
                            pe.matmul(ps[:, 2 + h // 2, (h % 2) * S:(h % 2 + 1) * S], col("rotm"), qm[:, h, :],
                                      start=True, stop=True)
                        last = pe.matmul(ps[:, 1, 0:S], col("rotm"), zT[:, T_KPE, :], start=True, stop=True)
                        last.then_inc(mlarot_ready, 1)
                    for h in range(2):
                        w = half_slot(2 * (n0 + B_CMP + which) + h, 8)
                        for j in range(8):
                            last = product(ps[:, 7, which * 16:which * 16 + 16], [v[:, j, :] for v in w],
                                           [v[:, which, 8 * h + j, :] for v in (blk_hi, blk_lo)],
                                           h == 0 and j == 0, h == 1 and j == 7)
                        last.then_inc(half_done, 1)
                pe.wait_ge(cmpact_ready, l + 1)
                pe.matmul(ps[:, 7, 32:32 + NCMP], col("cmpw2", 192 * l, P), hidc[:, 0, 0:NCMP], start=True, stop=True)
                pe.matmul(ps[0:NCMP, 7, 64:128], hidc[:, 1, 0:NCMP], col("cmpw2", 192 * l + P, 64), start=True, stop=True)\
                    .then_inc(cmp_ready, 1)
                pe.wait_ge(mla_ready, l + 1)
                pe.wait_ge(cmp_kept, l + 1)
                attention(l)
                pe.wait_ge(mixed_kept, GROUP_BASE[1 + l] + 12)
                cat_transpose(8)
                pe.wait_ge(catT_kept, 10 + 4 * l)
                row_product(n0 + B_OUT, 4, branch=True)
                rowsT(7 + 2 * l)
                step0 = J1 + l * J2

                def ready(j):
                    return step0 + j + 1

                n = n0 + B_MLP
                for j in range(J2 + 1):
                    if j < J2:
                        up(n, [j % 2], j, ready)
                        n += 1
                    if j >= 1:
                        down(n, j - 1, ready, j == 1, j == J2)
                        n += 1

        @block.vector
        def _(dve):
            steps = [0]

            def link(ins):
                steps[0] += 1
                ins.then_inc(dve_step, 1)
                dve.wait_ge(dve_step, steps[0])

            split_at, split_end = [0], [2 * W_MOE]

            def split_to(m_end):
                for m in range(split_at[0], min(m_end, split_end[0])):
                    dve.wait_ge(hi_ready, m + 1)
                    a = m % 2 * HALF
                    dve.tensor_tensor(w_lo[:, m % PAIRS, :], ring[:, m // 2 % RING, a:a + HALF],
                                      w_hi[:, m % PAIRS, :].bitcast(F32), ALU.subtract).then_inc(lo_ready, 1)
                    split_at[0] = m + 1

            def slots_done(n):
                split_to(2 * n + PAIRS)
                dve.wait_ge(half_done, 2 * n)

            def split(hi, lo, src):
                link(dve.tensor_copy(hi, src))
                return dve.tensor_tensor(lo, src, hi.bitcast(F32), ALU.subtract)

            roots = [0]

            def root(src, n, scale, eps):
                dve.tensor_scalar(stat[:, 0:n], src, scale, eps, ALU.mult, ALU.add).then_inc(root_asked, 1)
                roots[0] += 1
                dve.wait_ge(root_ready, roots[0])

            norms = [0]

            def norm_rows():
                link(dve.tensor_tensor_reduce(out=rows[:, 0, :], in0=resid[:, 0, :], in1=resid[:, 0, :],
                                              scale=1.0, scalar=0.0, op0=ALU.mult, op1=ALU.add,
                                              accum_out=stat[:, 8:9]))
                norms[0] += 1
                dve.wait_ge(squared, norms[0])
                root(stat[:, 8:10], 2, 1.0 / D, RMS_EPS)
                for t in range(QB):
                    dve.tensor_scalar(rows[:, t, :], resid[:, t, :], stat[:, t:t + 1], None, ALU.mult)\
                        .then_inc(rows_scaled, 1)

            ahead = [0]

            def norm(k, gain, shift=None):
                norm_rows()
                split_to(ahead[0])

                def lo(b):
                    h, t = b // 2, b % 2
                    dve.wait_ge(normed_hi, 4 * k + b + 1)
                    at = slice(None), slice(4 * h, 4 * h + 4), slice(t * P, (t + 1) * P)
                    dve.tensor_tensor(x_lo[at], xT[at], x_hi[at].bitcast(F32), ALU.subtract).then_inc(normed, 1)

                for b in range(4):
                    h, t = b // 2, b % 2
                    dve.wait_ge(rowsT_ready, 4 * k + b + 1)
                    src = ps[:, 4 + b, :].rearrange("p (f s) -> p f s", f=4)
                    dst = xT[:, 4 * h:4 * h + 4, t * P:(t + 1) * P]
                    ins = dve.tensor_tensor(dst, src, bc(gain[:, 4 * h:4 * h + 4], P), ALU.mult)
                    if shift is not None:
                        link(ins)
                        ins = dve.tensor_tensor(dst, dst, bc(shift[:, 4 * h:4 * h + 4], P), ALU.add)
                    ins.then_inc(gained, 1)
                    if b >= 1:
                        lo(b - 1)
                lo(3)

            def gain(k):
                return col("gain", 8 * k, 8)

            branches = [0]

            def add_branch(end, gate=None):
                split_to(2 * end + PAIRS - 1)
                ahead[0] = 2 * end + PAIRS
                branches[0] += 1
                for t in range(QB):
                    if t == 0:
                        dve.wait_ge(first_rows, branches[0])
                    else:
                        dve.wait_ge(half_done, 2 * end)
                    src = bank(4 + 2 * t, 2)
                    if gate is not None:
                        link(dve.tensor_tensor(rows[:, t, :], src, gate, ALU.mult))
                        src = rows[:, t, :]
                    ins = dve.tensor_tensor(resid[:, t, :], resid[:, t, :], src, ALU.add)
                ins.then_inc(resid_ready, 1)

            def attention(layer, meanwhile=None):
                groups = attention_groups(layer)
                base = GROUP_BASE[0 if layer is None else layer + 1]

                def soften(i):
                    kind, qb, hg = groups[i]
                    g = base + i
                    kw = NCMP if kind == "nsac" else P * (qb + 1)
                    src = bank(2 * (g % 2), 2).rearrange("p (u k) -> p u k", u=4)[:, :, 0:kw]
                    sc = score[:, g % 2, :, 0:kw]
                    m = soft[:, g % 4, 0, :]
                    scale = 96.0 ** -0.5 if kind == "mla" else 0.125
                    dve.wait_ge(scores_ready, g + 1)
                    if i >= 2:
                        dve.wait_ge(probT_ready, g - 1)
                    if kind in ("diff", "mla"):
                        link(dve.tensor_tensor(sc, src, rep(col("causal", qb * S, kw), 4), ALU.add))
                    else:
                        table = {"swa": col("window", qb * S, kw), "nsac": col("nsac", qb * NCMP, NCMP)}
                        first = {"swa": 0, "moba": 2}.get(kind, 1)
                        for u in range(4):
                            ins = dve.scalar_tensor_tensor(
                                out=sc[:, u, :], in0=table.get(kind, col("alibi", qb * S, kw)),
                                scalar=SLOPES[first + 3 * head_of(kind, u)] * 8.0, in1=src[:, u, :], op0=ALU.mult, op1=ALU.add)
                        link(ins)
                    if kind == "swa":
                        sc = score[:, g % 2, :, 0:kw + 1]
                        link(dve.tensor_scalar(sc[:, :, kw:kw + 1].rearrange("p u o -> p (u o)"), sink[:, layer, :],
                                               8.0, None, ALU.mult))
                    link(dve.tensor_reduce(m, sc, AX.X, ALU.max))
                    if kind == "nsac":
                        dve.tensor_scalar(m, m, GUARD, -scale, ALU.max, ALU.mult).then_inc(max_ready, 1)
                    else:
                        dve.tensor_scalar(m, m, -scale, None, ALU.mult).then_inc(max_ready, 1)

                def finish(i):
                    kind, qb, hg = groups[i]
                    g = base + i
                    den, rden, coef = (soft[:, g % 4, n, :] for n in (1, 2, 3))
                    dve.wait_ge(exp_ready, g + 1)
                    link(dve.tensor_scalar(den, den, TINY, None, ALU.max))
                    link(dve.reciprocal(rden, den))
                    w = P if kind == "diff" else 64
                    src = ps[:, 6 + g % 2, 0:4 * w].rearrange("p (u n) -> p u n", u=4)
                    if kind == "diff":
                        link(dve.tensor_tensor(coef, rden, lam[:, 4:8], ALU.mult))
                        dve.wait_ge(mixed_ready, g + 1)
                        tmp = xT[:, 0:2, :].rearrange("p a (b n) -> p (a b) n", b=2)
                        link_kept(dve.tensor_tensor(tmp, src, bc(coef, P), ALU.mult), g)
                        link(dve.tensor_tensor(rows[:, qb, hg * S:(hg + 1) * S], xT[:, 0, :], xT[:, 1, :], ALU.add))
                        return
                    m0 = {"swa": 0, "mla": 256, "moba": 768}.get(kind, 512)
                    dst = rows[:, qb, m0:m0 + 256].rearrange("p (u n) -> p u n", u=4)
                    if kind.startswith("nsa"):
                        b = "csw".index(kind[3])
                        if (kind, qb) == ("nsac", 0):
                            dve.wait_ge(gates_ready, layer + 1)
                        link(dve.tensor_tensor(coef, rden, gates[:, qb, 4 * b:4 * b + 4], ALU.mult))
                        dve.wait_ge(mixed_ready, g + 1)
                        if kind == "nsac":
                            link_kept(dve.tensor_tensor(dst, src, bc(coef, 64), ALU.mult), g)
                        else:
                            tmp = ff[:, 2, 0:256].rearrange("p (u n) -> p u n", u=4)
                            link_kept(dve.tensor_tensor(tmp, src, bc(coef, 64), ALU.mult), g)
                            link(dve.tensor_tensor(dst, dst, tmp, ALU.add))
                    else:
                        dve.wait_ge(mixed_ready, g + 1)
                        link_kept(dve.tensor_tensor(dst, src, bc(rden, 64), ALU.mult), g)

                soften(0)
                soften(1)
                if meanwhile is not None:
                    meanwhile()
                for i in range(len(groups)):
                    if i + 2 < len(groups):
                        soften(i + 2)
                    if i >= 1:
                        finish(i - 1)
                finish(len(groups) - 1)

            def link_kept(ins, g):
                ins.then_inc(mixed_kept, 1)
                dve.wait_ge(mixed_kept, g + 1)

            hids = [0]

            def hidden(j, ready, done, paired):
                split_to(2 * done + PAIRS)
                dve.wait_ge(act_ready, ready(j))
                p = j % 2
                other = acth[:, p, :]
                if paired:
                    slots_done(done)
                    other = ps[:, 2 * p + 1, :]
                if hids[0]:
                    dve.wait_ge(hid_ready, hids[0])
                link(dve.tensor_tensor(ff[:, 2, :], acth[:, p, :], other, ALU.mult))
                split(h_hi[:, p, :], h_lo[:, p, :], ff[:, 2, :]).then_inc(hid_ready, 1)
                hids[0] += 1

            def keep_cat(count, before, gain=None):
                for n in range(count):
                    dve.wait_ge(catT_hi, before + n + 1)
                    t, h = (n, 0) if count == 2 else (n // 2, n % 2)
                    at = slice(None), slice(4 * h, 4 * h + 4), slice(t * P, (t + 1) * P)
                    src = ps[:, 4 + 2 * t + h, :].rearrange("p (f s) -> p f s", f=4)
                    hi = x_hi[at].bitcast(F32)
                    if gain is None:
                        ins = dve.tensor_tensor(x_lo[at], src, hi, ALU.subtract)
                    else:
                        ins = dve.scalar_tensor_tensor(out=x_lo[at], in0=src, scalar=gain, in1=hi,
                                                       op0=ALU.mult, op1=ALU.subtract)
                    ins.then_inc(catT_kept, 1)

            def split_c():
                link(dve.tensor_copy(c_hi[:, :, :], bc(csilu[:, :], P)))
                dve.tensor_tensor(c_lo[:, :, :], bc(csilu[:, :], P), c_hi[:, :, :].bitcast(F32), ALU.subtract)\
                    .then_inc(c_split, 1)

            dve.memset(ones[:, :], 1.0).then_inc(consts_made, 1)
            dve.wait_ge(consts_in, 16)
            split_to(PAIRS)
            dve.wait_ge(resid_in, 16)
            norm(0, gain(0))
            split_to(PAIRS + 1)
            dve.wait_ge(params_in, 16 * 4)
            link(dve.tensor_copy(ang, posi[:, :]))
            link(dve.tensor_scalar(ang, ang, col("invf"), None, ALU.mult))
            magic = 1.5 * 2.0 ** 23
            link(dve.tensor_scalar(turns, ang, 1.0 / (2 * math.pi), magic, ALU.mult, ALU.add))
            link(dve.tensor_scalar(turns, turns, -magic, None, ALU.add))
            split_to(PAIRS + 2)
            c1 = 6.28125
            c2 = math.floor((2 * math.pi - c1) * 2 ** 21) / 2 ** 21
            c3 = 2 * math.pi - c1 - c2
            for c in (c1, c2, c3):
                link(dve.scalar_tensor_tensor(out=ang, in0=turns, scalar=-c, in1=ang, op0=ALU.mult, op1=ALU.add))
            lim = float(np.nextafter(np.float32(math.pi), np.float32(0)))
            link(dve.tensor_scalar(ang, ang, -lim, lim, ALU.max, ALU.min))
            link(dve.tensor_scalar(turns, ang, -1.0, None, ALU.mult))
            link(dve.tensor_tensor(turns, turns, ang, ALU.max))
            dve.tensor_scalar(turns, turns, -1.0, math.pi / 2, ALU.mult, ALU.add).then_inc(angles_ready, 1)
            split_to(PAIRS + 4)
            for i in range(2):
                link(dve.tensor_tensor_reduce(out=rows[:, 0, 0:64], in0=lamv[:, 128 * i:128 * i + 64],
                                              in1=lamv[:, 128 * i + 64:128 * i + 128], scale=1.0, scalar=0.0,
                                              op0=ALU.mult, op1=ALU.add, accum_out=lam[:, i:i + 1]))
            dve.memset(lam[:, 4:8], 1.0).then_inc(lam_asked, 1)
            split_to(2 * W_BCH + PAIRS)
            dve.wait_ge(lam_exp, 1)
            link(dve.tensor_tensor(lam[:, 0:1], lam[:, 3:4], lam[:, 2:3], ALU.subtract))
            link(dve.tensor_scalar(lam[:, 0:1], lam[:, 0:1], -LAMBDA_INIT, None, ALU.add))
            for i in (6, 7):
                dve.tensor_copy(lam[:, i:i + 1], lam[:, 0:1])
            link(dve.tensor_scalar(sub8[:, :], col("subln"), 1.0 - LAMBDA_INIT, None, ALU.mult))
            split_to(2 * (W_BCH + 1) + PAIRS)
            dve.wait_ge(tables_in, 16)
            dve.wait_ge(rot_ready, 1)
            dve.wait_ge(sines_ready, 2)
            rot = bank(4, 4).rearrange("p (t s) -> p t s", s=S)
            rtmp = rows[:, :, :].rearrange("p b (t s) -> p (b t) s", s=S)
            link(dve.tensor_tensor(rtmp, rot, rep(sin0, 8), ALU.mult))
            split_to(2 * (W_BCH + 1) + PAIRS + 1)
            link(dve.tensor_tensor(zqk, zqk, rep(cos0, 8), ALU.mult))
            split_to(2 * (W_BCH + 1) + PAIRS + 2)
            dve.tensor_tensor(zqk, zqk, rtmp, ALU.add).then_inc(roped, 1)
            split_to(2 * W_V + PAIRS)
            dve.wait_ge(projT_kept, 10)
            zb, zc, zh = zbch[:, 0:4, :], zbch[:, 4:8, :], zbch[:, 8:12, :]
            link(dve.tensor_tensor(zc, zc, zh, ALU.mult))
            for i in range(4):
                ins = dve.tensor_scalar(zh[:, i, :], zc[:, i, :], col("conv", 3 * i + 2, 1), None, ALU.mult)
            link(ins)
            for tap in (1, 0):
                lag = 2 - tap
                for i in range(4):
                    ins = dve.scalar_tensor_tensor(out=zh[:, i, lag:S], in0=zc[:, i, 0:S - lag],
                                                   scalar=col("conv", 3 * i + tap, 1), in1=zh[:, i, lag:S],
                                                   op0=ALU.mult, op1=ALU.add)
                link(ins)
            link(dve.tensor_tensor(zh, zh, zb, ALU.mult))
            slots_done(W_OUT0)

            def keep_conv():
                split(x_hi[:, 4:8, :], x_lo[:, 4:8, :], zh).then_inc(conv_ready, 1)

            attention(None, keep_conv)
            heads = rows[:, :, 0:512].rearrange("p b (h n) -> p b h n", h=4)
            sq = xT[:, 0:4, :].rearrange("p (b a) (h n) -> p b (a h) n", b=2, h=2)
            for t in range(QB):
                link(dve.tensor_tensor(sq[:, t], heads[:, t], heads[:, t], ALU.mult))
            link(dve.tensor_reduce(stat[:, 8:16], sq.rearrange("p b h n -> p (b h) n"), AX.X, ALU.add))
            root(stat[:, 8:16], 8, 1.0 / P, RMS_EPS)
            for t in range(QB):
                ins = dve.tensor_tensor(heads[:, t], heads[:, t], bc(stat[:, 4 * t:4 * t + 4], P), ALU.mult)
                if t == 0:
                    link(ins)
            ins.then_inc(heads_ready, 1)
            keep_cat(2, 0, sub8[:, 0:1])
            dve.wait_ge(csilu_ready, 1)
            split_c()
            add_branch(W_OUT0 + 4)
            dve.wait_ge(resid_ready, 1)
            norm(1, gain(1))
            for j in range(J1):
                hidden(j, lambda j: j + 1, W_FFN0 + swiglu_up(j) + 1, True)
            add_branch(W_FFN0 + 3 * J1)
            dve.wait_ge(resid_ready, 2)

            def ple(layer, n):
                for t in range(QB):
                    for half in range(2):
                        c = slice(half * BANK, (half + 1) * BANK)
                        dve.wait_ge(ple_gated, 4 * layer + 2 * t + half + 1)
                        link(dve.tensor_tensor(rows[:, t, c], rows[:, t, c], ps[:, 4 + 2 * t + half, :], ALU.mult))
                        ins = dve.tensor_tensor(resid[:, t, c], resid[:, t, c], rows[:, t, c], ALU.add)
                        if (t, half) == (1, 1):
                            ins.then_inc(resid_ready, 1)
                            dve.wait_ge(resid_ready, n)
                        else:
                            link(ins)

            def split_ple(layer):
                split(h_hi[:, 0, :], h_lo[:, 0, :], col("ple", 2 * S * layer, 2 * S)).then_inc(ple_split, 1)

            split_ple(0)
            norm(2, gain(2))
            slots_done(W_PLE0 + 5)
            ple(0, 3)
            norm(3, gain(3))
            slots_done(W_COUT)
            for t in range(QB):
                dve.wait_ge(gelu_done, 4 + 2 * t + 2)
                for half in range(2):
                    ins = dve.bn_stats(bn[:, t, half, :], v_rows[:, t, half * BANK:(half + 1) * BANK])
                link(ins)
                link(dve.bn_aggr(mv[:, t, :], bn[:, t].rearrange("p a b -> p (a b)")))
                link(dve.tensor_copy(stat[:, 8 + t:9 + t], mv[:, t, 1:2]))
            root(stat[:, 8:10], 2, 1.0, LN_EPS)
            dve.wait_ge(ln_in, 16 * 3)
            for t in range(QB):
                link(dve.tensor_scalar(v_rows[:, t, :], v_rows[:, t, :], mv[:, t, 0:1], stat[:, t:t + 1],
                                       ALU.subtract, ALU.mult))
                link(dve.tensor_tensor(v_rows[:, t, :], v_rows[:, t, :], ln_g, ALU.mult))
                dve.tensor_tensor(v_rows[:, t, :], v_rows[:, t, :], ln_b, ALU.add).then_inc(vn_ready, 1)
            for t in range(QB):
                for half in range(2):
                    dve.wait_ge(spatial_ready, 2 * t + half + 1)
                    for i in range(4):
                        g = 4 * half + i
                        ins = dve.scalar_tensor_tensor(out=rows[:, t, g * P:(g + 1) * P],
                                                       in0=ps[:, 2 * t + half, i * P:(i + 1) * P],
                                                       scalar=col("bs", g, 1), in1=u_rows[:, t, g * P:(g + 1) * P],
                                                       op0=ALU.add, op1=ALU.mult)
            ins.then_inc(heads_ready, 1)
            keep_cat(4, 2)
            add_branch(W_COUT + 4)
            dve.wait_ge(resid_ready, 4)
            norm(4, gain(4))
            dve.wait_ge(logits_ready, 1)
            link(dve.tensor_copy(logit[:, :, :].rearrange("p b e -> p (b e)"), ps[:, 0, 0:16]))
            for t in range(QB):
                link(dve.max(top[:, t, :], logit[:, t, :]))
                link(dve.max_index(topi[:, t, :], top[:, t, :], logit[:, t, :]))
                link(dve.tensor_copy(route[:, t, 0, :], topi[:, t, :]))
                ins = dve.tensor_tensor(route[:, t, 1, 0:1], top[:, t, 1:2], top[:, t, 0:1], ALU.subtract)
                if t == 0:
                    link(ins)
            ins.then_inc(route_asked, 1)
            dve.wait_ge(route_exp, 2)
            prob = [route[:, :, 1, n:n + 1].rearrange("p b o -> p (b o)") for n in range(5)]
            link(dve.tensor_scalar(prob[2], prob[1], 1.0, None, ALU.add))
            link(dve.reciprocal(prob[3], prob[2]))
            dve.tensor_tensor(prob[4], prob[1], prob[3], ALU.mult)
            for t in range(QB):
                for n in range(2):
                    ins = dve.tensor_scalar(route[:, t, 2 + n, :], col("iota"), route[:, t, 0, n:n + 1],
                                            None, ALU.is_equal)
            link(ins)
            link(dve.tensor_tensor(member[:, :, :], route[:, :, 2, :], route[:, :, 3, :], ALU.add))
            for t in range(QB):
                for n in range(2):
                    ins = dve.tensor_scalar(route[:, t, 2 + n, :], route[:, t, 2 + n, :], route[:, t, 1, 3 + n:4 + n],
                                            None, ALU.mult)
            link(ins)
            link(dve.tensor_tensor(route[:, :, 2, :], route[:, :, 2, :], route[:, :, 3, :], ALU.add))
            dve.memset(most[:, 0:1], 0.0).then_inc(member_ready, 1)
            dve.wait_ge(ranks_ready, 1)
            dve.tensor_copy(gate[:, :, 0:NE], route[:, :, 2, :])
            link(dve.tensor_copy(place[:, :, 0:NE], ps[:, 1, 0:16].rearrange("p (b e) -> p b e", b=QB)))
            dve.memset(gate[:, :, NE:NE + 1], 0.0)
            dve.memset(place[:, :, NE:NE + 1], -1.0)
            link(dve.tensor_reduce(most[:, 0:1], ps[:, 1, 16:24], AX.X, ALU.max))
            link(dve.tensor_copy(most_i[:, :], most[:, 0:1]))
            link(dve.tensor_scalar(member[:, :, :], member[:, :, :], -1000.0, 1000.0, ALU.mult, ALU.add))
            dve.tensor_tensor(place[:, :, 0:NE], place[:, :, 0:NE], member[:, :, :], ALU.add).then_inc(routed, 1)
            dve.wait_ge(routed, 1)

            def select(w, n):
                rank = col("slot", w.chunk * P, P)
                for t in range(QB):
                    pl = place[:, t, bass.ds(n, 1)]
                    dve.tensor_scalar(sel[:, t, :], rank, pl, None, ALU.is_equal)
                    ins = dve.tensor_scalar(selg[:, t, :], rank, pl, gate[:, t, bass.ds(n, 1)],
                                            ALU.is_equal, ALU.mult)
                ins.then_inc(w.sel_ready, 1)

            def take(w, counts):
                for h in range(2):
                    dve.wait_ge(w.gather_ready, counts[h])
                    dve.tensor_tensor(xT[:, 4 * h:4 * h + 4, 0:P],
                                      ps[:, 6 + h, :].rearrange("p (f c) -> p f c", f=4),
                                      bc(gain(4)[:, 4 * h:4 * h + 4], P), ALU.mult).then_inc(w.gathered, 1)
                for h in range(2):
                    dve.wait_ge(w.gathered_hi, counts[h])
                    f = slice(4 * h, 4 * h + 4)
                    dve.tensor_tensor(x_lo[:, f, 0:P], xT[:, f, 0:P], x_hi[:, f, 0:P].bitcast(F32), ALU.subtract)\
                        .then_inc(w.gathered_lo, 1)

            def experts(w):
                select(w, 0)
                take(w, [1, 2])
                dve.memset(most[:, 2:3], 0.0).then_inc(w.merged, 1)
                with dve.Fori(0, NE // 2) as turn:
                    at = [0]
                    for x in range(2):
                        expert(w, turn, x, at)

            def expert(w, turn, x, at):
                def e(per, plus):
                    return turn * (2 * per) + (x * per + plus)

                def ahead(halves):
                    for m in range(at[0], min(x * EH + halves + PAIRS, BODY)):
                        dve.wait_ge(w.hi_ready, turn * BODY + (2 * w.first + m + 1))
                        a = m % 2 * HALF
                        dve.tensor_tensor(w_lo[:, m % PAIRS, :], ring[:, m // 2 % RING, a:a + HALF],
                                          w_hi[:, m % PAIRS, :].bitcast(F32), ALU.subtract).then_inc(w.lo_ready, 1)
                        at[0] = m + 1

                def lo(j):
                    dve.wait_ge(w.hidT_hi, e(J1, j + 1))
                    c = 256 * (j % 2)
                    dve.tensor_tensor(h_lo[:, j % 2, 0:256], ps[:, 2, c:c + 256], h_hi[:, j % 2, 0:256].bitcast(F32),
                                      ALU.subtract).then_inc(w.hidT_lo, 1)

                for j in range(J1):
                    if j >= 1:
                        ahead(2 * swiglu_up(j))
                        lo(j - 1)
                    ahead(2 * (swiglu_up(j) + 1))
                    dve.wait_ge(w.act_ready, e(J1, j + 1))
                    dve.tensor_tensor(hid_rows[:, j % 2, :], act_rows[:, j % 2, :], ps[:, j % 2, 256:512], ALU.mult)\
                        .then_inc(w.hid_ready, 1)
                    if j == 3:
                        dve.wait_ge(w.selT_ready, e(1, 1))
                        select(w, turn * 2 + (x + 1))
                ahead(EH - 2)
                lo(J1 - 1)
                ahead(EH)
                take(w, [e(2, 3), e(2, 4)])
                for t in range(QB):
                    dve.wait_ge(w.scattered, e(2, t + 1))
                    ins = dve.tensor_tensor(resid[:, t, :], resid[:, t, :], bank((4, 2)[t], 2), ALU.add)
                ins.then_inc(w.merged, 1)
                dve.wait_ge(w.merged, e(1, 2))

            experts(first_pass)
            with dve.If(overflowing(dve)):
                experts(second_pass)
            split_at[0], split_end[0] = 2 * W_PLE1, 2 * SLOTS
            split_to(2 * W_PLE1 + PAIRS)
            dve.memset(most[:, 1:2], 0.0).then_inc(resid_ready, 1)
            dve.wait_ge(resid_ready, 5)
            split_ple(1)
            norm(5, gain(5))
            slots_done(W_PLE1 + 5)
            ple(1, 6)
            norm_rows()
            dve.wait_ge(rows_scaled, 14)
            dve.wait_ge(fin_in, 16)
            for t in range(QB):
                ins = dve.tensor_tensor(resid[:, t, :], rows[:, t, :], ln_g, ALU.mult)
                if t == 0:
                    link(ins)
            ins.then_inc(resid_ready, 1)
            dve.wait_ge(resid_ready, 7)
            for l in range(2):
                n0 = W_BLK + l * B_ALL
                for part in range(4):
                    slots_done(n0 + B_ADA + 4 * (part + 1))
                    for h in range(2):
                        if (l, part, h) != (0, 0, 0):
                            dve.wait_ge(ada_taken, 8 * l + 2 * part + h)
                        link(dve.tensor_tensor(ff[:, 2, :].rearrange("p (f s) -> p f s", f=4),
                                               ps[:, 2 * part + h, :].rearrange("p (f s) -> p f s", f=4),
                                               rep(ident, 4), ALU.mult))
                        c = 8 * part + 4 * h
                        dve.tensor_reduce(ada[:, c:c + 4], ff[:, 2, :].rearrange("p (f s) -> p f s", f=4), AX.X,
                                          ALU.add).then_inc(ada_taken, 1)
                dve.wait_ge(ada_taken, 8 * (l + 1))
                link(dve.tensor_tensor(ada[:, :], ada[:, :], col("bada", 32 * l, 32), ALU.add))
                for i in range(2):
                    ins = dve.scalar_tensor_tensor(out=modg[:, i, :], in0=ada[:, 16 * i + 8:16 * i + 16], scalar=1.0,
                                                   in1=gain(6 + 2 * l + i), op0=ALU.add, op1=ALU.mult)
                link(ins)
                slots_done(n0 + B_IN)
                dve.wait_ge(bada_in, 16 * (l + 1))
                ins = dve.tensor_tensor(grow[:, :, :].rearrange("p a n -> p (a n)"),
                                        grow[:, :, :].rearrange("p a n -> p (a n)"), bank(0, 4), ALU.add)
                ins.then_inc(grow_ready, 1)
                norm(6 + 2 * l, modg[:, 0, :], ada[:, 0:8])
                job0 = 10 + 9 * l
                split_to(2 * (n0 + B_IN + 3) + PAIRS)
                dve.wait_ge(projT_kept, job0 + 3)
                dve.tensor_tensor(flat0[:, 0:3 * S], arena[:, T_CKV * S:(T_CKV + 3) * S],
                                  arena[:, T_CKV * S:(T_CKV + 3) * S], ALU.mult).then_inc(squares_ready, 1)
                split_to(2 * (n0 + B_IN + LATENT_SLOTS) + PAIRS)
                dve.wait_ge(latsum_ready, l + 1)
                lat = flat0[:, 0:2 * S]
                link(dve.tensor_scalar(lat[:, 0:S], ps[:, 6, 0:S], 1.0 / 128, RMS_EPS, ALU.mult, ALU.add))
                dve.tensor_scalar(lat[:, S:2 * S], ps[:, 6, S:2 * S], 1.0 / 192, RMS_EPS, ALU.mult, ALU.add)\
                    .then_inc(latms_ready, 1)
                split_to(2 * (n0 + B_IN + LATENT_SLOTS) + PAIRS + 1)
                dve.wait_ge(latroot_ready, l + 1)
                link(dve.reciprocal(flat0[:, 2 * S:4 * S], lat))
                for t, r, g in ((T_CKV, 2, 0), (T_CQ, 3, 1), (T_CQ + 1, 3, 2)):
                    ins = dve.scalar_tensor_tensor(out=zT[:, t, :], in0=zT[:, t, :], scalar=col("mlag", 3 * l + g, 1),
                                                   in1=flat0[:, r * S:(r + 1) * S], op0=ALU.mult, op1=ALU.mult)
                link(ins)
                split_to(2 * (n0 + B_IN + LATENT_SLOTS) + PAIRS + 3)
                split(lat_hi, lat_lo, zT[:, T_CKV:T_CKV + 3, :]).then_inc(latent_ready, 1)
                split_to(2 * (n0 + B_IN + LATENT_SLOTS) + PAIRS + 5)
                dve.memset(blk[:, :, :, NCMP:16], 0.0)
                for which in range(2):
                    for par in range(2):
                        z = zT[64 * par:64 * par + 64, T_KC + which, :].rearrange("p (n l) -> p l n", l=16)
                        for hi in range(2):
                            ins = dve.tensor_tensor(
                                blk[64 * par:64 * par + 64, which, 8 * hi:8 * hi + 8, 0:NCMP],
                                z[:, par:16:2, hi:hi + NCMP],
                                bc(col("pos", 32 * l + 16 * which + 8 * hi, 8)[64 * par:64 * par + 64], NCMP), ALU.add)
                link(ins)
                split(blk_hi, blk_lo, blk).then_inc(cmpblk_ready, 1)
                split_to(2 * (n0 + B_CMP + 1) + PAIRS)
                dve.wait_ge(mlarot_ready, l + 1)
                cm, sm = col("cosm"), col("sinm")
                tmp = flat0[:, 0:4 * S].rearrange("p (h s) -> p h s", h=4)
                link(dve.tensor_tensor(tmp, bank(2, 2).rearrange("p (h s) -> p h s", h=4), rep(sm, 4), ALU.mult))
                link(dve.tensor_tensor(qm, qm, rep(cm, 4), ALU.mult))
                link(dve.tensor_tensor(qm, qm, tmp, ALU.add))
                kpe = zT[:, T_KPE, :]
                link(dve.tensor_tensor(flat0[:, 0:S], ps[:, 1, 0:S], sm, ALU.mult))
                link(dve.tensor_tensor(kpe, kpe, cm, ALU.mult))
                link(dve.tensor_tensor(kpe, kpe, flat0[:, 0:S], ALU.add))
                dve.tensor_copy(km[64:128, :, :], rep(kpe[64:128], 4)).then_inc(mla_ready, 1)
                split_to(2 * (n0 + B_OUT) + PAIRS)
                attention(l)
                keep_cat(4, 6 + 4 * l)
                if l == 0:
                    split_c()
                add_branch(n0 + B_OUT + 4, grow[:, 0, :])
                dve.wait_ge(resid_ready, 8 + 2 * l)
                norm(7 + 2 * l, modg[:, 1, :], ada[:, 16:24])
                base = J1 + l * J2
                for j in range(J2):
                    hidden(j, lambda j: base + j + 1, n0 + B_MLP + mlp_up(j) + 1, False)
                add_branch(n0 + B_ALL, grow[:, 1, :])
                dve.wait_ge(resid_ready, 9 + 2 * l)
            norm_rows()
            dve.wait_ge(rows_scaled, 24)
            dve.wait_ge(fin_in, 32)
            fin = ff[:, 0:2, :].rearrange("p a s -> p (a s)")
            for t in range(QB):
                ins = dve.tensor_tensor(rows[:, t, :], rows[:, t, :], fin, ALU.mult)
                if t == 0:
                    link(ins)
            ins.then_inc(resid_ready, 1)

        @block.scalar
        def _(act):
            steps = [0]

            def link(ins):
                steps[0] += 1
                ins.then_inc(act_step, 1)
                act.wait_ge(act_step, steps[0])

            split_at, split_end = [0], [2 * W_MOE]

            def split_to(m_end):
                for m in range(split_at[0], min(m_end, split_end[0])):
                    n, a = m // 2, m % 2 * HALF
                    act.wait_ge(landed[n % RING], 16 * (n // RING + 1))
                    if m >= PAIRS:
                        act.wait_ge(half_done, m + 1 - PAIRS)
                    act.activation(w_hi[:, m % PAIRS, :], ring[:, n % RING, a:a + HALF], ACT.Copy)\
                        .then_inc(hi_ready, 1)
                    split_at[0] = m + 1

            def slots_done(n):
                split_to(2 * n + PAIRS)
                act.wait_ge(half_done, 2 * n)

            norms = [0]

            def square_rows():
                if norms[0]:
                    act.wait_ge(resid_ready, norms[0])
                act.activation(rows[:, 1, :], resid[:, 1, :], ACT.Square, accum_out=stat[:, 9:10]).then_inc(squared, 1)
                norms[0] += 1

            def norm_hi(k):
                square_rows()
                for b in range(4):
                    h, t = b // 2, b % 2
                    act.wait_ge(gained, 4 * k + b + 1)
                    at = slice(None), slice(4 * h, 4 * h + 4), slice(t * P, (t + 1) * P)
                    act.activation(x_hi[at], xT[at], ACT.Copy).then_inc(normed_hi, 1)

            act.dma_start(con[:, 0:FIRST_COLS], consts[:, 0:FIRST_COLS]).then_inc(consts_in, 16)
            act.dma_start(posi[:, :], pos.partition_broadcast(P)).then_inc(params_in, 16)
            act.dma_start(lamv[:, :], lam_in.partition_broadcast(P)).then_inc(params_in, 16)
            for l in range(2):
                act.dma_start(sink[:, l, :], sinks[l].partition_broadcast(P)).then_inc(params_in, 16)
            act.dma_start(con[:, FIRST_COLS:NCOLS], consts[:, FIRST_COLS:NCOLS]).then_inc(tables_in, 16)
            act.dma_start(grow[:, :, :].rearrange("p a n -> p (a n)"), bada_rows[0].partition_broadcast(P))\
                .then_inc(bada_in, 16)
            act.wait_ge(consts_in, 16)
            act.activation(csilu[:, :], col("c"), ACT.Silu).then_inc(csilu_ready, 1)

            def keep_tiles(dst, count, n0, first=0):
                for s in range(first, count):
                    slots_done(n0 + s + 1)
                    act.activation(dst[:, 2 * s:2 * s + 2, :].rearrange("p a s -> p (a s)"),
                                   ps[:, s % 4, :], ACT.Copy).then_inc(projT_kept, 1)

            def attention(layer):
                groups = attention_groups(layer)
                base = GROUP_BASE[0 if layer is None else layer + 1]

                def exps(i):
                    kind, qb, hg = groups[i]
                    g = base + i
                    kw = NCMP if kind == "nsac" else P * (qb + 1) + (kind == "swa")
                    act.wait_ge(max_ready, g + 1)
                    for u in range(4):
                        o = head_of(kind, u)
                        sc = score[:, g % 2, u, 0:kw]
                        ins = act.activation(sc, sc, ACT.Exp, bias=soft[:, g % 4, 0, u:u + 1],
                                             scale=96.0 ** -0.5 if kind == "mla" else 0.125,
                                             accum_out=soft[:, g % 4, 1, o:o + 1])
                    ins.then_inc(exp_ready, 1)

                def keep(i):
                    kind, qb, hg = groups[i]
                    g = base + i
                    nkb = 1 if kind == "nsac" else qb + 1
                    kp = NCMP if kind == "nsac" else P
                    act.wait_ge(probT_ready, g + 1)
                    if i >= 2:
                        act.wait_ge(mixed_ready, g - 1)
                    act.activation(probT[0:kp, g % 2, 0:4 * nkb, :].rearrange("p a b -> p (a b)"),
                                   bank(4, 2)[0:kp, 0:4 * nkb * P], ACT.Copy).then_inc(probT_kept, 1)

                exps(0)
                exps(1)
                for i in range(len(groups)):
                    keep(i)
                    if i + 2 < len(groups):
                        exps(i + 2)

            def keep_cat(count, before, gain=None):
                for n in range(count):
                    act.wait_ge(catT_ready, before + n + 1)
                    t, half = (n, 0) if count == 2 else (n // 2, n % 2)
                    act.activation(x_hi[:, 4 * half:4 * half + 4, t * P:(t + 1) * P],
                                   ps[:, 4 + 2 * t + half, :].rearrange("p (f s) -> p f s", f=4),
                                   ACT.Copy, scale=1.0 if gain is None else gain).then_inc(catT_hi, 1)

            def activations(j, done, func, paired):
                slots_done(done)
                act.activation(acth[:, j % 2, :], ps[:, (2 if paired else 1) * (j % 2), :], func)\
                    .then_inc(act_ready, 1)

            split_to(PAIRS)
            act.wait_ge(resid_in, 16)
            norm_hi(0)
            keep_tiles(zqk, 4, W_QK)
            act.wait_ge(angles_ready, 1)
            act.activation(sin0, ang, ACT.Sin).then_inc(sines_ready, 1)
            act.activation(cos0, turns, ACT.Sin).then_inc(sines_ready, 1)
            act.wait_ge(lam_asked, 1)
            act.activation(lam[:, 2:4], lam[:, 0:2], ACT.Exp).then_inc(lam_exp, 1)
            keep_tiles(zbch, 6, W_BCH)
            slots_done(W_V + 2)
            act.activation(v1.rearrange("p b n -> p (b n)"), bank(4, 2), ACT.Copy).then_inc(vrows_kept, 1)
            attention(None)
            keep_cat(2, 0, sub8[:, 0:1])
            split_to(2 * (W_OUT0 + 4) + PAIRS)
            norm_hi(1)
            for j in range(J1):
                activations(j, W_FFN0 + swiglu_up(j) + 1, ACT.Silu, True)
            slots_done(W_PLE0)
            act.dma_start(ln_g, ln_rows[0].partition_broadcast(P)).then_inc(ln_in, 16)
            act.dma_start(ln_b, ln_rows[1].partition_broadcast(P)).then_inc(ln_in, 16)
            act.dma_start(ws, w_s).then_inc(ln_in, 16)

            def ple(layer):
                slots_done((W_PLE0, W_PLE1)[layer] + 5)
                for b in range(4):
                    act.activation(rows[:, b // 2, (b % 2) * BANK:(b % 2 + 1) * BANK], ps[:, b, :], ACT.Sigmoid)\
                        .then_inc(ple_gated, 1)

            norm_hi(2)
            ple(0)
            norm_hi(3)
            for part, dst in enumerate((u_rows, v_rows)):
                slots_done(W_CIN + 4 * part + 4)
                for b in range(4):
                    act.activation(dst[:, b // 2, (b % 2) * BANK:(b % 2 + 1) * BANK], ps[:, 4 * part + b, :], ACT.Gelu)\
                        .then_inc(gelu_done, 1)
            keep_cat(4, 2)
            split_to(2 * (W_COUT + 4))
            norm_hi(4)
            act.wait_ge(route_asked, 1)
            for t in range(QB):
                act.activation(route[:, t, 1, 1:2], route[:, t, 1, 0:1], ACT.Exp).then_inc(route_exp, 1)

            def take(w, counts):
                for h in range(2):
                    act.wait_ge(w.gathered, counts[h])
                    f = slice(4 * h, 4 * h + 4)
                    act.activation(x_hi[:, f, 0:P], xT[:, f, 0:P], ACT.Copy).then_inc(w.gathered_hi, 1)

            def experts(w):
                take(w, [1, 2])
                with act.Fori(0, NE // 2) as turn:
                    at = [0]
                    for x in range(2):
                        expert(w, turn, x, at)

            def expert(w, turn, x, at):
                def e(per, plus):
                    return turn * (2 * per) + (x * per + plus)

                def ahead(halves):
                    for m in range(at[0], min(x * EH + halves + PAIRS, BODY)):
                        n, a = m // 2, m % 2 * HALF
                        act.wait_ge(w.landed[n % RING],
                                    turn * (16 * (BODY // 2 // RING)) + 16 * (w.first // RING + n // RING + 1))
                        if m >= PAIRS:
                            act.wait_ge(w.done, turn * BODY + (2 * w.first + m + 1 - PAIRS))
                        act.activation(w_hi[:, m % PAIRS, :], ring[:, n % RING, a:a + HALF], ACT.Copy)\
                            .then_inc(w.hi_ready, 1)
                        at[0] = m + 1

                def done(halves):
                    ahead(halves)
                    act.wait_ge(w.done, turn * BODY + (2 * w.first + x * EH + halves))

                ahead(0)

                def hi(j):
                    act.wait_ge(w.hidT_ready, e(J1, j + 1))
                    c = 256 * (j % 2)
                    act.activation(h_hi[:, j % 2, 0:256], ps[:, 2, c:c + 256], ACT.Copy).then_inc(w.hidT_hi, 1)

                for j in range(J1):
                    if j >= 1:
                        ahead(2 * swiglu_up(j))
                        hi(j - 1)
                    done(2 * (swiglu_up(j) + 1))
                    act.activation(act_rows[:, j % 2, :], ps[:, j % 2, 0:256], ACT.Silu).then_inc(w.act_ready, 1)
                    if j == 2:
                        act.wait_ge(w.selT_ready, e(1, 1))
                        act.activation(selT.rearrange("p b s -> p (b s)"), ps[:, 3, 0:256], ACT.Copy)\
                            .then_inc(w.selT_kept, 1)
                ahead(EH - 2)
                hi(J1 - 1)
                done(EH)
                for h in range(2):
                    act.activation(y_rows[:, h * BANK:(h + 1) * BANK], ps[:, 4 + h, :], ACT.Copy)\
                        .then_inc(w.y_kept, 1)
                take(w, [e(2, 3), e(2, 4)])

            experts(first_pass)
            with act.If(overflowing(act)):
                experts(second_pass)
            act.dma_start(ln_g, fin_row[0].partition_broadcast(P)).then_inc(fin_in, 16)
            split_at[0], split_end[0] = 2 * W_PLE1, 2 * SLOTS
            split_to(2 * W_PLE1 + PAIRS)
            norm_hi(5)
            ple(1)
            square_rows()
            for l in range(2):
                n0 = W_BLK + l * B_ALL
                if l == 1:
                    split_to(2 * n0 + PAIRS)
                    act.wait_ge(resid_ready, 9)
                    act.dma_start(grow[:, :, :].rearrange("p a n -> p (a n)"), bada_rows[1].partition_broadcast(P))\
                        .then_inc(bada_in, 16)
                split_to(2 * (n0 + B_IN) + PAIRS)
                norm_hi(6 + 2 * l)
                keep_tiles(zT, LATENT_SLOTS, n0 + B_IN)
                split_to(2 * (n0 + B_IN + LATENT_SLOTS) + PAIRS + 1)
                act.wait_ge(latms_ready, l + 1)
                act.activation(flat0[:, 0:2 * S], flat0[:, 0:2 * S], ACT.Sqrt).then_inc(latroot_ready, 1)
                act.wait_ge(gateT_ready, l + 1)
                act.activation(gates[:, :, 0:12], ps[:, 7, 0:2 * P].rearrange("p (b n) -> p b n", b=2)[:, :, 0:12],
                               ACT.Sigmoid).then_inc(gates_ready, 1)
                keep_tiles(zT, 9, n0 + B_IN, LATENT_SLOTS)
                slots_done(n0 + B_SMALL)
                act.activation(v2.rearrange("p b n -> p (b n)"), bank(4, 2), ACT.Copy).then_inc(vrows_kept, 1)
                slots_done(n0 + B_CMP)
                link(act.activation(qm.rearrange("p h s -> p (h s)"), bank(2, 2), ACT.Copy))
                link(act.activation(km[0:64].rearrange("p h s -> p (h s)"), bank(4, 2)[0:64], ACT.Copy))
                act.activation(vm.rearrange("p b n -> p (b n)"), bank(6), ACT.Copy).then_inc(mlaheads_kept, 1)
                slots_done(n0 + B_OUT)
                act.activation(hidc[:, :, 0:NCMP], ps[:, 7, 0:32].rearrange("p (v n) -> p v n", v=2)[:, :, 0:NCMP],
                               ACT.Gelu_apprx_tanh).then_inc(cmpact_ready, 1)
                act.wait_ge(cmp_ready, l + 1)
                link(act.activation(kcmp[:, 0:NCMP], ps[:, 7, 32:32 + NCMP], ACT.Copy))
                act.activation(vcmp[0:NCMP, :], ps[0:NCMP, 7, 64:128], ACT.Copy).then_inc(cmp_kept, 1)
                attention(l)
                keep_cat(4, 6 + 4 * l)
                split_to(2 * (n0 + B_MLP) + PAIRS)
                norm_hi(7 + 2 * l)
                for j in range(J2):
                    activations(j, n0 + B_MLP + mlp_up(j) + 1, ACT.Relu, False)
            slots_done(SLOTS)
            act.dma_start(ff[:, 0:2, :].rearrange("p a s -> p (a s)"), fin_row[1].partition_broadcast(P))\
                .then_inc(fin_in, 16)
            square_rows()

        @block.gpsimd
        def _(pool):
            pool.memset(neghalf[:, :], -0.5).then_inc(pool_step, 1)
            pool.wait_ge(pool_step, 1)
            widths = [2, 8] + [2] * 12
            for n, w in enumerate(widths):
                if n == 5:
                    pool.wait_ge(ln_in, 16 * 3)
                    pool.affine_select(out=ws, in_=ws, pattern=[[0, 8], [1, P]], compare_op=ALU.is_ge, fill=0.0,
                                       base=0, channel_multiplier=-1).then_inc(ws_masked, 1)
                pool.wait_ge(root_asked, n + 1)
                pool.tensor_tensor(stat[:, 0:w], stat[:, 0:w], neghalf[:, 0:w], ALU.pow).then_inc(root_ready, 1)


def row_tiles(w, k):
    n = w.shape[-1]
    return np.ascontiguousarray(w.reshape(k, P, n).transpose(1, 0, 2)).reshape(P, k * n)


def column_slots(w):
    return [row_tiles(w[:, j:j + 256], KT) for j in range(0, w.shape[1], 256)]


def tile_slots(w):
    return [np.concatenate([row_tiles(w[:, j + a:j + a + P], KT) for a in (0, P)], 1)
            for j in range(0, w.shape[1], 2 * P)]


def row_slots(w):
    return [row_tiles(w[j:j + 256], 2) for j in range(0, w.shape[0], 256)]


def swiglu_slots(w1, w3, w2, up_slots):
    a, b, c = up_slots(w1), up_slots(w3), row_slots(w2)
    out = []
    for j in range(J1 + 1):
        if j < J1:
            out += [a[j], b[j]]
        if j >= 1:
            out.append(c[j - 1])
    return out


def lay_out(i):
    f = np.float32
    slots = []
    w = np.asarray(i["a_w_in"])[0]
    slots += tile_slots(w[:, 0:1024]) + tile_slots(w[:, 1536:3072])
    wv = w[:, 1024:1536]
    slots += [row_tiles(wv[0:512], 4), row_tiles(wv[512:1024], 4)]
    slots += row_slots(np.asarray(i["a_w_out"])[0])
    slots += swiglu_slots(*(np.asarray(i[n])[0] for n in ("ffn_w1", "ffn_w3", "ffn_w2")), tile_slots)
    pg, pp = np.asarray(i["ple_gate"]), np.asarray(i["ple_proj"])
    slots += row_slots(pg[0]) + row_slots(pp[0])
    w = np.asarray(i["c_w_in"])[0]
    slots += row_slots(w[:, 0:1024]) + row_slots(w[:, 1024:2048])
    slots += row_slots(np.asarray(i["c_w_out"])[0])
    m1, m3, m2 = (np.asarray(i[n])[0] for n in ("moe_w1", "moe_w3", "moe_w2"))
    for e in range(NE):
        slots += swiglu_slots(m1[e], m3[e], m2[e], column_slots)
    slots += row_slots(pg[1]) + row_slots(pp[1])
    for l in range(2):
        w = np.asarray(i["w_ada_2"])[l]
        sh1, sc1, g1, sh2, sc2, g2 = (w[:, n * D:(n + 1) * D] for n in range(6))
        for part in (sh1, sc1, sh2, sc2, g1, g2):
            slots += row_slots(part)
        w = np.asarray(i["w_in_2"])[l]
        z = {}
        at = 0
        for name, n in (("swaq", 256), ("swak", 128), ("swav", 128), ("cq", 192), ("ckv", 128), ("kpe", 32),
                        ("nsaq", 256), ("kc", 64), ("vc", 64), ("ks", 64), ("vs", 64), ("kw", 64), ("vw", 64),
                        ("gl", 12), ("mobq", 256), ("mobk", 256), ("mobv", 256)):
            z[name] = w[:, at:at + n]
            at += n

        def pad(n):
            return np.zeros((D, n), f)

        sq = z["swaq"]
        cols = [sq[:, 0:64], sq[:, 128:192], sq[:, 64:128], sq[:, 192:256], z["swak"], z["ckv"], z["cq"], pad(64),
                pad(64), z["kpe"], pad(32), z["gl"], pad(116), z["nsaq"]]
        for name in ("kc", "vc", "ks", "kw"):
            cols += [z[name], z[name]]
        cols += [z["mobq"], z["mobk"]]
        slots += tile_slots(np.concatenate(cols, 1))
        wv = np.concatenate([z["swav"], z["vs"], z["vw"], z["mobv"]], 1)
        slots += [row_tiles(wv[0:512], 4), row_tiles(wv[512:1024], 4)]
        uq = np.asarray(i["mla_w_uq_2"])[l].reshape(192, 4, 96)
        uqp = np.zeros((256, 4, 128), f)
        uqp[0:192, :, 0:96] = uq
        ukv = np.asarray(i["mla_w_ukv_2"])[l].reshape(128, 4, 128)
        small = np.zeros((P, SLOT), f)
        small[:, 0:1024] = row_tiles(uqp.reshape(256, 512), 2)
        for h in range(4):
            small[:, 1024 + 128 * h:1024 + 128 * h + 64] = ukv[:, h, 0:64]
        small[:, 1536:1792] = ukv[:, :, 64:128].reshape(128, 256)
        slots.append(small)
        for n in ("nsa_cmp_k_w1_2", "nsa_cmp_v_w1_2"):
            slots.append(row_tiles(np.asarray(i[n])[l], 16))
        slots += row_slots(np.asarray(i["w_out_2"])[l])
        a, b = tile_slots(np.asarray(i["w_up_2"])[l]), row_slots(np.asarray(i["w_down_2"])[l])
        for j in range(J2 + 1):
            if j < J2:
                slots.append(a[j])
            if j >= 1:
                slots.append(b[j - 1])
    assert len(slots) == SLOTS, (len(slots), SLOTS)
    stream = np.stack(slots)
    del slots

    def colvec(v):
        return np.asarray(v).reshape(-1, P).T

    con = {}
    lm, lf, lp = (np.asarray(i[n]) for n in ("ln_mix", "ln_ffn", "ln_ple"))
    nm, nl = np.asarray(i["norm_mix_g_2"]), np.asarray(i["norm_mlp_g_2"])
    con["gain"] = np.concatenate([colvec(v) for v in (lm[0], lf[0], lp[0], lm[1], lf[1], lp[1], nm[0], nl[0],
                                                      nm[1], nl[1])], 1)
    con["subln"] = colvec(np.asarray(i["a_subln"])[0])
    con["conv"] = np.asarray(i["a_conv_w"])[0].reshape(4, P, 3).transpose(1, 0, 2).reshape(P, 12)
    half = 8
    inv = np.float32(500000.0) ** (-np.arange(0, 16, 2, dtype=f) / np.float32(16))
    invf = np.zeros((2, 64), f)
    invf[:, 0:half] = inv
    invf[:, half:2 * half] = inv
    con["invf"] = invf.reshape(P, 1)
    con["bs"] = np.asarray(i["c_b_s"])[0].T
    con["router"] = row_tiles(np.asarray(i["router_w"])[0], KT)
    con["iota"] = np.tile(np.arange(8, dtype=f), (P, 1))
    con["c"] = colvec(np.asarray(i["c_2"])[0])
    ba = np.asarray(i["b_ada_2"])
    con["bada"] = np.concatenate([colvec(ba[l, n * D:(n + 1) * D]) for l in range(2) for n in (0, 1, 3, 4)], 1)
    ck2, cv2 = np.asarray(i["nsa_cmp_k_w2_2"]), np.asarray(i["nsa_cmp_v_w2_2"])
    con["cmpw2"] = np.concatenate([v for l in range(2) for v in (ck2[l], ck2[l], cv2[l])], 1)
    qg, kg = np.asarray(i["mla_q_norm_g_2"]), np.asarray(i["mla_kv_norm_g_2"])
    mlag = np.zeros((P, 6), f)
    for l in range(2):
        mlag[:, 3 * l] = kg[l]
        mlag[:, 3 * l + 1] = qg[l, 0:128]
        mlag[0:64, 3 * l + 2] = qg[l, 128:192]
    con["mlag"] = mlag
    con["pos"] = np.concatenate([np.asarray(i[n])[l].reshape(16, P).T for l in range(2)
                                 for n in ("nsa_cmp_pos_k_2", "nsa_cmp_pos_v_2")], 1)
    t = np.arange(S)
    cend = np.arange(NCMP) * 16 + 31
    dc = (t[:, None] - cend[None, :]).astype(f)
    con["nsac"] = np.where(dc >= 0, -dc, f(NEG)).reshape(2, P, NCMP).transpose(1, 0, 2).reshape(P, -1)
    con["ident"] = np.eye(P, dtype=f)
    con["before"] = np.triu(np.ones((P, P), f), 1)
    con["slot"] = np.tile(np.arange(2 * P, dtype=f), (P, 1))
    rot0, rotm = np.zeros((P, P), f), np.zeros((P, P), f)
    for h in range(2):
        for d in range(half):
            rot0[64 * h + d + half, 64 * h + d] = -1
            rot0[64 * h + d, 64 * h + d + half] = 1
    for d in range(16):
        rotm[64 + d + 16, 64 + d] = -1
        rotm[64 + d, 64 + d + 16] = 1
    con["rot0"], con["rotm"] = rot0, rotm
    fr = np.float32(10000.0) ** (-np.arange(16, dtype=f) / np.float32(16))
    ang = (t.astype(f)[:, None] * fr[None, :]).astype(np.float64)
    cosm, sinm = np.ones((P, S), f), np.zeros((P, S), f)
    for r in (64, 80):
        cosm[r:r + 16] = np.cos(ang).T
        sinm[r:r + 16] = np.sin(ang).T
    con["cosm"], con["sinm"] = cosm, sinm
    dist = (t[:, None] - t[None, :]).astype(f)

    def by_block(m):
        return m.astype(f).reshape(2, P, S).transpose(1, 0, 2).reshape(P, 2 * S)

    con["alibi"] = by_block(np.where(dist >= 0, -dist, f(NEG)))
    con["causal"] = by_block(np.where(dist >= 0, f(0), f(NEG)))
    con["window"] = by_block(np.where((dist >= 0) & (dist < 128), -dist, f(NEG)))
    p = np.asarray(i["p"])
    con["ple"] = np.concatenate([row_tiles(np.ascontiguousarray(p[l, 0].T), 2) for l in range(2)], 1)
    consts = np.concatenate([con[n] for n in COLS], 1)
    assert consts.shape == (P, NCOLS), consts.shape
    return {
        "stream": stream,
        "x": np.ascontiguousarray(np.asarray(i["x"])[0]),
        "consts": np.ascontiguousarray(consts.astype(f, copy=False)),
        "pos": np.ascontiguousarray(np.asarray(i["positions"])[0]),
        "lam": np.ascontiguousarray(np.asarray(i["a_lambda"])[0].reshape(-1)),
        "ln_rows": np.stack([np.asarray(i["c_ln_g"])[0], np.asarray(i["c_ln_b"])[0]]),
        "w_s": np.ascontiguousarray(np.asarray(i["c_w_s"])[0].transpose(2, 0, 1)),
        "sinks": np.ascontiguousarray(np.asarray(i["swa_sinks_2"])),
        "bada_rows": np.ascontiguousarray(np.concatenate([ba[:, 2 * D:3 * D], ba[:, 5 * D:6 * D]], 1)),
        "fin_row": np.stack([np.asarray(i["final_norm"]), np.asarray(i["final_norm_g_2"])]),
    }


def kernel(**inputs):
    import concourse.bacc as bacc
    from concourse.bass_utils import run_bass_kernel_spmd

    nc = bacc.Bacc("TRN2", target_bir_lowering=False, num_devices=1)
    arrays = lay_out(inputs)
    aps = {n: nc.dram_tensor(f"in_{n}", a.shape, mybir.dt.from_np(a.dtype), kind="ExternalInput").ap()
           for n, a in arrays.items()}
    out = nc.dram_tensor("out", (S, D), F32, kind="ExternalOutput").ap()
    build(nc, aps, out)
    r = run_bass_kernel_spmd(nc, [{f"in_{n}": a for n, a in arrays.items()}], core_ids=[0])
    return r.results[0]["out"].reshape(1, S, D)
```
